# Optimizing a Trainium2 kernel written in Bass

```python
import math
import jax, jax.numpy as jnp
from jax import lax
import numpy as np

D_MODEL = 1024
BATCH = 1
SEQ = 512
DEPTH = 2

D_MIX = D_MODEL
SSD_WIDTH = D_MIX // 2
SSD_HEADDIM = 64
SSD_HEADS = SSD_WIDTH // SSD_HEADDIM
SSD_GROUPS = 2
SSD_HEADS_PER_GROUP = SSD_HEADS // SSD_GROUPS
SSD_STATE = 128
SSD_XBC = SSD_WIDTH + 2 * SSD_GROUPS * SSD_STATE
CONV_WIDTH = 4
CHUNK = 128
ATTN_WIDTH = D_MIX - SSD_WIDTH
DIFF_HEAD_DIM = 64
DIFF_HEADS = ATTN_WIDTH // (2 * DIFF_HEAD_DIM)
DIFF_V_DIM = 2 * DIFF_HEAD_DIM
ATTN_QK = DIFF_HEADS * 2 * DIFF_HEAD_DIM
ATTN_V = DIFF_HEADS * DIFF_V_DIM
Q_BLOCK = 128
ROPE_THETA = 10000.0
D_FF = -(-(8 * D_MODEL) // (3 * 256)) * 256
IN_SPLITS = (SSD_WIDTH, SSD_XBC, SSD_HEADS, ATTN_QK, ATTN_QK, ATTN_V)
D_IN_PROJ = SSD_WIDTH + SSD_XBC + SSD_HEADS + 2 * ATTN_QK + ATTN_V
ALPHA = (2 * DEPTH) ** 0.25
BETA = (8 * DEPTH) ** -0.25
N_MOD = 6
EPS = 1e-5

kernel_name = 'hymba_ssd_diffattn_deepnorm_adaln'

def layer_norm(x, g, b):
    xf = x.astype(jnp.float32)
    mu = jnp.mean(xf, -1, keepdims=True)
    var = jnp.mean(jnp.square(xf - mu), -1, keepdims=True)
    return ((xf - mu) * lax.rsqrt(var + EPS) * g + b).astype(x.dtype)

def rms_norm(x, g):
    xf = x.astype(jnp.float32)
    return (xf * lax.rsqrt(jnp.mean(xf * xf, -1, keepdims=True) + EPS) * g).astype(x.dtype)

def rope_tables(seq, dim):
    inv = 1.0 / (ROPE_THETA ** (jnp.arange(0, dim, 2, dtype=jnp.float32) / dim))
    ang = jnp.arange(seq, dtype=jnp.float32)[:, None] * inv[None, :]
    ang = jnp.concatenate([ang, ang], -1)
    return jnp.cos(ang), jnp.sin(ang)

def apply_rope(x, cos, sin):
    half = x.shape[-1] // 2
    rot = jnp.concatenate([-x[..., half:], x[..., :half]], -1)
    shape = (1, cos.shape[0]) + (1,) * (x.ndim - 3) + (cos.shape[1],)
    return x * cos.reshape(shape) + rot * sin.reshape(shape)

def causal_depthwise_conv(u, w, b):
    k = w.shape[0]
    out = lax.conv_general_dilated(
        u, w[:, None, :].astype(u.dtype), window_strides=(1,), padding=((k - 1, 0),),
        dimension_numbers=('NWC', 'WIO', 'NWC'), feature_group_count=u.shape[-1])
    return out + b

def segsum_exp(a):
    cs = jnp.cumsum(a, -1)
    n = a.shape[-1]
    diff = cs[..., :, None] - cs[..., None, :]
    mask = jnp.tril(jnp.ones((n, n), dtype=bool))
    return jnp.exp(jnp.where(mask, diff, -jnp.inf))

def ssd_chunked(xs, a, bm, cm):
    f32 = jnp.float32
    xs, a, bm, cm = xs.astype(f32), a.astype(f32), bm.astype(f32), cm.astype(f32)
    b, s, g, e, p = xs.shape
    n = bm.shape[-1]
    c = s // CHUNK
    xs = xs.reshape(b, c, CHUNK, g, e, p)
    bm = bm.reshape(b, c, CHUNK, g, n)
    cm = cm.reshape(b, c, CHUNK, g, n)
    a = a.reshape(b, c, CHUNK, g, e).transpose(0, 3, 4, 1, 2)
    a_cs = jnp.cumsum(a, -1)
    lmat = segsum_exp(a)
    cb = jnp.einsum('bclgn,bcsgn->bgcls', cm, bm)
    y_diag = jnp.einsum('bgcls,bgecls,bcsgep->bclgep', cb, lmat, xs)
    decay_states = jnp.exp(a_cs[..., -1:] - a_cs)
    states = jnp.einsum('bclgn,bgecl,bclgep->bcgepn', bm, decay_states, xs)
    chunk_decay = jnp.exp(a_cs[..., -1])

    def step(h, inp):
        st, dec = inp
        return dec[..., None, None] * h + st, h

    h0 = jnp.zeros((b, g, e, p, n), f32)
    _, prev = lax.scan(step, h0, (states.transpose(1, 0, 2, 3, 4, 5),
                                  chunk_decay.transpose(3, 0, 1, 2)))
    prev = prev.transpose(1, 0, 2, 3, 4, 5)
    y_off = jnp.einsum('bclgn,bcgepn,bgecl->bclgep', cm, prev, jnp.exp(a_cs))
    return (y_diag + y_off).reshape(b, s, g, e, p)

def diff_attention(q, k, v, lam):
    b, s, nh, _, d = q.shape
    nblk = s // Q_BLOCK
    qb = q.reshape(b, nblk, Q_BLOCK, nh, 2, d).transpose(1, 0, 2, 3, 4, 5)
    key_pos = jnp.arange(s)

    def block(args):
        qi, i = args
        scores = jnp.einsum('bqhmd,bkhmd->bhmqk', qi, k, preferred_element_type=jnp.float32)
        q_pos = i * Q_BLOCK + jnp.arange(Q_BLOCK)
        mask = key_pos[None, :] <= q_pos[:, None]
        prob = jax.nn.softmax(jnp.where(mask, scores, -jnp.inf), axis=-1)
        w = prob[:, :, 0] - lam * prob[:, :, 1]
        return jnp.einsum('bhqk,bkhv->bqhv', w.astype(v.dtype), v)

    out = lax.map(block, (qb, jnp.arange(nblk)))
    return out.transpose(1, 0, 2, 3, 4).reshape(b, s, nh, v.shape[-1])

def hybrid_mixer(h, w_in, conv_w, conv_b, dt_bias, a_log, d_skip, ssd_norm_w,
                 lam_qk, attn_norm_w, w_out, lambda_init, cos, sin):
    b, s, _ = h.shape
    proj = h @ w_in
    offs = np.cumsum(IN_SPLITS)[:-1].tolist()
    z, xbc, dt, q, k, v = jnp.split(proj, offs, axis=-1)

    xbc = jax.nn.silu(causal_depthwise_conv(xbc, conv_w, conv_b))
    xs, bm, cm = jnp.split(xbc, [SSD_WIDTH, SSD_WIDTH + SSD_GROUPS * SSD_STATE], axis=-1)
    xs = xs.reshape(b, s, SSD_GROUPS, SSD_HEADS_PER_GROUP, SSD_HEADDIM)
    bm = bm.reshape(b, s, SSD_GROUPS, SSD_STATE)
    cm = cm.reshape(b, s, SSD_GROUPS, SSD_STATE)
    dt = jax.nn.softplus(dt.astype(jnp.float32) + dt_bias.astype(jnp.float32))
    dt = dt.reshape(b, s, SSD_GROUPS, SSD_HEADS_PER_GROUP)
    a_head = -jnp.exp(a_log.astype(jnp.float32)).reshape(SSD_GROUPS, SSD_HEADS_PER_GROUP)
    y = ssd_chunked(xs * dt[..., None], a_head * dt, bm, cm)
    y = y + d_skip.reshape(SSD_GROUPS, SSD_HEADS_PER_GROUP)[:, :, None] * xs
    y = y.reshape(b, s, SSD_WIDTH) * jax.nn.silu(z.astype(jnp.float32))
    y = rms_norm(y.reshape(b, s, SSD_GROUPS, SSD_WIDTH // SSD_GROUPS),
                 ssd_norm_w.reshape(SSD_GROUPS, SSD_WIDTH // SSD_GROUPS))
    y_ssd = y.reshape(b, s, SSD_WIDTH).astype(h.dtype)

    q = q.reshape(b, s, DIFF_HEADS, 2, DIFF_HEAD_DIM)
    k = k.reshape(b, s, DIFF_HEADS, 2, DIFF_HEAD_DIM)
    v = v.reshape(b, s, DIFF_HEADS, DIFF_V_DIM)
    q = (apply_rope(q, cos, sin) * (DIFF_HEAD_DIM ** -0.5)).astype(h.dtype)
    k = apply_rope(k, cos, sin).astype(h.dtype)
    lq = lam_qk.astype(jnp.float32)
    lam = jnp.exp(jnp.sum(lq[0] * lq[1])) - jnp.exp(jnp.sum(lq[2] * lq[3])) + lambda_init
    o = diff_attention(q, k, v, lam)
    o = rms_norm(o, attn_norm_w) * (1.0 - lambda_init)
    y_attn = o.reshape(b, s, ATTN_WIDTH).astype(h.dtype)

    return jnp.concatenate([y_ssd, y_attn], axis=-1) @ w_out

def swiglu(h, w_gate_up, w_down):
    g, u = jnp.split(h @ w_gate_up, 2, axis=-1)
    return (jax.nn.silu(g) * u) @ w_down

def setup_inputs(seed: int = 0) -> dict:
    key = jax.random.key(seed)
    ks = jax.random.split(key, 22)
    f32 = jnp.float32
    L = DEPTH

    def nrm(k, shape, scale):
        return jax.random.normal(k, shape, f32) * scale

    x = nrm(ks[0], (BATCH, SEQ, D_MODEL), 1.0)
    c = nrm(ks[1], (BATCH, D_MODEL), 1.0)
    w_mod = nrm(ks[2], (L, D_MODEL, N_MOD * D_MODEL), 0.01)
    b_mod = nrm(ks[3], (L, N_MOD * D_MODEL), 0.01)
    w_in = nrm(ks[4], (L, D_MODEL, D_IN_PROJ), D_MODEL ** -0.5)
    conv_w = nrm(ks[5], (L, CONV_WIDTH, SSD_XBC), CONV_WIDTH ** -0.5)
    conv_b = nrm(ks[6], (L, SSD_XBC), 0.02)
    dt0 = jnp.exp(jax.random.uniform(ks[7], (L, SSD_HEADS), f32, math.log(1e-3), math.log(1e-1)))
    dt_bias = dt0 + jnp.log(-jnp.expm1(-dt0))
    a_log = jnp.log(jax.random.uniform(ks[8], (L, SSD_HEADS), f32, 1.0, 16.0))
    d_skip = 1.0 + nrm(ks[9], (L, SSD_HEADS), 0.02)
    ssd_norm_w = 1.0 + nrm(ks[10], (L, SSD_WIDTH), 0.02)
    lam_qk = nrm(ks[11], (L, 4, DIFF_HEAD_DIM), 0.1)
    attn_norm_w = 1.0 + nrm(ks[12], (L, DIFF_V_DIM), 0.02)
    w_out = nrm(ks[13], (L, D_MIX, D_MODEL), BETA * D_MIX ** -0.5)
    ln1_g = 1.0 + nrm(ks[14], (L, D_MODEL), 0.02)
    ln1_b = nrm(ks[15], (L, D_MODEL), 0.02)
    w_gate_up = nrm(ks[16], (L, D_MODEL, 2 * D_FF), D_MODEL ** -0.5)
    w_down = nrm(ks[17], (L, D_FF, D_MODEL), BETA * D_FF ** -0.5)
    ln2_g = 1.0 + nrm(ks[18], (L, D_MODEL), 0.02)
    ln2_b = nrm(ks[19], (L, D_MODEL), 0.02)
    return {'x': x, 'c': c, 'w_mod': w_mod, 'b_mod': b_mod, 'w_in': w_in,
            'conv_w': conv_w, 'conv_b': conv_b, 'dt_bias': dt_bias, 'a_log': a_log,
            'd_skip': d_skip, 'ssd_norm_w': ssd_norm_w, 'lam_qk': lam_qk,
            'attn_norm_w': attn_norm_w, 'w_out': w_out, 'ln1_g': ln1_g, 'ln1_b': ln1_b,
            'w_gate_up': w_gate_up, 'w_down': w_down, 'ln2_g': ln2_g, 'ln2_b': ln2_b}

def reference(x, c, w_mod, b_mod, w_in, conv_w, conv_b, dt_bias, a_log, d_skip,
              ssd_norm_w, lam_qk, attn_norm_w, w_out, ln1_g, ln1_b, w_gate_up,
              w_down, ln2_g, ln2_b):
    cos, sin = rope_tables(x.shape[1], DIFF_HEAD_DIM)
    cond = jax.nn.silu(c)
    for l in range(DEPTH):
        mod = (cond @ w_mod[l] + b_mod[l])[:, None, :]
        shift1, scale1, gate1, shift2, scale2, gate2 = jnp.split(mod, N_MOD, axis=-1)
        lambda_init = 0.8 - 0.6 * math.exp(-0.3 * l)
        h = x * (1.0 + scale1) + shift1
        y = hybrid_mixer(h, w_in[l], conv_w[l], conv_b[l], dt_bias[l], a_log[l], d_skip[l],
                         ssd_norm_w[l], lam_qk[l], attn_norm_w[l], w_out[l],
                         lambda_init, cos, sin)
        x = layer_norm(ALPHA * x + (1.0 + gate1) * y, ln1_g[l], ln1_b[l])
        h = x * (1.0 + scale2) + shift2
        y = swiglu(h, w_gate_up[l], w_down[l])
        x = layer_norm(ALPHA * x + (1.0 + gate2) * y, ln2_g[l], ln2_b[l])
    return x


_drawn_inputs = setup_inputs


def setup_inputs(seed=0):
    import zlib

    import numpy as np

    out = dict(_drawn_inputs(seed))
    spreads = {}
    factors = {'b_mod': 3.553, 'conv_b': 5.262, 'd_skip': 8.0, 'ssd_norm_w': 8.0, 'attn_norm_w': 8.0}
    for name, (base, spread) in spreads.items():
        noise = np.random.default_rng([zlib.crc32(name.encode()), seed]).standard_normal(out[name].shape)
        drawn = base * np.exp(spread * noise) if base else spread * noise
        out[name] = __import__('jax').numpy.asarray(drawn.astype(out[name].dtype))
    for name, factor in factors.items():
        out[name] = (out[name] * factor).astype(out[name].dtype)
    return out
```

```python
import math
from contextlib import ExitStack

import numpy as np

import concourse.bass as bass
from concourse import mybir

F32 = mybir.dt.float32
F32R = mybir.dt.float32r
BF16 = mybir.dt.bfloat16
ALU = mybir.AluOpType
ACT = mybir.ActivationFunctionType
AXX = mybir.AxisListType.X

P = 128
LAYERS = 2
D = 1024
SEQ = 512
CH = SEQ // P
KD = D // P
HEADS = 8
HDIM = 64
AH = 4
D_FF = 2816
FT = D_FF // P
EPS = 1e-5
ALPHA = (2 * LAYERS) ** 0.25
NEG = -1.0e30
RING = 4

GROUPS = ["xs", "bc", "q", "k", "v", "z", "out0", "out1"] + [f"mlp{g}" for g in range(FT // 2)] + ["down0", "down1"]
NG = len(GROUPS)
MLP_G = FT // 2
U_MLP = 32
U_DOWN = U_MLP + 4 * MLP_G
DOWN_SLABS = FT // 2
UNITS = U_DOWN + 2 * DOWN_SLABS
MOD_BLOCKS = 12
MOD_FRONT = 4
MOD_A_UNITS = 12
MOD_DOWN = 12

C_BMOD, C_LN1G, C_LN1B, C_LN2G, C_LN2B = 0, 48, 56, 64, 72
C_CONVW, C_CONVB, C_ATTNW, C_DTB, C_ALOG, C_DSKIP = 80, 112, 120, 121, 129, 137
NPAR = 145


def mod_block(i):
    if i < 10:
        return 0, i
    if i < 22:
        return 1, i - 10
    return 0, i - 12


def mod_bank(i):
    return 6 if i < 10 else 7


def raw_of(l, u):
    if u >= UNITS:
        return raw_of(l + 1, u - UNITS)
    if l == 0:
        front = 4 * MOD_FRONT
        if u < MOD_A_UNITS:
            return front + 3 * u
        if u < U_MLP:
            return front + 2 * MOD_A_UNITS + u
        i = u - U_MLP
        at = front + 2 * MOD_A_UNITS + U_MLP
        both = 4 * MLP_G + MOD_DOWN
        return at + 2 * i if i < both else at + both + i
    return raw_of(0, UNITS - 1) + 1 + u


def group_of(u):
    if u < U_DOWN:
        return u // 4, u % 4, 4
    return NG - 2 + (u - U_DOWN) // DOWN_SLABS, (u - U_DOWN) % DOWN_SLABS, DOWN_SLABS


def kernel_body(nc, xT, ccol, w_mod, w_in, w_out, w_gu, w_down, par, ssdw, lamqk, wdt, consts, rope, outT):
    ctx = ExitStack()
    with ctx:
        base = nc.sbuf_base
        base += -base % 32
        used = [0]

        def place(name, shape, dt, at=None):
            size = int(np.prod(shape[1:])) * (2 if dt == BF16 else 4)
            off = used[0] if at is None else at
            if at is None:
                used[0] += size + (-size) % 32
            return nc.alloc_sbuf_tensor_at(name, shape, dt, offset=base + off)

        KB = 1024
        xr = place("residual", [P, KD, SEQ], F32)
        h_hi = place("h_hi", [P, KD, SEQ], F32R)
        h_lo = place("h_lo", [P, KD, SEQ], F32R)
        F0 = used[0]
        used[0] += 88 * KB
        T0 = used[0]
        used[0] += 12 * KB
        f_hi = place("f_hi", [P, FT, SEQ], F32R, F0)
        f_lo = place("f_lo", [P, FT, SEQ], F32R, F0 + 44 * KB)
        conv_in = place("conv_in", [P, 8, SEQ + 3], F32, F0)
        q = place("q", [P, AH, SEQ], F32, F0)
        kpad = place("kpad", [P, 2, AH, SEQ], F32, F0 + 8 * KB)
        v = place("v", [P, CH, SEQ], F32, F0 + 24 * KB)
        xsF = place("xsF", [P, 4, SEQ], F32, F0 + 32 * KB)
        zs = place("zs", [P, CH, SEQ], F32, F0 + 32 * KB)
        yt = place("y_tok", [P, CH, SEQ], F32, F0 + 40 * KB)
        bcF = place("bcF", [P, 4, SEQ], F32, F0 + 48 * KB)
        xs_tok = place("xs_tok", [P, CH, SEQ], F32, F0 + 56 * KB)
        y_hi = place("y_hi", [P, KD, SEQ], F32R, F0 + 48 * KB)
        b_tok = place("b_tok", [P, CH, 256], F32, F0 + 64 * KB)
        xdt = place("xdt", [P, SEQ], F32, F0 + 68 * KB)
        xdec = place("xdec", [P, SEQ], F32, F0 + 70 * KB)
        lm = place("decay_l", [P, HEADS, P], F32, F0 + 72 * KB)
        mm = place("m_t", [P, HEADS, P], F32, F0 + 76 * KB)
        conv_th = place("conv_th", [P, 2, SEQ], F32, F0 + 76 * KB)
        y_lo = place("y_lo", [P, KD, SEQ], F32R, F0 + 64 * KB)
        o_tok = place("o_tok", [P, SEQ], F32, F0 + 80 * KB)
        junk = place("junk", [P, SEQ], F32, F0 + 82 * KB)
        cosT = place("cosT", [P, SEQ], F32, F0 + 84 * KB)
        sinT = place("sinT", [P, SEQ], F32, F0 + 86 * KB)
        ssdw_row = place("ssdw_row", [P, SEQ], F32, F0 + 84 * KB)
        s1 = place("s1", [P, SEQ], F32, T0)
        s2 = place("s2", [P, SEQ], F32, T0 + 2 * KB)
        sq = place("sq", [P, 2, SEQ], F32, T0 + 4 * KB)
        diag = place("diag", [P, 2, CH, P], F32, T0 + 4 * KB)
        h32 = place("h32", [P, 2, SEQ], F32, T0 + 8 * KB)
        rot = place("rot", [P, 2, SEQ], F32, T0)
        state = place("state", [P, SEQ], F32, T0 + 4 * KB)
        prob = place("prob", [P, 2, 2, SEQ], F32, T0)
        wT = place("wT", [P, 2, CH, P], F32, T0 + 8 * KB)
        lamt = place("lamt", [P, LAYERS, 4, 64], F32, T0)
        lamp = place("lamp", [P, LAYERS, 2, 64], F32, T0 + 2 * KB)
        raw = place("raw", [P, RING, 2, SEQ], F32)
        w_hi = place("w_hi", [P, RING, 2, SEQ], F32R)
        w_lo = place("w_lo", [P, RING, 2, SEQ], F32R)
        macc = place("mod_acc", [P, SEQ], F32)
        cst = place("consts", [P, 4 * P], F32)
        ident, tri, maskf, ones = (cst[:, i * P:(i + 1) * P] for i in range(4))
        maskb = place("mask_bf", [P, P], BF16)
        identb = place("ident_bf", [P, P], BF16)
        meancol = place("meancol", [P, 1], F32)
        prm = place("params", [P, LAYERS, NPAR], F32)
        modc = place("modc", [P, LAYERS, 48], F32)
        cond = place("cond", [P, 3, KD], F32)
        cvec = cond[:, 0, :]
        wdt_raw = place("wdt_raw", [P, KD, HEADS], F32)
        wdt_hi = place("wdt_hi", [P, KD, HEADS], F32R)
        wdt_lo = place("wdt_lo", [P, KD, HEADS], F32R)
        dts = place("dts", [P, 12, CH * HEADS], F32)
        (DU, DA, DE, DW, DN, DL, DT, DAA, DCS, DEA, DDEC, DTOT) = range(12)
        expa = place("expa", [P, LAYERS, HEADS], F32)
        lam = place("lam", [P, LAYERS, 4], F32)
        awc = place("attn_w", [P, LAYERS], F32)
        att = place("att_small", [P, 4, 2 * AH], F32)
        nrm = place("norm_small", [P, 6, 8], F32)
        ssq = place("ssq", [P, 8], F32)
        vecs = place("ln_vecs", [P, 6, KD], F32)
        (VGP, VS, VG, VB, VAG, VAB) = range(6)
        assert base + used[0] <= nc.sbuf_usable_end, (used[0], nc.sbuf_usable_end - base)

        ps = ctx.enter_context(nc.psum_tensor("ps", [P, 8, SEQ], F32))

        def sem(name):
            return ctx.enter_context(nc.semaphore(name))

        raw_loaded = [sem(f"raw_loaded{i}") for i in range(RING)]
        small_loaded = sem("small_loaded")
        c_loaded = sem("c_loaded")
        x_loaded = sem("x_loaded")
        wdt_loaded = sem("wdt_loaded")
        rope_loaded = sem("rope_loaded")
        ssdw_loaded = sem("ssdw_loaded")
        hi_ready = sem("hi_ready")
        slab_split = sem("slab_split")
        slab_used = sem("slab_used")
        bank_done = sem("bank_done")
        dve_chain = sem("dve_chain")
        act_chain = sem("act_chain")
        consts_ready = sem("consts_ready")
        cond_half = sem("cond_half")
        cond_tanh = sem("cond_tanh")
        lam_sums = sem("lam_sums")
        lam_exp = sem("lam_exp")
        mod_mm = sem("mod_mm")
        mod_col = sem("mod_col")
        vec_ready = sem("vec_ready")
        h_hi_ready = sem("h_hi_ready")
        h_ready = sem("h_ready")
        xa_ready = sem("xa_ready")
        wdt_hi_ready = sem("wdt_hi_ready")
        wdt_ready = sem("wdt_ready")
        conv_raw = sem("conv_raw")
        pads_ready = sem("pads_ready")
        conv_lin = sem("conv_lin")
        conv_tanh = sem("conv_tanh")
        conv_out = sem("conv_out")
        dt_mm = sem("dt_mm")
        dt_abs = sem("dt_abs")
        dt_exp = sem("dt_exp")
        dt_w = sem("dt_w")
        dt_ln = sem("dt_ln")
        a_ready = sem("a_ready")
        cs_mm = sem("cs_mm")
        cs_ready = sem("cs_ready")
        cs_exp = sem("cs_exp")
        ssd_p1 = sem("ssd_p1")
        tok_copied = sem("tok_copied")
        l_ready = sem("l_ready")
        m_ready = sem("m_ready")
        xd_ready = sem("xd_ready")
        ssd_p2 = sem("ssd_p2")
        skip_ready = sem("skip_ready")
        ssd_d2 = sem("ssd_d2")
        qk_raw = sem("qk_raw")
        rot_dma = [sem(f"rot_dma{i}") for i in range(2)]
        rope_done = sem("rope_done")
        pad_half = sem("pad_half")
        kpad_ready = sem("kpad_ready")
        v_ready = sem("v_ready")
        z_tanh = sem("z_tanh")
        z_ready = sem("z_ready")
        gated = sem("gated")
        gate_sq = sem("gate_sq")
        ssd_v = sem("ssd_v")
        ssd_y0 = sem("ssd_y0")
        ys_scaled = sem("ys_scaled")
        trs_mm = sem("trs_mm")
        ys_hi = sem("ys_hi")
        ys_ready = sem("ys_ready")
        qk_done = sem("qk_done")
        nb_ready = sem("nb_ready")
        exp_done = sem("exp_done")
        w_ready = sem("w_ready")
        wt_mm = sem("wt_mm")
        wt_ready = sem("wt_ready")
        pv_done = sem("pv_done")
        o_copied = sem("o_copied")
        o_sq = sem("o_sq")
        att_v = sem("att_v")
        att_y0 = sem("att_y0")
        o_scaled = sem("o_scaled")
        tro_mm = sem("tro_mm")
        yo_hi = sem("yo_hi")
        yo_ready = sem("yo_ready")
        ln_r = sem("ln_r")
        ln_s1 = sem("ln_s1")
        ln_sq = sem("ln_sq")
        ln_s2 = sem("ln_s2")
        ln_stats = sem("ln_stats")
        ln_v = sem("ln_v")
        ln_y0 = sem("ln_y0")
        ln_diag = sem("ln_diag")
        ln_rows = sem("ln_rows")
        ln_t = sem("ln_t")
        h32_ready = sem("h32_ready")
        mlp_th = sem("mlp_th")
        mlp_a = sem("mlp_a")
        mlp_f = sem("mlp_f")
        f_hi_ready = sem("f_hi_ready")
        f_ready = sem("f_ready")
        out_tile = sem("out_tile")
        out_stored = sem("out_stored")

        def wait_loaded(eng, r, it=0, step=0):
            eng.wait_ge(raw_loaded[r % RING], 16 * (r // RING + 1) + (16 * step // RING) * it)

        def wait_used(eng, s, it=0):
            if s < 0:
                return
            l, u = divmod(s, UNITS)
            g, j, n = group_of(u)
            if j == n - 1:
                eng.wait_ge(bank_done, 4 * (NG * l + g + 1) + 4 * it)
            else:
                before = (UNITS - NG) * l + (3 * g if u < U_DOWN else 3 * (NG - 2) + (n - 1) * (g - NG + 2))
                eng.wait_ge(slab_used, before + j + 1 + 3 * it)

        def raw_step(l):
            return 8 if l == 0 else 4

        block = ctx.enter_context(nc.Block())

        @block.sync
        def _(sp):
            def w_src(l, u, it=0):
                g, j, _ = group_of(u)
                rows = slice(2 * j * P, 2 * (j + 1) * P)
                if u < 24:
                    return w_in[l, rows, g * SEQ:(g + 1) * SEQ].rearrange("(k p) n -> p k n", p=P)
                if u < U_MLP:
                    return w_out[l, rows, (g - 6) * SEQ:(g - 5) * SEQ].rearrange("(k p) n -> p k n", p=P)
                return w_down[l, rows, (g - NG + 2) * SEQ:(g - NG + 3) * SEQ].rearrange("(k p) n -> p k n", p=P)

            def room(r, it=0, step=0):
                if r >= RING:
                    sp.wait_ge(slab_split, r - RING + 1 + step * it)

            def load_w(l, u):
                r = raw_of(l, u)
                room(r)
                sp.dma_start(raw[:, r % RING, :, :], w_src(l, u)).then_inc(raw_loaded[r % RING], 16)

            def load_gu(l, j, it):
                r = raw_of(l, U_MLP + j)
                room(r, it, raw_step(l))
                src = w_gu[l, 2 * j * P:2 * (j + 1) * P, :].rearrange("(k p) n -> p k n", p=P)
                sp.dma_start(raw[:, r % RING, :, :], src[:, :, bass.ds(it * SEQ, SEQ)])\
                  .then_inc(raw_loaded[r % RING], 16)

            def load_mod(r, lb, j, it=0, step=0, blk=0):
                room(r, it, step)
                src = w_mod[lb, 2 * j * P:2 * (j + 1) * P, :].rearrange("(k p) n -> p k n", p=P)
                sp.dma_start(raw[:, r % RING, :, :], src[:, :, bass.ds(blk * SEQ, SEQ)])\
                  .then_inc(raw_loaded[r % RING], 16)

            for r in range(4 * MOD_FRONT):
                load_mod(r, 0, r % 4, blk=r // 4)
            for l in range(LAYERS):
                if l:
                    sp.wait_ge(bank_done, 4 * NG * l)
                sp.dma_start(cosT[:, :], rope[0]).then_inc(rope_loaded, 16)
                sp.dma_start(sinT[:, :], rope[1]).then_inc(rope_loaded, 16)
                sp.dma_start(wdt_raw[:, :, :], wdt[l]).then_inc(wdt_loaded, 16)
                for u in range(U_MLP):
                    load_w(l, u)
                    if l == 0 and u < MOD_A_UNITS:
                        for i in (2 * u, 2 * u + 1):
                            load_mod(raw_of(0, u) + 1 + i % 2, 0, i % 4, blk=MOD_FRONT + i // 4)
                    if u == 24:
                        sp.wait_ge(rope_done, 8 * (l + 1))
                        sp.dma_start(ssdw_row[:, :], ssdw[l]).then_inc(ssdw_loaded, 16)
                with sp.Fori(0, MLP_G) as g:
                    for j in range(4):
                        load_gu(l, j, g)
                        if l == 0:
                            load_mod(raw_of(0, U_MLP + j) + 1, 1, j, it=g, step=8, blk=g)
                for u in range(U_DOWN, UNITS):
                    load_w(l, u)
                    i = u - U_DOWN
                    if l == 0 and i < MOD_DOWN:
                        lb, blk = mod_block(21 + i // 4)
                        load_mod(raw_of(0, u) + 1, lb, i % 4, blk=blk)
            for k in range(KD):
                sp.wait_ge(out_tile, k + 1)
                sp.dma_start(outT[k * P:(k + 1) * P, :], xr[:, k, :]).then_inc(out_stored, 16)
            sp.wait_ge(out_stored, 16 * KD)

        @block.tensor
        def _(pe):
            def slab(l, u, act_hi, act_lo, ready, weights_move=False, bank_free=None, it=0):
                s = UNITS * l + u
                g, j, n = group_of(u)
                step = raw_step(l)
                pe.wait_ge(slab_split, raw_of(l, u) + 1 + step * it)
                c = s % RING
                for kk in range(2):
                    k = 2 * j + kk
                    ready(k)
                    for m in range(4):
                        if k == 0 and bank_free:
                            bank_free(m)
                        cols = slice(m * P, (m + 1) * P)
                        if weights_move:
                            trio = [(act_hi[:, k, cols], w_hi[:, c, kk, :]), (act_hi[:, k, cols], w_lo[:, c, kk, :]),
                                    (act_lo[:, k, cols], w_hi[:, c, kk, :])]
                        else:
                            trio = [(w_hi[:, c, kk, cols], act_hi[:, k, :]), (w_hi[:, c, kk, cols], act_lo[:, k, :]),
                                    (w_lo[:, c, kk, cols], act_hi[:, k, :])]
                        for i, (stat, mov) in enumerate(trio):
                            mmi = pe.matmul(ps[:, m, :], stat, mov, start=(k == 0 and i == 0),
                                            stop=(k == 2 * n - 1 and i == 2))
                        if k == 2 * n - 1:
                            mmi.then_inc(bank_done, 1)
                    yield_after(l, u, kk)
                if j < n - 1:
                    mmi.then_inc(slab_used, 1)

            def mod_reduce(i, it=0):
                if i < MOD_FRONT:
                    r = 4 * i + 3
                elif i < 10:
                    r = raw_of(0, 2 * (i - MOD_FRONT) + 1) + 2
                else:
                    r = raw_of(0, U_MLP + 4 * (i - 10) + 3) + 1
                pe.wait_ge(slab_split, r + 1 + 8 * it)
                for j in range(4):
                    last = pe.matmul(ps[:, mod_bank(i), j:j + 1], macc[:, j * P:(j + 1) * P], ones[:, 0:1],
                                     start=True, stop=True)
                last.then_inc(mod_mm, 1)

            def dt_project(l):
                pe.wait_ge(wdt_ready, l + 1)
                for c in range(CH):
                    for k in range(KD):
                        tok = slice(c * P, (c + 1) * P)
                        for i, (a, w) in enumerate([(h_hi, wdt_hi), (h_hi, wdt_lo), (h_lo, wdt_hi)]):
                            last = pe.matmul(ps[:, 7, c * HEADS:(c + 1) * HEADS], a[:, k, tok], w[:, k, :],
                                             start=(k == 0 and i == 0), stop=(k == KD - 1 and i == 2))
                last.then_inc(dt_mm, 1)

            def cumsum(l):
                pe.wait_ge(a_ready, l + 1)
                pe.matmul(ps[:, 7, 32:64], tri, dts[:, DAA, :], start=True, stop=True)
                pe.matmul(ps[:, 7, 64:96], ones, dts[:, DAA, :], start=True, stop=True).then_inc(cs_mm, 1)

            def ssd_first(l, c):
                if c == 0:
                    pe.wait_ge(conv_out, 8 * (l + 1))
                    pe.wait_ge(cs_ready, l + 1)
                    pe.wait_ge(cs_exp, l + 1)
                else:
                    pe.wait_ge(ssd_d2, CH * l + c)
                tok = slice(c * P, (c + 1) * P)
                for j in range(4):
                    pe.transpose(ps[:, 6, j * P:(j + 1) * P], xsF[:, j, tok], ident)
                for g in range(2):
                    pe.transpose(ps[:, 7, 256 + g * P:256 + (g + 1) * P], bcF[:, g, tok], ident)
                for g in range(2):
                    pe.matmul(ps[:, 7, g * P:(g + 1) * P], bcF[:, g, tok], bcF[:, 2 + g, tok], start=True, stop=True)
                for b in range(2):
                    bank = ps[:, 4 + b, :].rearrange("p (e t) -> p e t", e=4)
                    pe.matmul(bank, identb[:, :], maskb[:, :].unsqueeze(1).to_broadcast([P, 4, P]), start=True, stop=False,
                              skip_group_check=True)
                    for e in range(4):
                        col = c * HEADS + 4 * b + e
                        last = pe.matmul(bank[:, e, :], dts[:, DAA, col:col + 1].to_broadcast([P, P]), tri,
                                         start=False, stop=(e == 3), skip_group_check=True)
                last.then_inc(ssd_p1, 1)

            def ssd_second(l, c):
                pe.wait_ge(m_ready, CH * l + c + 1)
                pe.wait_ge(xd_ready, CH * l + c + 1)
                tok = slice(c * P, (c + 1) * P)
                for hh in range(HEADS):
                    pd = slice(hh * HDIM, (hh + 1) * HDIM)
                    pe.matmul(ps[:, 4, pd], mm[:, hh, :], xdt[:, pd], start=True, stop=True)
                if c > 0:
                    for g in range(2):
                        gd = slice(g * 256, (g + 1) * 256)
                        pe.matmul(ps[:, 5, gd], bcF[:, 2 + g, tok], state[:, gd], start=True, stop=True)
                pe.wait_ge(tok_copied, CH * l + c + 1)
                for g in range(2):
                    gd = slice(g * 256, (g + 1) * 256)
                    last = pe.matmul(ps[:, 6, gd], b_tok[:, c, g * P:(g + 1) * P], xdec[:, gd], start=True, stop=True)
                last.then_inc(ssd_p2, 1)

            def qk(l, t):
                i, h = divmod(t, AH)
                if t == 0:
                    pe.wait_ge(rope_done, 8 * (l + 1))
                    pe.wait_ge(kpad_ready, AH * (l + 1))
                    pe.wait_ge(ssd_d2, CH * (l + 1))
                else:
                    pe.wait_ge(exp_done, 16 * l + t)
                n = (i + 1) * P
                for m in range(2):
                    pe.matmul(ps[:, 4 + m, 0:n], q[:, h, i * P:(i + 1) * P], kpad[:, m, h, 0:n], start=True, stop=False,
                              skip_group_check=True)
                    last = pe.matmul(ps[:, 4 + m, i * P:n], maskb[:, :], identb[:, :], start=False, stop=True,
                                     skip_group_check=True)
                last.then_inc(qk_done, 1)

            def turn_w(l, t):
                pe.wait_ge(w_ready, 16 * l + t + 1)
                if t:
                    pe.wait_ge(wt_ready, 16 * l + t)
                for j in range(t // AH + 1):
                    last = pe.transpose(ps[:, 6, j * P:(j + 1) * P], prob[:, t % 2, 0, j * P:(j + 1) * P], ident)
                last.then_inc(wt_mm, 1)

            def pv(l, t):
                i, h = divmod(t, AH)
                pe.wait_ge(wt_ready, 16 * l + t + 1)
                if t == 0:
                    pe.wait_ge(v_ready, CH * (l + 1))
                if h == 0 and i:
                    pe.wait_ge(o_copied, CH * l + i)
                    pe.wait_ge(o_sq, CH * l + i)
                for j in range(i + 1):
                    last = pe.matmul(ps[:, 7, h * P:(h + 1) * P], wT[:, t % 2, j, :], v[:, j, h * P:(h + 1) * P],
                                     start=(j == 0), stop=(j == i))
                last.then_inc(pv_done, 1)

            def turn_o(l, i):
                pe.wait_ge(o_scaled, CH * l + i + 1)
                for h in range(AH):
                    last = pe.transpose(ps[:, 6, h * P:(h + 1) * P], o_tok[:, h * P:(h + 1) * P], ident)
                last.then_inc(tro_mm, 1)

            def step(l, t):
                if t < 16:
                    qk(l, t)
                if 1 <= t <= 16:
                    turn_w(l, t - 1)
                if 2 <= t <= 17:
                    pv(l, t - 2)
                if t >= 7 and t % 4 == 3:
                    i = (t - 7) // 4
                    pe.wait_ge(wt_ready, 16 * l + min(t, 16))
                    turn_o(l, i)
                    pe.wait_ge(yo_hi, CH * l + i + 1)
                    pe.wait_ge(yo_ready, CH * l + i + 1)

            def turn_ys(l):
                for c in range(CH):
                    pe.wait_ge(ys_scaled, CH * l + c + 1)
                    if c:
                        pe.wait_ge(ys_hi, CH * l + c)
                        pe.wait_ge(ys_ready, CH * l + c)
                    for j in range(4):
                        last = pe.transpose(ps[:, 6, j * P:(j + 1) * P], yt[:, c, j * P:(j + 1) * P], ident)
                    last.then_inc(trs_mm, 1)
                pe.wait_ge(ys_hi, CH * (l + 1))
                pe.wait_ge(ys_ready, CH * (l + 1))

            def ln_sums(n):
                pe.wait_ge(ln_s1, 7 * (n + 1))
                pe.wait_ge(ln_s2, 7 * (n + 1))
                for i, src in enumerate((s1, s2)):
                    for c in range(CH):
                        last = pe.matmul(ps[:, 4, 4 * i + c:4 * i + c + 1], src[:, c * P:(c + 1) * P], meancol[:, :],
                                         start=True, stop=True)
                last.then_inc(ln_stats, 1)

            def ln_spread(n):
                for i in range(2):
                    pe.wait_ge(ln_diag, 2 * n + i + 1)
                    pe.matmul(ps[:, 5 + i, :], ones, diag[:, i, :, :], start=True, stop=True).then_inc(ln_rows, 1)

            STEPS = {(21, 1): [0], (22, 0): [1], (22, 1): [2], (23, 0): [3], (23, 1): [4],
                     (24, 0): [8], (24, 1): [9], (25, 0): [10], (25, 1): [11, 12, 13, 14, 15, 16, 17, 18, 19]}

            def yield_after(l, u, kk):
                for t in STEPS.get((u, kk), []):
                    step(l, t)

            pe.wait_ge(consts_ready, 1)
            for i in range(MOD_FRONT):
                mod_reduce(i)
            for l in range(LAYERS):
                def h_tile(k, e=2 * l):
                    pe.wait_ge(h_ready, 8 * e + k + 1)

                def none(k):
                    pass

                def y_tile(k):
                    if k == 0:
                        pe.wait_ge(ys_ready, CH * (l + 1))
                    if k == 4:
                        pe.wait_ge(yo_ready, CH * (l + 1))

                frees = {
                    1: lambda m: pe.wait_ge(conv_raw, 8 * l + m + 1),
                    2: lambda m: pe.wait_ge(conv_raw, 8 * l + 4 + m + 1),
                    3: lambda m: pe.wait_ge(qk_raw, 8 * l + m + 1),
                    4: lambda m: pe.wait_ge(qk_raw, 8 * l + 4 + m + 1),
                    5: lambda m: pe.wait_ge(v_ready, CH * l + m + 1),
                    6: lambda m: pe.wait_ge(z_ready, CH * l + m + 1),
                    7: lambda m: pe.wait_ge(ln_r, 16 * l + m + 1),
                }
                for u in range(U_MLP):
                    g = u // 4
                    if l == 0 and u < 10 and u % 2 == 1 or (l == 0 and u == 0):
                        mod_reduce(MOD_FRONT + (u + 1) // 2)
                    if u == 24:
                        for t in (5, 6, 7):
                            step(l, t)
                        turn_ys(l)
                    if u < 24:
                        slab(l, u, h_hi, h_lo, h_tile if g == 0 else none, weights_move=GROUPS[g] in "vz",
                             bank_free=frees.get(g))
                    else:
                        slab(l, u, y_hi, y_lo, y_tile, bank_free=frees[g])
                    if u == 3:
                        dt_project(l)
                    if u == 6:
                        cumsum(l)
                    if 13 <= u <= 20:
                        c = (u - 13) // 2
                        (ssd_first if (u - 13) % 2 == 0 else ssd_second)(l, c)
                ln_sums(2 * l)
                ln_spread(2 * l)

                def h2_tile(k, e=2 * l + 1):
                    pe.wait_ge(h_ready, 8 * e + k + 1)

                def mlp_group(g, first):
                    def free(m):
                        sm = mlp_a if m < 2 else mlp_f
                        pe.wait_ge(sm, FT * l + m % 2 + 1 + 2 * (g - 1))

                    for j in range(4):
                        if l == 0 and j == 1:
                            mod_reduce(10, it=g)
                        slab(l, U_MLP + j, h_hi, h_lo, h2_tile if first else none, bank_free=None if first else free, it=g)

                mlp_group(0, True)
                with pe.Fori(1, MLP_G) as g:
                    mlp_group(g, False)

                def f_tile(k):
                    pe.wait_ge(f_ready, FT * l + k + 1)

                for u in range(U_DOWN, UNITS):
                    i = u - U_DOWN
                    if l == 0 and i < MOD_DOWN and i % 4 == 1:
                        mod_reduce(21 + i // 4)
                    if i < DOWN_SLABS:
                        free = lambda m: pe.wait_ge(mlp_a if m < 2 else mlp_f, FT * (l + 1) - 1 + m % 2)
                    else:
                        free = lambda m: pe.wait_ge(ln_r, 16 * l + 8 + m + 1)
                    slab(l, u, f_hi, f_lo, f_tile, bank_free=free)
                ln_sums(2 * l + 1)
                ln_spread(2 * l + 1)

        @block.scalar
        def _(act):
            chained = [0]

            def chain(ins):
                chained[0] += 1
                ins.then_inc(act_chain, 1)
                act.wait_ge(act_chain, chained[0])

            def hi(l, u, it=0):
                if UNITS * l + u >= LAYERS * UNITS:
                    return
                s = UNITS * l + u
                r = raw_of(l, u)
                wait_loaded(act, r, it, raw_step(l))
                wait_used(act, s - RING, it)
                act.activation(w_hi[:, s % RING, :, :], raw[:, r % RING, :, :], ACT.Copy).then_inc(hi_ready, 1)

            def affine(e, k):
                n = e - 1
                if n < 0:
                    if k == 0:
                        act.wait_ge(x_loaded, 16)
                else:
                    act.wait_ge(ln_t, 8 * n + k + 1)
                if k == 0:
                    act.wait_ge(vec_ready, e + 1)
                if k >= 2:
                    act.wait_ge(h_ready, 8 * e + k - 1)
                act.activation(h32[:, k % 2, :], xr[:, k, :], ACT.Identity, bias=vecs[:, VB, k:k + 1],
                               scale=vecs[:, VG, k:k + 1]).then_inc(h32_ready, 1)
                act.wait_ge(h32_ready, 8 * e + k + 1)
                act.activation(h_hi[:, k, :], h32[:, k % 2, :], ACT.Copy).then_inc(h_hi_ready, 1)

            def conv_evac(l, t):
                act.wait_ge(bank_done, 4 * (NG * l + t // 4) + t % 4 + 1)
                act.activation(conv_in[:, t, 3:SEQ + 3], ps[:, t % 4, :], ACT.Copy).then_inc(conv_raw, 1)

            def conv_tanhs(l, t):
                act.wait_ge(conv_lin, 8 * l + t + 1)
                if t >= 2:
                    act.wait_ge(conv_out, 8 * l + t - 1)
                src = xsF[:, t, :] if t < 4 else bcF[:, t - 4, :]
                act.activation(conv_th[:, t % 2, :], src, ACT.Tanh).then_inc(conv_tanh, 1)

            def qk_evac(l, t):
                act.wait_ge(bank_done, 4 * (NG * l + 2 + t // 4) + t % 4 + 1)
                dst = q[:, t, :] if t < 4 else kpad[:, 0, t - 4, :]
                act.activation(dst, ps[:, t % 4, :], ACT.Copy).then_inc(qk_raw, 1)

            def ssd_act(l, c):
                act.wait_ge(ssd_p1, CH * l + c + 1)
                act.activation(xs_tok[:, c, :], ps[:, 6, :], ACT.Copy)
                act.activation(b_tok[:, c, :], ps[:, 7, 256:512], ACT.Copy).then_inc(tok_copied, 1)
                if c:
                    act.wait_ge(m_ready, CH * l + c)
                for hh in range(HEADS):
                    col = c * HEADS + hh
                    last = act.activation(lm[:, hh, :], ps[:, 4 + hh // 4, (hh % 4) * P:(hh % 4 + 1) * P], ACT.Exp,
                                          bias=dts[:, DN, col:col + 1])
                last.then_inc(l_ready, 1)

            def exps(l, t):
                i, h = divmod(t, AH)
                act.wait_ge(nb_ready, 16 * l + t + 1)
                if t >= 2:
                    act.wait_ge(wt_mm, 16 * l + t - 1)
                n = (i + 1) * P
                for m in range(2):
                    last = act.activation(prob[:, t % 2, m, 0:n], ps[:, 4 + m, 0:n], ACT.Exp,
                                          bias=att[:, 0, 2 * h + m:2 * h + m + 1], scale=0.125,
                                          accum_out=att[:, 1, 2 * h + m:2 * h + m + 1])
                last.then_inc(exp_done, 1)

            def wt_copy(l, t):
                act.wait_ge(wt_mm, 16 * l + t + 1)
                if t >= 2:
                    act.wait_ge(pv_done, 16 * l + t - 1)
                n = t // AH + 1
                act.activation(wT[:, t % 2, 0:n, :], ps[:, 6, 0:n * P].rearrange("p (j t) -> p j t", j=n), ACT.Copy)\
                   .then_inc(wt_ready, 1)

            def o_squares(l, i):
                act.wait_ge(pv_done, 16 * l + 4 * i + 4)
                for h in range(AH):
                    last = act.activation(junk[:, h * P:(h + 1) * P], ps[:, 7, h * P:(h + 1) * P], ACT.Square,
                                          accum_out=ssq[:, h:h + 1])
                last.then_inc(o_sq, 1)

            def root(v_sem, value, y_sem, n):
                act.wait_ge(v_sem, value)
                chain(act.activation(nrm[:, 1, 0:n], nrm[:, 0, 0:n], ACT.Ln))
                act.activation(nrm[:, 2, 0:n], nrm[:, 1, 0:n], ACT.Exp, scale=-0.5).then_inc(y_sem, 1)

            def yo_high(l, i):
                act.wait_ge(tro_mm, CH * l + i + 1)
                act.activation(y_hi[:, 4:8, i * P:(i + 1) * P], ps[:, 6, :].rearrange("p (h t) -> p h t", h=4),
                               ACT.Copy, scale=awc[:, l:l + 1]).then_inc(yo_hi, 1)

            def step(l, t):
                if 1 <= t <= 16:
                    wt_copy(l, t - 1)
                if t < 16:
                    exps(l, t)
                if t >= 5 and t % 4 == 1:
                    o_squares(l, (t - 5) // 4)
                if t >= 6 and t % 4 == 2:
                    i = (t - 6) // 4
                    root(att_v, CH * l + i + 1, att_y0, 4)
                if t >= 7 and t % 4 == 3:
                    yo_high(l, (t - 7) // 4)

            def squares(n, m):
                act.wait_ge(ln_r, 8 * n + m + 1)
                if m >= 2:
                    act.wait_ge(ln_s2, 7 * n + max(m - 2, 1))
                act.activation(sq[:, m % 2, :], xr[:, m, :], ACT.Square).then_inc(ln_sq, 1)

            def ln_head(n):
                root(ln_v, n + 1, ln_y0, 4)

            def mlp_evac(l, it, last=False):
                for j in range(2):
                    act.wait_ge(bank_done, 4 * (NG * l + 8) + j + 1 + 4 * it)
                    act.activation(sq[:, j, :], ps[:, j, :], ACT.Tanh, scale=0.5).then_inc(mlp_th, 1)
                for j in range(2):
                    act.wait_ge(mlp_f, FT * l + j + 1 + 2 * it)
                    act.activation(f_hi[:, bass.ds(2 * it + j, 1), :], h32[:, j:j + 1, :], ACT.Copy).then_inc(f_hi_ready, 1)

            act.dma_start(cvec, ccol).then_inc(c_loaded, 16)
            act.dma_start(cst[:, :], consts).then_inc(small_loaded, 16)
            act.dma_start(prm[:, :, :], par).then_inc(small_loaded, 16)
            act.dma_start(lamt[:, :, :, :], lamqk).then_inc(small_loaded, 16)
            act.dma_start(xr[:, :, :], xT.rearrange("(k p) t -> p k t", p=P)).then_inc(x_loaded, 16)
            act.preload_act_table_set("exp_and_others")
            act.wait_ge(cond_half, 1)
            act.activation(cond[:, 2, :], cond[:, 1, :], ACT.Tanh).then_inc(cond_tanh, 1)
            act.wait_ge(small_loaded, 48)
            for l in range(LAYERS):
                last = act.activation(expa[:, l, :], prm[:, l, C_ALOG:C_ALOG + HEADS], ACT.Exp)
            act.wait_ge(lam_sums, 1)
            act.activation(lam[:, :, 2:4], lam[:, :, 0:2], ACT.Exp).then_inc(lam_exp, 1)
            hi(0, 0)
            hi(0, 1)
            hi(0, 2)
            affine(0, 0)
            affine(0, 1)
            for l in range(LAYERS):
                for u in range(U_MLP):
                    if u in (4, 8):
                        for t in range(4):
                            conv_evac(l, u - 4 + t)
                    if u in (12, 16):
                        for t in range(4):
                            qk_evac(l, u - 12 + t)
                    if u == 20:
                        for c in range(CH):
                            act.wait_ge(bank_done, 4 * (NG * l + 4) + c + 1)
                            act.activation(v[:, c, :], ps[:, c, :], ACT.Copy).then_inc(v_ready, 1)
                    if u == 24:
                        for c in range(CH):
                            act.wait_ge(bank_done, 4 * (NG * l + 5) + c + 1)
                            act.activation(zs[:, c, :], ps[:, c, :], ACT.Tanh, scale=0.5).then_inc(z_tanh, 1)
                        act.preload_act_table_set("natural_log_exp_and_others")
                    hi(l, u + 3)
                    if u < 3:
                        affine(2 * l, 2 * u + 2)
                        affine(2 * l, 2 * u + 3)
                    if u == 0:
                        act.wait_ge(wdt_loaded, 16 * (l + 1))
                        act.activation(wdt_hi[:, :, :], wdt_raw[:, :, :], ACT.Copy).then_inc(wdt_hi_ready, 1)
                    if u == 4:
                        act.preload_act_table_set("natural_log_exp_and_others")
                        act.wait_ge(dt_abs, l + 1)
                        act.activation(dts[:, DE, :], dts[:, DA, :], ACT.Exp, scale=-1.0).then_inc(dt_exp, 1)
                        act.wait_ge(dt_w, l + 1)
                        act.activation(dts[:, DL, :], dts[:, DW, :], ACT.Ln).then_inc(dt_ln, 1)
                        act.preload_act_table_set("exp_and_others")
                    if 5 <= u <= 12:
                        conv_tanhs(l, u - 5)
                    if u == 7:
                        act.wait_ge(cs_ready, l + 1)
                        act.activation(dts[:, DEA, :], dts[:, DCS, :], ACT.Exp)
                        act.activation(dts[:, DDEC, :], dts[:, DDEC, :], ACT.Exp)
                        act.activation(dts[:, DTOT, :], ps[:, 7, 64:96], ACT.Exp).then_inc(cs_exp, 1)
                    if 14 <= u <= 20 and u % 2 == 0:
                        ssd_act(l, (u - 14) // 2)
                    for t in {21: [0], 22: [1, 2], 23: [3, 4], 24: [5]}.get(u, []):
                        step(l, t)
                    if u == 24:
                        for c in range(CH):
                            act.wait_ge(gated, CH * l + c + 1)
                            for g in range(2):
                                last = act.activation(zs[:, c, g * 256:(g + 1) * 256], yt[:, c, g * 256:(g + 1) * 256], ACT.Square,
                                                      accum_out=nrm[:, 5, 2 * c + g:2 * c + g + 1])
                            last.then_inc(gate_sq, 1)
                        step(l, 6)
                        root(ssd_v, l + 1, ssd_y0, 8)
                        step(l, 7)
                        for c in range(CH):
                            act.wait_ge(trs_mm, CH * l + c + 1)
                            act.activation(y_hi[:, 0:4, c * P:(c + 1) * P], ps[:, 6, :].rearrange("p (h t) -> p h t", h=4),
                                           ACT.Copy).then_inc(ys_hi, 1)
                    for t in {24: [8, 9], 25: [10, 11, 12, 13, 14, 15, 16, 17, 18, 19]}.get(u, []):
                        step(l, t)
                    if u == 28:
                        for m in range(4):
                            squares(2 * l, m)
                hi(l, U_MLP + 3)
                for m in range(4, 8):
                    squares(2 * l, m)
                ln_head(2 * l)
                act.preload_act_table_set("exp_and_others")
                affine(2 * l + 1, 0)
                affine(2 * l + 1, 1)
                for j in range(4):
                    if j:
                        hi(l, U_MLP + j + 3)
                    if j < 3:
                        affine(2 * l + 1, 2 * j + 2)
                        affine(2 * l + 1, 2 * j + 3)
                with act.Fori(1, MLP_G) as g:
                    mlp_evac(l, g - 1)
                    for j in range(4):
                        hi(l, U_MLP + j + 3, it=g)
                for u in range(U_DOWN, UNITS):
                    if u == U_DOWN:
                        mlp_evac(l, MLP_G - 1)
                        act.preload_act_table_set("natural_log_exp_and_others")
                    if u < UNITS - 1 or l + 1 == LAYERS:
                        hi(l, u + 3)
                    if u == U_DOWN + DOWN_SLABS:
                        for m in range(4):
                            squares(2 * l + 1, m)
                for m in range(4, 8):
                    squares(2 * l + 1, m)
                ln_head(2 * l + 1)
                if l + 1 < LAYERS:
                    hi(l, UNITS - 1 + 3)
                    act.preload_act_table_set("exp_and_others")
                    affine(2 * l + 2, 0)
                    affine(2 * l + 2, 1)

        @block.gpsimd
        def _(pool):
            def rotate(l, t):
                src = q[:, t, :] if t < 4 else kpad[:, 0, t - 4, :]
                pool.wait_ge(qk_raw, 8 * l + t + 1)
                if t >= 2:
                    pool.wait_ge(rope_done, 8 * l + t - 1)
                for b in range(4):
                    o = b ^ 1
                    pool.dma_start(rot[32 * b:32 * b + 32, t % 2, :], src[32 * o:32 * o + 32, :])\
                        .then_inc(rot_dma[t % 2], 16)

            def pad(l, h):
                pool.wait_ge(rope_done, 8 * l + 4 + h + 1)
                pool.memset(kpad[64:128, 0, h, :], 0.0).then_inc(pad_half, 1)
                pool.wait_ge(pad_half, AH * l + h + 1)
                pool.memset(kpad[0:64, 1, h, :], 0.0).then_inc(kpad_ready, 1)
                pool.wait_ge(kpad_ready, AH * l + h + 1)

            def skip_term(l, c):
                pool.wait_ge(tok_copied, CH * l + c + 1)
                d = prm[:, l, C_DSKIP:C_DSKIP + HEADS].unsqueeze(2).to_broadcast([P, HEADS, HDIM])
                pool.tensor_tensor(yt[:, c, :].rearrange("p (h d) -> p h d", h=HEADS),
                                   xs_tok[:, c, :].rearrange("p (h d) -> p h d", h=HEADS), d, ALU.mult)\
                    .then_inc(skip_ready, 1)
                pool.wait_ge(skip_ready, CH * l + c + 1)

            def sum_squares(n, m):
                pool.wait_ge(ln_sq, 8 * n + m + 1)
                if m == 1:
                    pool.tensor_tensor(s2[:, :], sq[:, 0, :], sq[:, 1, :], ALU.add).then_inc(ln_s2, 1)
                elif m > 1:
                    pool.wait_ge(ln_s2, 7 * n + m - 1)
                    pool.tensor_tensor(s2[:, :], s2[:, :], sq[:, m % 2, :], ALU.add).then_inc(ln_s2, 1)

            def next_residual(e, k):
                pool.wait_ge(h_hi_ready, 8 * e + k + 1)
                if e == 0:
                    pool.tensor_scalar(xr[:, k, :], xr[:, k, :], ALPHA, 0.0, ALU.mult, ALU.add).then_inc(xa_ready, 1)
                else:
                    pool.tensor_scalar(xr[:, k, :], xr[:, k, :], vecs[:, VAG, k:k + 1], vecs[:, VAB, k:k + 1],
                                       ALU.mult, ALU.add).then_inc(xa_ready, 1)

            for k in range(KD):
                next_residual(0, k)
            for l in range(LAYERS):
                pool.wait_ge(h_ready, 8 * (2 * l + 1))
                pool.memset(conv_in[:, :, 0:3], 0.0).then_inc(pads_ready, 1)
                for t in range(4):
                    rotate(l, t)
                skip_term(l, 0)
                skip_term(l, 1)
                for t in range(4, 8):
                    rotate(l, t)
                    if t >= 6:
                        pad(l, t - 6)
                skip_term(l, 2)
                pad(l, 2)
                skip_term(l, 3)
                pad(l, 3)
                for m in range(8):
                    sum_squares(2 * l, m)
                for k in range(KD):
                    next_residual(2 * l + 1, k)
                for m in range(8):
                    sum_squares(2 * l + 1, m)
                if l + 1 < LAYERS:
                    for k in range(KD):
                        next_residual(2 * l + 2, k)

        @block.vector
        def _(dve):
            chained = [0]

            def chain(ins, loop=0):
                chained[0] += 1
                ins.then_inc(dve_chain, 1)
                dve.wait_ge(dve_chain, chained[0] + loop)

            def split(l, u, it=0):
                if UNITS * l + u >= LAYERS * UNITS:
                    return
                s = UNITS * l + u
                r = raw_of(l, u)
                dve.wait_ge(hi_ready, s + 1 + 4 * it)
                dve.tensor_tensor(w_lo[:, s % RING, :, :], raw[:, r % RING, :, :], w_hi[:, s % RING, :, :].bitcast(F32),
                                  ALU.subtract).then_inc(slab_split, 1)

            def fold_mod(i, j, it=0, loop=0):
                if i < MOD_FRONT:
                    r = 4 * i + j
                elif i < 10:
                    m = 4 * (i - MOD_FRONT) + j
                    r = raw_of(0, m // 2) + 1 + m % 2
                else:
                    r = raw_of(0, U_MLP + 4 * (i - 10) + j) + 1
                step = 8
                wait_loaded(dve, r, it, step)
                if j == 0:
                    if i:
                        dve.wait_ge(mod_mm, i + it)
                    chain(dve.tensor_scalar(macc[:, :], raw[:, r % RING, 0, :], cvec[:, 0:1], None, ALU.mult), loop)
                else:
                    dve.wait_ge(slab_split, r + step * it)
                    chain(dve.scalar_tensor_tensor(macc[:, :], raw[:, r % RING, 0, :], cvec[:, 2 * j:2 * j + 1], macc[:, :],
                                                   ALU.mult, ALU.add), loop)
                dve.scalar_tensor_tensor(macc[:, :], raw[:, r % RING, 1, :], cvec[:, 2 * j + 1:2 * j + 2], macc[:, :],
                                         ALU.mult, ALU.add).then_inc(slab_split, 1)

            def mod_bias(i, it=0):
                lb, blk = mod_block(i)
                dve.wait_ge(mod_mm, i + 1 + it)
                dst = modc[:, lb, bass.ds(4 * it + 4 * blk, 4)]
                bias = prm[:, lb, bass.ds(4 * it + 4 * blk, 4)]
                dve.tensor_tensor(dst, ps[:, mod_bank(i), 0:4], bias, ALU.add).then_inc(mod_col, 1)

            def mod_in_a(u):
                if u >= MOD_A_UNITS:
                    return
                for m in (2 * u, 2 * u + 1):
                    i, j = MOD_FRONT + m // 4, m % 4
                    fold_mod(i, j)
                    if j == 1 and i > MOD_FRONT:
                        mod_bias(i - 1)

            def h_low(e, k):
                dve.wait_ge(h_hi_ready, 8 * e + k + 1)
                dve.tensor_tensor(h_lo[:, k, :], h32[:, k % 2, :], h_hi[:, k, :].bitcast(F32), ALU.subtract)\
                   .then_inc(h_ready, 1)

            def vectors(e):
                n = e - 1
                m = modc
                if n % 2 == 0:
                    l = n // 2
                    dve.wait_ge(mod_col, 10)
                    gate, sc, sh = m[:, l, 16:24], m[:, l, 32:40], m[:, l, 24:32]
                    g, b = prm[:, l, C_LN1G:C_LN1G + KD], prm[:, l, C_LN1B:C_LN1B + KD]
                else:
                    l = n // 2
                    dve.wait_ge(mod_col, 24)
                    gate = m[:, l, 40:48]
                    g, b = prm[:, l, C_LN2G:C_LN2G + KD], prm[:, l, C_LN2B:C_LN2B + KD]
                    if l + 1 < LAYERS:
                        sc, sh = m[:, l + 1, 8:16], m[:, l + 1, 0:8]
                if n:
                    dve.wait_ge(xa_ready, 8 * e)
                chain(dve.tensor_scalar(vecs[:, VGP, :], gate, 1.0, None, ALU.add))
                if n == 2 * LAYERS - 1:
                    return
                chain(dve.tensor_scalar(vecs[:, VS, :], sc, 1.0, None, ALU.add))
                dve.tensor_scalar(vecs[:, VAG, :], g, ALPHA, None, ALU.mult)
                dve.tensor_scalar(vecs[:, VAB, :], b, ALPHA, None, ALU.mult)
                dve.tensor_tensor(vecs[:, VG, :], g, vecs[:, VS, :], ALU.mult)
                chain(dve.tensor_tensor(vecs[:, VB, :], b, vecs[:, VS, :], ALU.mult))
                dve.tensor_tensor(vecs[:, VB, :], vecs[:, VB, :], sh, ALU.add).then_inc(vec_ready, 1)

            def residual(n, m):
                l, w = divmod(n, 2)
                g = NG * l + (6 if w == 0 else NG - 2) + m // 4
                dve.wait_ge(xa_ready, 8 * n + m + 1)
                dve.wait_ge(bank_done, 4 * g + m % 4 + 1)
                dve.scalar_tensor_tensor(xr[:, m, :], ps[:, m % 4, :], vecs[:, VGP, m:m + 1], xr[:, m, :], ALU.mult, ALU.add)\
                   .then_inc(ln_r, 1)
                dve.wait_ge(ln_r, 8 * n + m + 1)
                if m == 1:
                    dve.tensor_tensor(s1[:, :], xr[:, 0, :], xr[:, 1, :], ALU.add).then_inc(ln_s1, 1)
                elif m > 1:
                    dve.wait_ge(ln_s1, 7 * n + m - 1)
                    dve.tensor_tensor(s1[:, :], s1[:, :], xr[:, m, :], ALU.add).then_inc(ln_s1, 1)

            def newton(w):
                v0, y0, a = nrm[:, 0, 0:w], nrm[:, 2, 0:w], nrm[:, 3, 0:w]
                chain(dve.tensor_tensor(a, y0, y0, ALU.mult))
                chain(dve.tensor_tensor(a, a, v0, ALU.mult))
                chain(dve.tensor_scalar(a, a, -0.5, 1.5, ALU.mult, ALU.add))
                chain(dve.tensor_tensor(a, a, y0, ALU.mult))

            def ln_scale(n):
                dve.wait_ge(ln_stats, n + 1)
                st = nrm[:, 4, :]
                chain(dve.tensor_copy(st, ps[:, 4, 0:8]))
                chain(dve.tensor_tensor(nrm[:, 3, 0:4], st[:, 0:4], st[:, 0:4], ALU.mult))
                dve.scalar_tensor_tensor(nrm[:, 0, 0:4], st[:, 4:8], EPS, nrm[:, 3, 0:4], ALU.add, ALU.subtract)\
                   .then_inc(ln_v, 1)
                dve.wait_ge(ln_y0, n + 1)
                newton(4)
                y = nrm[:, 3, 0:4]
                eye = ident.unsqueeze(1).to_broadcast([P, CH, P])
                dve.tensor_tensor(diag[:, 0, :, :], eye, y.unsqueeze(2).to_broadcast([P, CH, P]), ALU.mult)\
                   .then_inc(ln_diag, 1)
                chain(dve.scalar_tensor_tensor(nrm[:, 5, 0:4], st[:, 0:4], -1.0, y, ALU.mult, ALU.mult))
                dve.tensor_tensor(diag[:, 1, :, :], eye, nrm[:, 5, 0:4].unsqueeze(2).to_broadcast([P, CH, P]), ALU.mult)\
                   .then_inc(ln_diag, 1)

            def ln_tiles(n, ks):
                for k in ks:
                    dve.wait_ge(ln_rows, 2 * (n + 1))
                    chain(dve.tensor_tensor(xr[:, k, :], xr[:, k, :], ps[:, 5, :], ALU.mult))
                    dve.tensor_tensor(xr[:, k, :], xr[:, k, :], ps[:, 6, :], ALU.add).then_inc(ln_t, 1)
                if n < 2 * LAYERS - 1:
                    for k in ks:
                        h_low(n + 1, k)

            def conv(l, t):
                dve.wait_ge(conv_raw, 8 * l + t + 1)
                if t == 0:
                    dve.wait_ge(pads_ready, l + 1)
                dst = xsF[:, t, :] if t < 4 else bcF[:, t - 4, :]
                w = prm[:, l, C_CONVW + 4 * t:C_CONVW + 4 * t + 4]
                chain(dve.tensor_scalar(dst, conv_in[:, t, 3:SEQ + 3], w[:, 3:4], prm[:, l, C_CONVB + t:C_CONVB + t + 1],
                                        ALU.mult, ALU.add))
                for i in (2, 1, 0):
                    ins = dve.scalar_tensor_tensor(dst, conv_in[:, t, i:i + SEQ], w[:, i:i + 1], dst, ALU.mult, ALU.add)
                    if i:
                        chain(ins)
                ins.then_inc(conv_lin, 1)

            def conv_end(l, t):
                dve.wait_ge(conv_tanh, 8 * l + t + 1)
                dst = xsF[:, t, :] if t < 4 else bcF[:, t - 4, :]
                dve.scalar_tensor_tensor(dst, conv_th[:, t % 2, :], 1.0, dst, ALU.add, ALU.mult).then_inc(conv_out, 1)

            def dt_first(l):
                dve.wait_ge(dt_mm, l + 1)
                bias = prm[:, l, C_DTB:C_DTB + HEADS].unsqueeze(1).to_broadcast([P, CH, HEADS])
                chain(dve.tensor_tensor(dts[:, DU, :].rearrange("p (c h) -> p c h", c=CH),
                                        ps[:, 7, 0:32].rearrange("p (c h) -> p c h", c=CH), bias, ALU.add))
                dve.scalar_tensor_tensor(dts[:, DA, :], dts[:, DU, :], -1.0, dts[:, DU, :], ALU.mult, ALU.max)\
                   .then_inc(dt_abs, 1)

            def dt_second(l):
                dve.wait_ge(dt_exp, l + 1)
                dve.tensor_scalar(dts[:, DW, :], dts[:, DE, :], 1.0, None, ALU.add).then_inc(dt_w, 1)
                dve.wait_ge(dt_w, l + 1)
                dve.scalar_tensor_tensor(dts[:, DN, :], dts[:, DW, :], -1.0, dts[:, DE, :], ALU.add, ALU.subtract)
                chain(dve.reciprocal(dts[:, DA, :], dts[:, DW, :]))
                chain(dve.tensor_tensor(dts[:, DN, :], dts[:, DN, :], dts[:, DA, :], ALU.mult))
                chain(dve.scalar_tensor_tensor(dts[:, DT, :], dts[:, DU, :], 0.0, dts[:, DN, :], ALU.max, ALU.subtract))
                dve.wait_ge(dt_ln, l + 1)
                chain(dve.tensor_tensor(dts[:, DT, :], dts[:, DT, :], dts[:, DL, :], ALU.add))
                ea = expa[:, l, :].unsqueeze(1).to_broadcast([P, CH, HEADS])
                dve.scalar_tensor_tensor(dts[:, DAA, :].rearrange("p (c h) -> p c h", c=CH),
                                         dts[:, DT, :].rearrange("p (c h) -> p c h", c=CH), -1.0, ea, ALU.mult, ALU.mult)\
                   .then_inc(a_ready, 1)

            def sums(l):
                dve.wait_ge(cs_mm, l + 1)
                chain(dve.tensor_copy(dts[:, DCS, :], ps[:, 7, 32:64]))
                dve.tensor_scalar(dts[:, DN, :], dts[:, DCS, :], -1.0, None, ALU.mult)
                dve.tensor_tensor(dts[:, DDEC, :], ps[:, 7, 64:96], dts[:, DCS, :], ALU.subtract).then_inc(cs_ready, 1)

            def per_head(ap):
                return ap.unsqueeze(2).to_broadcast([P, HEADS, HDIM])

            def heads(ap):
                return ap.rearrange("p (h d) -> p h d", h=HEADS)

            def ssd_mid(l, c):
                cs = slice(c * HEADS, (c + 1) * HEADS)
                if c == 0:
                    dve.wait_ge(cs_exp, l + 1)
                    chain(dve.tensor_tensor(dts[:, DDEC, :], dts[:, DDEC, :], dts[:, DT, :], ALU.mult))
                dve.wait_ge(tok_copied, CH * l + c + 1)
                dve.tensor_tensor(heads(xdt[:, :]), heads(xs_tok[:, c, :]), per_head(dts[:, DT, cs]), ALU.mult)
                dve.tensor_tensor(heads(xdec[:, :]), heads(xs_tok[:, c, :]), per_head(dts[:, DDEC, cs]), ALU.mult)\
                   .then_inc(xd_ready, 1)
                dve.wait_ge(l_ready, CH * l + c + 1)
                for g in range(2):
                    cb = ps[:, 7, g * P:(g + 1) * P].unsqueeze(1).to_broadcast([P, 4, P])
                    last = dve.tensor_tensor(mm[:, 4 * g:4 * g + 4, :], lm[:, 4 * g:4 * g + 4, :], cb, ALU.mult)
                last.then_inc(m_ready, 1)

            def ssd_end(l, c):
                cs = slice(c * HEADS, (c + 1) * HEADS)
                dve.wait_ge(ssd_p2, CH * l + c + 1)
                dve.wait_ge(skip_ready, CH * l + c + 1)
                off = lm[:, 0:4, :].rearrange("p a b -> p (a b)")
                if c:
                    dve.tensor_tensor(heads(off), heads(ps[:, 5, :]), per_head(dts[:, DEA, cs]), ALU.mult)
                chain(dve.tensor_tensor(yt[:, c, :], yt[:, c, :], ps[:, 4, :], ALU.add))
                if c:
                    chain(dve.tensor_tensor(heads(state[:, :]), heads(state[:, :]), per_head(dts[:, DTOT, cs]), ALU.mult))
                    dve.tensor_tensor(yt[:, c, :], yt[:, c, :], off, ALU.add)
                    dve.tensor_tensor(state[:, :], state[:, :], ps[:, 6, :], ALU.add).then_inc(ssd_d2, 1)
                else:
                    dve.tensor_copy(state[:, :], ps[:, 6, :]).then_inc(ssd_d2, 1)
                dve.wait_ge(ssd_d2, CH * l + c + 1)

            def rope_tile(l, t):
                if t == 0:
                    dve.wait_ge(rope_loaded, 32 * (l + 1))
                dve.wait_ge(rot_dma[t % 2], 64 * (4 * l + t // 2 + 1))
                x = q[:, t, :] if t < 4 else kpad[:, 0, t - 4, :]
                r = rot[:, t % 2, :]
                dve.tensor_tensor(r, r, sinT[:, :], ALU.mult)
                chain(dve.tensor_tensor(x, x, cosT[:, :], ALU.mult))
                if t < 4:
                    dve.tensor_tensor(x, x, r, ALU.add).then_inc(rope_done, 1)
                else:
                    h = t - 4
                    dve.tensor_tensor(kpad[0:64, 0, h, :], x[0:64, :], r[0:64, :], ALU.add)
                    dve.tensor_tensor(kpad[64:128, 1, h, :], x[64:128, :], r[64:128, :], ALU.add).then_inc(rope_done, 1)

            def biggest(l, t):
                i, h = divmod(t, AH)
                dve.wait_ge(qk_done, 16 * l + t + 1)
                chain(dve.tensor_reduce(att[:, 2, 2 * h:2 * h + 2], ps[:, 4:6, 0:(i + 1) * P], AXX, ALU.max))
                dve.tensor_scalar(att[:, 0, 2 * h:2 * h + 2], att[:, 2, 2 * h:2 * h + 2], -0.125, None, ALU.mult)\
                   .then_inc(nb_ready, 1)

            def combine(l, t):
                i, h = divmod(t, AH)
                n = (i + 1) * P
                dve.wait_ge(exp_done, 16 * l + t + 1)
                rs = att[:, 3, 2 * h:2 * h + 2]
                chain(dve.reciprocal(rs, att[:, 1, 2 * h:2 * h + 2]))
                dve.tensor_tensor(rs[:, 1:2], rs[:, 1:2], lam[:, l, 0:1], ALU.mult)
                p0, p1 = prob[:, t % 2, 0, 0:n], prob[:, t % 2, 1, 0:n]
                chain(dve.tensor_scalar(p0, p0, rs[:, 0:1], None, ALU.mult))
                dve.scalar_tensor_tensor(p0, p1, rs[:, 1:2], p0, ALU.mult, ALU.add).then_inc(w_ready, 1)

            def o_out(l, i):
                dve.wait_ge(pv_done, 16 * l + 4 * i + 4)
                if i:
                    dve.wait_ge(tro_mm, CH * l + i)
                dve.wait_ge(o_sq, CH * l + i + 1)
                dve.tensor_copy(o_tok[:, :], ps[:, 7, :]).then_inc(o_copied, 1)
                dve.tensor_scalar(nrm[:, 0, 0:4], ssq[:, 0:4], 1.0 / P, EPS, ALU.mult, ALU.add).then_inc(att_v, 1)

            def o_scale(l, i):
                dve.wait_ge(att_y0, CH * l + i + 1)
                newton(4)
                o3 = o_tok[:, :].rearrange("p (h d) -> p h d", h=AH)
                dve.tensor_tensor(o3, o3, nrm[:, 3, 0:4].unsqueeze(2).to_broadcast([P, AH, P]), ALU.mult)\
                   .then_inc(o_scaled, 1)

            def yo_low(l, i):
                tok = slice(i * P, (i + 1) * P)
                dve.wait_ge(yo_hi, CH * l + i + 1)
                dve.scalar_tensor_tensor(y_lo[:, 4:8, tok], ps[:, 6, :].rearrange("p (h t) -> p h t", h=4), awc[:, l:l + 1],
                                         y_hi[:, 4:8, tok].bitcast(F32), ALU.mult, ALU.subtract).then_inc(yo_ready, 1)

            def step(l, t):
                if 1 <= t <= 16:
                    combine(l, t - 1)
                if t < 16:
                    biggest(l, t)
                if t >= 5 and t % 4 == 1:
                    o_out(l, (t - 5) // 4)
                if t >= 6 and t % 4 == 2:
                    o_scale(l, (t - 6) // 4)
                if t >= 7 and t % 4 == 3:
                    yo_low(l, (t - 7) // 4)

            def mlp_end(l, it):
                for j in range(2):
                    dve.wait_ge(mlp_th, FT * l + j + 1 + 2 * it)
                    dve.scalar_tensor_tensor(sq[:, j, :], sq[:, j, :], 1.0, ps[:, j, :], ALU.add, ALU.mult).then_inc(mlp_a, 1)
                for j in range(2):
                    dve.wait_ge(bank_done, 4 * (NG * l + 8) + 2 + j + 1 + 4 * it)
                    dve.wait_ge(mlp_a, FT * l + j + 1 + 2 * it)
                    dve.scalar_tensor_tensor(h32[:, j, :], sq[:, j, :], 0.5, ps[:, 2 + j, :], ALU.mult, ALU.mult)\
                       .then_inc(mlp_f, 1)
                for j in range(2):
                    dve.wait_ge(f_hi_ready, FT * l + j + 1 + 2 * it)
                    dve.tensor_tensor(f_lo[:, bass.ds(2 * it + j, 1), :], h32[:, j:j + 1, :],
                                      f_hi[:, bass.ds(2 * it + j, 1), :].bitcast(F32), ALU.subtract).then_inc(f_ready, 1)

            dve.wait_ge(c_loaded, 16)
            dve.memset(meancol[:, :], 1.0 / D)
            dve.tensor_scalar(cond[:, 1, :], cvec, 0.5, None, ALU.mult).then_inc(cond_half, 1)
            dve.wait_ge(cond_tanh, 1)
            chain(dve.scalar_tensor_tensor(cvec, cond[:, 2, :], 1.0, cond[:, 1, :], ALU.add, ALU.mult))
            fold_mod(0, 0)
            dve.wait_ge(small_loaded, 48)
            dve.tensor_copy(maskb[:, :], maskf)
            dve.tensor_copy(identb[:, :], ident).then_inc(consts_ready, 1)
            lq = lamt[:, :, :, :].rearrange("p l (a b) d -> p l a b d", b=2)
            chain(dve.tensor_tensor(lamp[:, :, :, :], lq[:, :, :, 0, :], lq[:, :, :, 1, :], ALU.mult))
            for l in range(LAYERS):
                last = dve.tensor_reduce(lam[:, l, 0:2], lamp[:, l, :, :], AXX, ALU.add)
            last.then_inc(lam_sums, 1)
            for l in range(LAYERS):
                init = 0.8 - 0.6 * math.exp(-0.3 * l)
                dve.tensor_scalar(prm[:, l, C_CONVW:C_CONVW + 40], prm[:, l, C_CONVW:C_CONVW + 40], 0.5, None, ALU.mult)
                dve.tensor_scalar(awc[:, l:l + 1], prm[:, l, C_ATTNW:C_ATTNW + 1], 1.0 - init, None, ALU.mult)
            dve.wait_ge(lam_exp, 1)
            for l in range(LAYERS):
                init = 0.8 - 0.6 * math.exp(-0.3 * l)
                chain(dve.tensor_tensor(lam[:, l, 0:1], lam[:, l, 3:4], lam[:, l, 2:3], ALU.subtract))
                chain(dve.tensor_scalar(lam[:, l, 0:1], lam[:, l, 0:1], -init, None, ALU.add))
            for i in range(MOD_FRONT):
                for j in range(4):
                    if i or j:
                        fold_mod(i, j)
                mod_bias(i)
            dve.wait_ge(mod_col, MOD_FRONT)
            dve.tensor_scalar(vecs[:, VG, :], modc[:, 0, 8:16], 1.0, None, ALU.add)
            dve.tensor_copy(vecs[:, VB, :], modc[:, 0, 0:8]).then_inc(vec_ready, 1)
            for u in range(3):
                split(0, u)
                mod_in_a(u)
            h_low(0, 0)
            h_low(0, 1)
            for l in range(LAYERS):
                e = 2 * l
                for u in range(U_MLP):
                    if u == 24:
                        for c in range(CH):
                            dve.wait_ge(z_tanh, CH * l + c + 1)
                            dve.scalar_tensor_tensor(zs[:, c, :], zs[:, c, :], 1.0, ps[:, c, :], ALU.add, ALU.mult)\
                               .then_inc(z_ready, 1)
                    split(l, u + 3)
                    if l == 0:
                        mod_in_a(u + 3)
                        if u + 3 >= U_MLP:
                            fold_mod(10, u + 3 - U_MLP)
                    if u == 8 and l == 0:
                        mod_bias(9)
                    if u < 3:
                        if l:
                            ln_tiles(2 * l - 1, [2 * u + 2, 2 * u + 3])
                        else:
                            h_low(0, 2 * u + 2)
                            h_low(0, 2 * u + 3)
                    if u == 0:
                        dve.wait_ge(wdt_hi_ready, l + 1)
                        dve.tensor_tensor(wdt_lo[:, :, :], wdt_raw[:, :, :], wdt_hi[:, :, :].bitcast(F32), ALU.subtract)\
                           .then_inc(wdt_ready, 1)
                    if u == 4:
                        dt_first(l)
                    if 4 <= u <= 11:
                        conv(l, u - 4)
                    if u == 4:
                        dt_second(l)
                    if 5 <= u <= 12:
                        conv_end(l, u - 5)
                    if u == 7:
                        sums(l)
                    if 14 <= u <= 20 and u % 2 == 0:
                        ssd_mid(l, (u - 14) // 2)
                    if 15 <= u <= 21 and u % 2 == 1:
                        ssd_end(l, (u - 15) // 2)
                    if 13 <= u <= 20:
                        rope_tile(l, u - 13)
                    for t in {21: [0], 22: [1, 2], 23: [3, 4], 24: [5]}.get(u, []):
                        step(l, t)
                    if u == 24:
                        for c in range(CH):
                            dve.wait_ge(z_ready, CH * l + c + 1)
                            dve.scalar_tensor_tensor(yt[:, c, :], yt[:, c, :], 0.5, zs[:, c, :], ALU.mult, ALU.mult)\
                               .then_inc(gated, 1)
                        step(l, 6)
                        dve.wait_ge(gate_sq, CH * (l + 1))
                        dve.tensor_scalar(nrm[:, 0, :], nrm[:, 5, :], 1.0 / 256, EPS, ALU.mult, ALU.add).then_inc(ssd_v, 1)
                        dve.wait_ge(ssd_y0, l + 1)
                        newton(8)
                        dve.wait_ge(ssdw_loaded, 16 * (l + 1))
                        for c in range(CH):
                            for g in range(2):
                                gd = slice(g * 256, (g + 1) * 256)
                                last = dve.scalar_tensor_tensor(yt[:, c, gd], yt[:, c, gd],
                                                                nrm[:, 3, 2 * c + g:2 * c + g + 1],
                                                                ssdw_row[:, gd], ALU.mult, ALU.mult)
                            last.then_inc(ys_scaled, 1)
                        step(l, 7)
                        for c in range(CH):
                            tok = slice(c * P, (c + 1) * P)
                            dve.wait_ge(ys_hi, CH * l + c + 1)
                            dve.tensor_tensor(y_lo[:, 0:4, tok], ps[:, 6, :].rearrange("p (h t) -> p h t", h=4),
                                              y_hi[:, 0:4, tok].bitcast(F32), ALU.subtract).then_inc(ys_ready, 1)
                    for t in {24: [8, 9], 25: [10, 11, 12, 13, 14, 15, 16, 17, 18, 19]}.get(u, []):
                        step(l, t)
                    if u == 26:
                        vectors(2 * l + 1)
                    if u == 28:
                        for m in range(4):
                            residual(2 * l, m)
                split(l, U_MLP + 3)
                if l == 0:
                    fold_mod(10, 3)
                for m in range(4, 8):
                    residual(2 * l, m)
                ln_scale(2 * l)
                ln_tiles(2 * l, [0, 1])

                def mlp_mod(j, it, loop):
                    if l:
                        return
                    fold_mod(10, (j + 3) % 4, it=it if j == 0 else it + 1, loop=loop)
                    if j == 2:
                        mod_bias(10, it)

                for j in range(4):
                    if j:
                        split(l, U_MLP + j + 3)
                        if l == 0:
                            fold_mod(11, j - 1)
                            if j == 2:
                                mod_bias(10)
                    if j < 3:
                        ln_tiles(2 * l, [2 * j + 2, 2 * j + 3])
                before = chained[0]
                with dve.Fori(1, MLP_G) as g:
                    loop = (g - 1) * (4 if l == 0 else 0)
                    mlp_end(l, g - 1)
                    for j in range(4):
                        split(l, U_MLP + j + 3, it=g)
                        mlp_mod(j, g, loop)
                if l == 0:
                    assert chained[0] - before == 4
                    chained[0] = before + 4 * (MLP_G - 1)
                for u in range(U_DOWN, UNITS):
                    i = u - U_DOWN
                    if i == 0:
                        mlp_end(l, MLP_G - 1)
                    if i < 2 * DOWN_SLABS - 1 or l + 1 == LAYERS:
                        split(l, u + 3)
                    if l == 0 and i + 3 < MOD_DOWN:
                        fold_mod(21 + (i + 3) // 4, (i + 3) % 4)
                    if l == 0 and i in (2, 6, 10):
                        mod_bias(21 + (i - 2) // 4)
                    if i == 11:
                        vectors(2 * l + 2)
                        for m in range(4):
                            residual(2 * l + 1, m)
                for m in range(4, 8):
                    residual(2 * l + 1, m)
                ln_scale(2 * l + 1)
                if l + 1 < LAYERS:
                    split(l, UNITS - 1 + 3)
                    ln_tiles(2 * l + 1, [0, 1])
                else:
                    ln_tiles(2 * l + 1, range(KD))
                    dve.wait_ge(ln_t, 8 * 2 * LAYERS)
                    for k in range(KD):
                        dve.tensor_scalar(xr[:, k, :], xr[:, k, :], prm[:, l, C_LN2G + k:C_LN2G + k + 1],
                                          prm[:, l, C_LN2B + k:C_LN2B + k + 1], ALU.mult, ALU.add).then_inc(out_tile, 1)


def kernel(**inputs):
    import numpy as _np
    import concourse.bacc as _bacc
    from concourse import mybir as _mybir
    from concourse.bass_utils import run_bass_kernel_spmd as _run

    f = {k: _np.asarray(a) for k, a in inputs.items()}
    L = LAYERS
    SSD_IN = 512

    def cols(a):
        return a.reshape(-1, P).T

    def rows(a):
        return _np.broadcast_to(a.reshape(1, -1), (P, a.size))

    w = f["w_in"]
    z, xbc, dt, qkv = w[:, :, :SSD_IN], w[:, :, SSD_IN:SSD_IN + D], w[:, :, SSD_IN + D:SSD_IN + D + HEADS], \
        w[:, :, SSD_IN + D + HEADS:]
    par = _np.stack([_np.concatenate(
        [cols(f["b_mod"][l]), cols(f["ln1_g"][l]), cols(f["ln1_b"][l]), cols(f["ln2_g"][l]), cols(f["ln2_b"][l])]
        + [f["conv_w"][l][:, t * P:(t + 1) * P].T for t in range(8)]
        + [cols(f["conv_b"][l]), cols(f["attn_norm_w"][l]), rows(f["dt_bias"][l]), rows(f["a_log"][l]),
           rows(f["d_skip"][l])], axis=1) for l in range(L)], axis=1)
    eye = _np.eye(P, dtype=_np.float32)
    tri = _np.triu(_np.ones((P, P), _np.float32))
    mask = ((tri - 1) * _np.float32(-NEG)).astype(_np.float32)
    inv = (1.0 / (_np.float32(10000.0) ** (_np.arange(0, HDIM, 2, dtype=_np.float32) / _np.float32(HDIM))))
    ang = _np.arange(SEQ, dtype=_np.float32)[:, None] * inv.astype(_np.float32)[None, :]
    ang = _np.concatenate([ang, ang], -1).T
    sign = _np.where(_np.arange(HDIM) < HDIM // 2, -1.0, 1.0).astype(_np.float32)[:, None]
    rope = _np.stack([_np.tile(_np.cos(ang), (2, 1)), _np.tile(_np.sin(ang) * sign, (2, 1))]).astype(_np.float32)
    arrays = {
        "xT": f["x"][0].T,
        "ccol": cols(f["c"][0]),
        "w_mod": f["w_mod"],
        "w_in": _np.concatenate([xbc, qkv, z], axis=2),
        "w_out": f["w_out"],
        "w_gu": f["w_gate_up"].reshape(L, D, 2, MLP_G, 256).transpose(0, 1, 3, 2, 4).reshape(L, D, 2 * D_FF),
        "w_down": f["w_down"],
        "par": par,
        "ssdw": _np.stack([rows(f["ssd_norm_w"][l]) for l in range(L)]),
        "lamqk": _np.broadcast_to(f["lam_qk"][None], (P, L, 4, 64)),
        "wdt": dt.reshape(L, KD, P, HEADS).transpose(0, 2, 1, 3),
        "consts": _np.concatenate([eye, tri, mask, _np.ones((P, P), _np.float32)], axis=1),
        "rope": rope,
    }
    arrays = {k: _np.ascontiguousarray(a) for k, a in arrays.items()}
    nc = _bacc.Bacc("TRN2", target_bir_lowering=False, num_devices=1)
    args = [nc.dram_tensor(f"in_{k}", a.shape, _mybir.dt.from_np(a.dtype), kind="ExternalInput").ap()
            for k, a in arrays.items()]
    out = nc.dram_tensor("outT", (D, SEQ), F32, kind="ExternalOutput").ap()
    kernel_body(nc, *args, out)
    r = _run(nc, [{f"in_{k}": a for k, a in arrays.items()}], core_ids=[0])
    return r.results[0]["outT"].T[None]
```

```python
import math
from contextlib import ExitStack

import numpy as np

import concourse.bass as bass
from concourse import mybir

F32 = mybir.dt.float32
F32R = mybir.dt.float32r
BF16 = mybir.dt.bfloat16
ALU = mybir.AluOpType
ACT = mybir.ActivationFunctionType
AXX = mybir.AxisListType.X

P = 128
LAYERS = 2
D = 1024
SEQ = 512
CH = SEQ // P
KD = D // P
HEADS = 8
HDIM = 64
AH = 4
D_FF = 2816
FT = D_FF // P
EPS = 1e-5
ALPHA = (2 * LAYERS) ** 0.25
NEG = -1.0e30
RING = 4

GROUPS = ["xs", "bc", "q", "k", "v", "z", "out_s0", "out_s1", "out_a0", "out_a1"] + \
    [f"mlp{g}" for g in range(FT // 2)] + ["down0", "down1"]
NG = len(GROUPS)
G_OUT, G_MLP = GROUPS.index("out_s0"), GROUPS.index("mlp0")
MLP_G = FT // 2
U_MLP = 32
U_OUT = 24
U_DOWN = U_MLP + 4 * MLP_G
DOWN_SLABS = FT // 2
UNITS = U_DOWN + 2 * DOWN_SLABS
MOD_BLOCKS = 12
MOD_FRONT = 4
MOD_A = [2] * 4 + [1] * 8 + [0] * 17 + [2, 2, 4]
MOD_DOWN = 12

C_BMOD, C_LN1G, C_LN1B, C_LN2G, C_LN2B = 0, 48, 56, 64, 72
C_CONVW, C_CONVB, C_ATTNW, C_DTB, C_ALOG, C_DSKIP = 80, 112, 120, 121, 129, 137
NPAR = 145


def mod_block(i):
    if i < 10:
        return 0, i
    if i < 22:
        return 1, i - 10
    return 0, i - 12


def mod_bank(i):
    return 6 if i < 8 else 7


def raw_of(l, u):
    if u >= UNITS:
        return raw_of(l + 1, u - UNITS)
    if l == 0:
        front = 4 * MOD_FRONT
        if u < U_MLP:
            return front + u + sum(MOD_A[:u])
        i = u - U_MLP
        at = front + sum(MOD_A) + U_MLP
        both = 4 * MLP_G + MOD_DOWN
        return at + 2 * i if i < both else at + both + i
    return raw_of(0, UNITS - 1) + 1 + u


def mod_behind(u):
    first = sum(MOD_A[:u])
    n = MOD_A[u] if u < len(MOD_A) else 0
    return [(MOD_FRONT + m // 4, m % 4, raw_of(0, u) + 1 + m - first) for m in range(first, first + n)]


MOD_LAST = {i: (u, r) for u in range(len(MOD_A)) for i, j, r in mod_behind(u) if j == 3}


def group_of(u):
    if u < U_OUT:
        return u // 4, u % 4, 4
    if u < U_MLP:
        return G_OUT + (u - U_OUT) // 2, (u - U_OUT) % 2, 2
    if u < U_DOWN:
        return G_MLP + (u - U_MLP) // 4, u % 4, 4
    return NG - 2 + (u - U_DOWN) // DOWN_SLABS, (u - U_DOWN) % DOWN_SLABS, DOWN_SLABS


STEP_COUNT = AH * CH + 2
AHEAD_OF_OUT = 9
FIRST_STEP_AT = 39
Z_PAIR = U_OUT - 2
BETWEEN = {17: [("dt", 0)]}
for c in range(CH):
    BETWEEN[2 * (26 + 3 * c) + 1] = [("first", c)]
    BETWEEN[2 * (28 + 3 * c) + 1] = [("second", c)]
for t in range(STEP_COUNT):
    at = FIRST_STEP_AT + t - (t > AHEAD_OF_OUT)
    if t != AHEAD_OF_OUT:
        BETWEEN.setdefault(2 * at + 1, []).append(("step_a", t))
        if t not in (AHEAD_OF_OUT - 1, STEP_COUNT - 1):
            BETWEEN.setdefault(2 * at + 2, []).append(("step_b", t))
for c in range(CH):
    BETWEEN[4 * Z_PAIR + 2 * c + 1].append(("z", c))
ROPE_AT = {13: [0, 1], 14: [2], 15: [3], 16: [4], 17: [5], 18: [6], 19: [7]}


def between(u):
    return [x for i in range(4) for x in BETWEEN.get(4 * u + i, [])]


def kernel_body(nc, xT, ccol, w_mod, w_in, w_out, w_gu, w_down, par, ssdw, lamqk, wdt, consts, rope, outT):
    ctx = ExitStack()
    with ctx:
        base = nc.sbuf_base
        base += -base % 32
        used = [0]

        def place(name, shape, dt, at=None):
            size = int(np.prod(shape[1:])) * (2 if dt == BF16 else 4)
            off = used[0] if at is None else at
            if at is None:
                used[0] += size + (-size) % 32
            return nc.alloc_sbuf_tensor_at(name, shape, dt, offset=base + off)

        KB = 1024
        xr = place("residual", [P, KD, SEQ], F32)
        h_hi = place("h_hi", [P, KD, SEQ], F32R)
        h_lo = place("h_lo", [P, KD, SEQ], F32R)
        F0 = used[0]
        used[0] += 88 * KB
        T0 = used[0]
        used[0] += 12 * KB
        f_hi = place("f_hi", [P, FT, SEQ], F32R, F0)
        f_lo = place("f_lo", [P, FT, SEQ], F32R, F0 + 44 * KB)
        conv_in = place("conv_in", [P, 8, SEQ + 3], F32, F0)
        q = place("q", [P, AH, SEQ], F32, F0)
        kpad = place("kpad", [P, 2, AH, SEQ], F32, F0 + 8 * KB)
        v = place("v", [P, CH, SEQ], F32, F0 + 24 * KB)
        xsF = place("xsF", [P, 4, SEQ], F32, F0 + 32 * KB)
        zs = place("zs", [P, CH, SEQ], F32, F0 + 32 * KB)
        yt = place("y_tok", [P, CH, SEQ], F32, F0 + 40 * KB)
        bcF = place("bcF", [P, 4, SEQ], F32, F0 + 48 * KB)
        xs_tok = place("xs_tok", [P, CH, SEQ], F32, F0 + 56 * KB)
        y_hi = place("y_hi", [P, KD, SEQ], F32R, F0 + 48 * KB)
        b_tok = place("b_tok", [P, CH, 256], F32, F0 + 64 * KB)
        xdt = place("xdt", [P, SEQ], F32, F0 + 68 * KB)
        xdec = place("xdec", [P, SEQ], F32, F0 + 70 * KB)
        lm = place("decay_l", [P, HEADS, P], F32, F0 + 72 * KB)
        mm = place("m_t", [P, HEADS, P], F32, F0 + 76 * KB)
        conv_th = place("conv_th", [P, 2, SEQ], F32, F0 + 76 * KB)
        y_lo = place("y_lo", [P, KD, SEQ], F32R, F0 + 64 * KB)
        o_tok = place("o_tok", [P, SEQ], F32, F0 + 80 * KB)
        junk = place("junk", [P, SEQ], F32, F0 + 82 * KB)
        cosT = place("cosT", [P, SEQ], F32, F0 + 84 * KB)
        sinT = place("sinT", [P, SEQ], F32, F0 + 86 * KB)
        ssdw_row = place("ssdw_row", [P, SEQ], F32, F0 + 84 * KB)
        s1 = place("s1", [P, SEQ], F32, T0)
        s2 = place("s2", [P, SEQ], F32, T0 + 2 * KB)
        sq = place("sq", [P, 2, SEQ], F32, T0 + 4 * KB)
        diag = place("diag", [P, 2, CH, P], F32, T0 + 4 * KB)
        h32 = place("h32", [P, 2, SEQ], F32, T0 + 8 * KB)
        dtF = place("dt_feature", [P, SEQ], F32, T0)
        rot = place("rot", [P, 2, SEQ], F32, F0 + 80 * KB)
        state = place("state", [P, SEQ], F32, T0 + 4 * KB)
        prob = place("prob", [P, 2, 2, SEQ], F32, T0)
        wT = place("wT", [P, 2, CH, P], F32, T0 + 8 * KB)
        lamt = place("lamt", [P, LAYERS, 4, 64], F32, T0)
        lamp = place("lamp", [P, LAYERS, 2, 64], F32, T0 + 2 * KB)
        raw = place("raw", [P, RING, 2, SEQ], F32)
        w_hi = place("w_hi", [P, RING, 2, SEQ], F32R)
        w_lo = place("w_lo", [P, RING, 2, SEQ], F32R)
        macc = place("mod_acc", [P, SEQ], F32)
        cst = place("consts", [P, 4 * P], F32)
        ident, tri, maskf, ones = (cst[:, i * P:(i + 1) * P] for i in range(4))
        maskb = place("mask_bf", [P, P], BF16)
        identb = place("ident_bf", [P, P], BF16)
        meancol = place("meancol", [P, 1], F32)
        prm = place("params", [P, LAYERS, NPAR], F32)
        modc = place("modc", [P, LAYERS, 48], F32)
        cond = place("cond", [P, 3, KD], F32)
        cvec = cond[:, 0, :]
        wdt_raw = place("wdt_raw", [P, KD, HEADS], F32)
        wdt_hi = place("wdt_hi", [P, KD, HEADS], F32R)
        wdt_lo = place("wdt_lo", [P, KD, HEADS], F32R)
        dts = place("dts", [P, 12, CH * HEADS], F32)
        (DU, DA, DE, DW, DN, DL, DT, DAA, DCS, DEA, DDEC, DTOT) = range(12)
        expa = place("expa", [P, LAYERS, HEADS], F32)
        lam = place("lam", [P, LAYERS, 4], F32)
        awc = place("attn_w", [P, LAYERS], F32)
        att = place("att_small", [P, 4, 2 * AH], F32)
        nrm = place("norm_small", [P, 6, 8], F32)
        ssq = place("ssq", [P, 8], F32)
        vecs = place("ln_vecs", [P, 6, KD], F32)
        (VGP, VS, VG, VB, VAG, VAB) = range(6)
        assert base + used[0] <= nc.sbuf_usable_end, (used[0], nc.sbuf_usable_end - base)

        ps = ctx.enter_context(nc.psum_tensor("ps", [P, 8, SEQ], F32))

        def sem(name):
            return ctx.enter_context(nc.semaphore(name))

        raw_loaded = [sem(f"raw_loaded{i}") for i in range(RING)]
        small_loaded = sem("small_loaded")
        c_loaded = sem("c_loaded")
        x_loaded = sem("x_loaded")
        wdt_loaded = sem("wdt_loaded")
        rope_loaded = sem("rope_loaded")
        ssdw_loaded = sem("ssdw_loaded")
        hi_ready = sem("hi_ready")
        slab_split = sem("slab_split")
        slab_used = sem("slab_used")
        bank_done = sem("bank_done")
        dve_chain = sem("dve_chain")
        act_chain = sem("act_chain")
        consts_ready = sem("consts_ready")
        cond_half = sem("cond_half")
        cond_tanh = sem("cond_tanh")
        lam_sums = sem("lam_sums")
        lam_exp = sem("lam_exp")
        mod_mm = sem("mod_mm")
        mod_col = sem("mod_col")
        vec_ready = sem("vec_ready")
        h_hi_ready = sem("h_hi_ready")
        h_ready = sem("h_ready")
        xa_ready = sem("xa_ready")
        wdt_hi_ready = sem("wdt_hi_ready")
        wdt_ready = sem("wdt_ready")
        conv_raw = sem("conv_raw")
        pads_ready = sem("pads_ready")
        conv_lin = sem("conv_lin")
        conv_tanh = sem("conv_tanh")
        conv_out = sem("conv_out")
        dt_mm = sem("dt_mm")
        dt_copied = sem("dt_copied")
        dt_turned = sem("dt_turned")
        dt_abs = sem("dt_abs")
        out_half = sem("out_half")
        dt_exp = sem("dt_exp")
        dt_w = sem("dt_w")
        dt_ln = sem("dt_ln")
        a_ready = sem("a_ready")
        cs_mm = sem("cs_mm")
        cs_ready = sem("cs_ready")
        cs_exp = sem("cs_exp")
        ssd_p1 = sem("ssd_p1")
        tok_copied = sem("tok_copied")
        l_ready = sem("l_ready")
        m_ready = sem("m_ready")
        xd_ready = sem("xd_ready")
        ssd_p2 = sem("ssd_p2")
        skip_ready = sem("skip_ready")
        ssd_d2 = sem("ssd_d2")
        qk_raw = sem("qk_raw")
        rot_dma = [sem(f"rot_dma{i}") for i in range(2)]
        rope_done = sem("rope_done")
        pad_half = sem("pad_half")
        kpad_ready = sem("kpad_ready")
        v_ready = sem("v_ready")
        z_tanh = sem("z_tanh")
        z_ready = sem("z_ready")
        gated = sem("gated")
        gate_sq = sem("gate_sq")
        ssd_v = sem("ssd_v")
        ssd_y0 = sem("ssd_y0")
        ys_scaled = sem("ys_scaled")
        trs_mm = sem("trs_mm")
        ys_hi = sem("ys_hi")
        ys_ready = sem("ys_ready")
        qk_done = sem("qk_done")
        nb_ready = sem("nb_ready")
        exp_done = sem("exp_done")
        w_ready = sem("w_ready")
        wt_mm = sem("wt_mm")
        wt_ready = sem("wt_ready")
        pv_done = sem("pv_done")
        o_copied = sem("o_copied")
        o_sq = sem("o_sq")
        att_v = sem("att_v")
        att_y0 = sem("att_y0")
        o_scaled = sem("o_scaled")
        tro_mm = sem("tro_mm")
        yo_hi = sem("yo_hi")
        yo_ready = sem("yo_ready")
        ln_r = sem("ln_r")
        ln_s1 = sem("ln_s1")
        ln_sq = sem("ln_sq")
        ln_s2 = sem("ln_s2")
        ln_stats = sem("ln_stats")
        ln_v = sem("ln_v")
        ln_y0 = sem("ln_y0")
        ln_diag = sem("ln_diag")
        ln_rows = sem("ln_rows")
        ln_t = sem("ln_t")
        h32_ready = sem("h32_ready")
        mlp_th = sem("mlp_th")
        mlp_a = sem("mlp_a")
        mlp_f = sem("mlp_f")
        f_hi_ready = sem("f_hi_ready")
        f_ready = sem("f_ready")
        out_tile = sem("out_tile")
        out_stored = sem("out_stored")

        def wait_loaded(eng, r, it=0, step=0):
            eng.wait_ge(raw_loaded[r % RING], 16 * (r // RING + 1) + (16 * step // RING) * it)

        def wait_used(eng, s, it=0):
            if s < 0:
                return
            l, u = divmod(s, UNITS)
            g, j, n = group_of(u)
            if j == n - 1:
                eng.wait_ge(bank_done, 4 * (NG * l + g + 1) + 4 * it)
            else:
                before = (UNITS - NG) * l + u - j - g
                eng.wait_ge(slab_used, before + j + 1 + 3 * it)

        def raw_step(l):
            return 8 if l == 0 else 4

        block = ctx.enter_context(nc.Block())

        @block.sync
        def _(sp):
            def w_src(l, u, it=0):
                g, j, _ = group_of(u)
                if g in (G_OUT + 2, G_OUT + 3):
                    j += 2
                rows = slice(2 * j * P, 2 * (j + 1) * P)
                if u < U_OUT:
                    return w_in[l, rows, g * SEQ:(g + 1) * SEQ].rearrange("(k p) n -> p k n", p=P)
                if u < U_MLP:
                    half = (g - G_OUT) % 2
                    return w_out[l, rows, half * SEQ:(half + 1) * SEQ].rearrange("(k p) n -> p k n", p=P)
                return w_down[l, rows, (g - NG + 2) * SEQ:(g - NG + 3) * SEQ].rearrange("(k p) n -> p k n", p=P)

            def room(r, it=0, step=0):
                if r >= RING:
                    sp.wait_ge(slab_split, r - RING + 1 + step * it)

            def load_w(l, u):
                r = raw_of(l, u)
                room(r)
                sp.dma_start(raw[:, r % RING, :, :], w_src(l, u)).then_inc(raw_loaded[r % RING], 16)

            def load_gu(l, j, it):
                r = raw_of(l, U_MLP + j)
                room(r, it, raw_step(l))
                src = w_gu[l, 2 * j * P:2 * (j + 1) * P, :].rearrange("(k p) n -> p k n", p=P)
                sp.dma_start(raw[:, r % RING, :, :], src[:, :, bass.ds(it * SEQ, SEQ)])\
                  .then_inc(raw_loaded[r % RING], 16)

            def load_mod(r, lb, j, it=0, step=0, blk=0):
                room(r, it, step)
                src = w_mod[lb, 2 * j * P:2 * (j + 1) * P, :].rearrange("(k p) n -> p k n", p=P)
                sp.dma_start(raw[:, r % RING, :, :], src[:, :, bass.ds(blk * SEQ, SEQ)])\
                  .then_inc(raw_loaded[r % RING], 16)

            for r in range(4 * MOD_FRONT):
                load_mod(r, 0, r % 4, blk=r // 4)
            for l in range(LAYERS):
                if l:
                    sp.wait_ge(bank_done, 4 * NG * l)
                sp.dma_start(cosT[:, :], rope[0]).then_inc(rope_loaded, 16)
                sp.dma_start(sinT[:, :], rope[1]).then_inc(rope_loaded, 16)
                sp.dma_start(wdt_raw[:, :, :], wdt[l]).then_inc(wdt_loaded, 16)
                for u in range(U_MLP):
                    load_w(l, u)
                    if l == 0:
                        for i, j, r in mod_behind(u):
                            load_mod(r, 0, j, blk=i)
                    if u == 24:
                        sp.wait_ge(rope_done, 8 * (l + 1))
                        sp.dma_start(ssdw_row[:, :], ssdw[l]).then_inc(ssdw_loaded, 16)
                with sp.Fori(0, MLP_G) as g:
                    for j in range(4):
                        load_gu(l, j, g)
                        if l == 0:
                            load_mod(raw_of(0, U_MLP + j) + 1, 1, j, it=g, step=8, blk=g)
                for u in range(U_DOWN, UNITS):
                    load_w(l, u)
                    i = u - U_DOWN
                    if l == 0 and i < MOD_DOWN:
                        lb, blk = mod_block(21 + i // 4)
                        load_mod(raw_of(0, u) + 1, lb, i % 4, blk=blk)
            for k in range(KD):
                sp.wait_ge(out_tile, k + 1)
                sp.dma_start(outT[k * P:(k + 1) * P, :], xr[:, k, :]).then_inc(out_stored, 16)
            sp.wait_ge(out_stored, 16 * KD)

        @block.tensor
        def _(pe):
            def slab(l, u, act_hi, act_lo, ready, weights_move=False, bank_free=None, it=0, slabs=1):
                g, j, n = group_of(u)
                step = raw_step(l)
                k0 = 4 if g in (G_OUT + 2, G_OUT + 3) else 0
                pe.wait_ge(slab_split, raw_of(l, u + slabs - 1) + 1 + step * it)

                def trio(kg, m, first):
                    k, kk, c = kg + k0, kg % 2, (UNITS * l + u + kg // 2 - j) % RING
                    if first:
                        ready(k)
                    if kg == 0 and bank_free:
                        bank_free(m)
                    cols = slice(m * P, (m + 1) * P)
                    if weights_move:
                        pairs = [(act_hi[:, k, cols], w_hi[:, c, kk, :]), (act_hi[:, k, cols], w_lo[:, c, kk, :]),
                                 (act_lo[:, k, cols], w_hi[:, c, kk, :])]
                    else:
                        pairs = [(w_hi[:, c, kk, cols], act_hi[:, k, :]), (w_hi[:, c, kk, cols], act_lo[:, k, :]),
                                 (w_lo[:, c, kk, cols], act_hi[:, k, :])]
                    for i, (stat, mov) in enumerate(pairs):
                        mmi = pe.matmul(ps[:, m, :], stat, mov, start=(kg == 0 and i == 0),
                                        stop=(kg == 2 * n - 1 and i == 2))
                    if kg == 2 * n - 1:
                        mmi.then_inc(bank_done, 1)
                    elif kg % 2 and m == 3:
                        mmi.then_inc(slab_used, 1)

                if slabs == 1:
                    for kk in range(2):
                        for m in range(4):
                            trio(2 * j + kk, m, m == 0)
                            if m % 2:
                                between_matmuls(l, u, 2 * kk + m // 2)
                else:
                    for m in range(4):
                        for kg in range(2 * j, 2 * (j + slabs)):
                            trio(kg, m, m == 0)
                            if kg % 2:
                                between_matmuls(l, u, 2 * m + (kg // 2) % 2)

            def mod_reduce(i, it=0):
                if i < MOD_FRONT:
                    r = 4 * i + 3
                elif i < 10:
                    r = MOD_LAST[i][1]
                else:
                    r = raw_of(0, U_MLP + 4 * (i - 10) + 3) + 1
                pe.wait_ge(slab_split, r + 1 + 8 * it)
                for j in range(4):
                    last = pe.matmul(ps[:, mod_bank(i), j:j + 1], macc[:, j * P:(j + 1) * P], ones[:, 0:1],
                                     start=True, stop=True)
                last.then_inc(mod_mm, 1)

            def dt_project(l):
                pe.wait_ge(wdt_ready, l + 1)
                for k in range(KD):
                    for i, (w, a) in enumerate([(wdt_hi, h_hi), (wdt_lo, h_hi), (wdt_hi, h_lo)]):
                        last = pe.matmul(ps[0:HEADS, 7, :], w[:, k, :], a[:, k, :], start=(k == 0 and i == 0),
                                         stop=(k == KD - 1 and i == 2))
                last.then_inc(dt_mm, 1)

            def dt_turn(l, _):
                pe.wait_ge(dt_copied, l + 1)
                for c in range(CH):
                    last = pe.transpose(ps[:, 7, c * HEADS:(c + 1) * HEADS], dtF[0:HEADS, c * P:(c + 1) * P],
                                        ident[0:HEADS, 0:HEADS])
                last.then_inc(dt_turned, 1)

            def cumsum(l):
                pe.wait_ge(a_ready, l + 1)
                pe.matmul(ps[:, 7, 32:64], tri, dts[:, DAA, :], start=True, stop=True)
                pe.matmul(ps[:, 7, 64:96], ones, dts[:, DAA, :], start=True, stop=True).then_inc(cs_mm, 1)

            def ssd_first(l, c):
                if c == 0:
                    pe.wait_ge(conv_out, 8 * (l + 1))
                    pe.wait_ge(cs_ready, l + 1)
                    pe.wait_ge(cs_exp, l + 1)
                else:
                    pe.wait_ge(ssd_d2, CH * l + c)
                tok = slice(c * P, (c + 1) * P)
                for j in range(4):
                    pe.transpose(ps[:, 6, j * P:(j + 1) * P], xsF[:, j, tok], ident)
                for g in range(2):
                    pe.transpose(ps[:, 7, 256 + g * P:256 + (g + 1) * P], bcF[:, g, tok], ident)
                for g in range(2):
                    pe.matmul(ps[:, 7, g * P:(g + 1) * P], bcF[:, g, tok], bcF[:, 2 + g, tok], start=True, stop=True)
                for b in range(2):
                    bank = ps[:, 4 + b, :].rearrange("p (e t) -> p e t", e=4)
                    pe.matmul(bank, identb[:, :], maskb[:, :].unsqueeze(1).to_broadcast([P, 4, P]), start=True, stop=False,
                              skip_group_check=True)
                    for e in range(4):
                        col = c * HEADS + 4 * b + e
                        last = pe.matmul(bank[:, e, :], dts[:, DAA, col:col + 1].to_broadcast([P, P]), tri,
                                         start=False, stop=(e == 3), skip_group_check=True)
                last.then_inc(ssd_p1, 1)

            def ssd_second(l, c):
                pe.wait_ge(m_ready, CH * l + c + 1)
                pe.wait_ge(xd_ready, CH * l + c + 1)
                tok = slice(c * P, (c + 1) * P)
                for hh in range(HEADS):
                    pd = slice(hh * HDIM, (hh + 1) * HDIM)
                    pe.matmul(ps[:, 4, pd], mm[:, hh, :], xdt[:, pd], start=True, stop=True)
                if c > 0:
                    for g in range(2):
                        gd = slice(g * 256, (g + 1) * 256)
                        pe.matmul(ps[:, 5, gd], bcF[:, 2 + g, tok], state[:, gd], start=True, stop=True)
                pe.wait_ge(tok_copied, CH * l + c + 1)
                for g in range(2):
                    gd = slice(g * 256, (g + 1) * 256)
                    last = pe.matmul(ps[:, 6, gd], b_tok[:, c, g * P:(g + 1) * P], xdec[:, gd], start=True, stop=True)
                last.then_inc(ssd_p2, 1)

            def qk(l, t):
                i, h = divmod(t, AH)
                if t < AH:
                    pe.wait_ge(rope_done, 8 * l + AH + h + 1)
                    pe.wait_ge(kpad_ready, AH * l + h + 1)
                if t == 0:
                    pe.wait_ge(ssd_d2, CH * (l + 1))
                else:
                    pe.wait_ge(exp_done, 16 * l + t)
                n = (i + 1) * P
                for m in range(2):
                    pe.matmul(ps[:, 4 + m, 0:n], q[:, h, i * P:(i + 1) * P], kpad[:, m, h, 0:n], start=True, stop=False,
                              skip_group_check=True)
                    last = pe.matmul(ps[:, 4 + m, i * P:n], maskb[:, :], identb[:, :], start=False, stop=True,
                                     skip_group_check=True)
                last.then_inc(qk_done, 1)

            def turn_w(l, t):
                pe.wait_ge(w_ready, 16 * l + t + 1)
                if t:
                    pe.wait_ge(wt_ready, 16 * l + t)
                if t >= 5 and t % 4 == 1:
                    pe.wait_ge(yo_hi, CH * l + (t - 1) // 4)
                    pe.wait_ge(yo_ready, CH * l + (t - 1) // 4)
                for j in range(t // AH + 1):
                    last = pe.transpose(ps[:, 6, j * P:(j + 1) * P], prob[:, t % 2, 0, j * P:(j + 1) * P], ident)
                last.then_inc(wt_mm, 1)

            def pv(l, t):
                i, h = divmod(t, AH)
                pe.wait_ge(wt_ready, 16 * l + t + 1)
                if t == 0:
                    pe.wait_ge(v_ready, CH * (l + 1))
                if h == 0 and i:
                    pe.wait_ge(o_copied, CH * l + i)
                    pe.wait_ge(o_sq, CH * l + i)
                for j in range(i + 1):
                    last = pe.matmul(ps[:, 7, h * P:(h + 1) * P], wT[:, t % 2, j, :], v[:, j, h * P:(h + 1) * P],
                                     start=(j == 0), stop=(j == i))
                last.then_inc(pv_done, 1)

            def turn_o(l, i):
                pe.wait_ge(o_scaled, CH * l + i + 1)
                pe.wait_ge(wt_ready, 16 * l + min(4 * i + 5, 16))
                for h in range(AH):
                    last = pe.transpose(ps[:, 6, h * P:(h + 1) * P], o_tok[:, h * P:(h + 1) * P], ident)
                last.then_inc(tro_mm, 1)

            def step_a(l, t):
                if t < 16:
                    qk(l, t)
                if 1 <= t <= 16:
                    turn_w(l, t - 1)

            def step_b(l, t):
                if t >= 5 and t % 4 == 1:
                    turn_o(l, (t - 5) // 4)
                if 1 <= t <= 16:
                    pv(l, t - 1)

            def turn_ys(l):
                for c in range(CH):
                    pe.wait_ge(ys_scaled, CH * l + c + 1)
                    for j in range(4):
                        last = pe.transpose(ps[:, c, j * P:(j + 1) * P], yt[:, c, j * P:(j + 1) * P], ident)
                    last.then_inc(trs_mm, 1)

            def ln_sums(n):
                for i, (src, done) in enumerate(((s1, ln_s1), (s2, ln_s2))):
                    pe.wait_ge(done, (KD - 1) * (n + 1))
                    for c in range(CH):
                        last = pe.matmul(ps[:, 4, 4 * i + c:4 * i + c + 1], src[:, c * P:(c + 1) * P], meancol[:, :],
                                         start=True, stop=True)
                last.then_inc(ln_stats, 1)

            def ln_spread(n):
                for i in range(2):
                    pe.wait_ge(ln_diag, 2 * n + i + 1)
                    pe.matmul(ps[:, 5 + i, :], ones, diag[:, i, :, :], start=True, stop=True).then_inc(ln_rows, 1)

            def between_matmuls(l, u, quarter):
                for what, t in BETWEEN.get(4 * u + quarter, []) if u < U_MLP else []:
                    {"dt": dt_turn, "first": ssd_first, "second": ssd_second, "step_a": step_a, "step_b": step_b,
                     "z": lambda l, c: None}[what](l, t)

            pe.wait_ge(consts_ready, 1)
            for i in range(MOD_FRONT):
                mod_reduce(i)
            for l in range(LAYERS):
                def h_tile(k, e=2 * l):
                    pe.wait_ge(h_ready, 8 * e + k + 1)

                def none(k):
                    pass

                def y_tile(k):
                    if k == 0:
                        pe.wait_ge(ys_ready, CH * (l + 1))
                    if k == 4:
                        pe.wait_ge(yo_ready, CH * (l + 1))

                frees = {
                    1: lambda m: pe.wait_ge(conv_raw, 8 * l + m + 1),
                    2: lambda m: pe.wait_ge(conv_raw, 8 * l + 4 + m + 1),
                    3: lambda m: pe.wait_ge(qk_raw, 8 * l + m + 1),
                    4: lambda m: pe.wait_ge(qk_raw, 8 * l + 4 + m + 1),
                    5: lambda m: pe.wait_ge(v_ready, CH * l + m + 1),
                    7: lambda m: pe.wait_ge(out_half, 8 * l + m + 1),
                    8: lambda m: pe.wait_ge(out_half, 8 * l + 4 + m + 1),
                    9: lambda m: pe.wait_ge(ln_r, 16 * l + m + 1),
                }
                for u in range(U_MLP):
                    g = group_of(u)[0]
                    if u == U_OUT:
                        step_b(l, AHEAD_OF_OUT - 1)
                        step_a(l, AHEAD_OF_OUT)
                        step_b(l, AHEAD_OF_OUT)
                        turn_ys(l)
                    pair = u in (Z_PAIR, U_OUT + 4, U_OUT + 6)
                    if u == U_OUT + 4:
                        step_b(l, STEP_COUNT - 1)
                    if l == 0:
                        for i in MOD_LAST:
                            if max(MOD_LAST[i][0] - 2, 0) == u:
                                mod_reduce(i)
                    if u - 1 in (Z_PAIR, U_OUT + 4, U_OUT + 6):
                        continue
                    if u < U_OUT:
                        slab(l, u, h_hi, h_lo, h_tile if g == 0 else none, weights_move=GROUPS[g] in "vz",
                             bank_free=frees.get(g), slabs=2 if pair else 1)
                    else:
                        slab(l, u, y_hi, y_lo, y_tile, bank_free=frees.get(g), slabs=2 if pair else 1)
                    if u == 3:
                        dt_project(l)
                    if u == 6:
                        cumsum(l)
                ln_sums(2 * l)
                ln_spread(2 * l)

                def h2_tile(k, e=2 * l + 1):
                    pe.wait_ge(h_ready, 8 * e + k + 1)

                def mlp_group(g, first):
                    def free(m):
                        sm = mlp_a if m < 2 else mlp_f
                        pe.wait_ge(sm, FT * l + m % 2 + 1 + 2 * (g - 1))

                    for j in range(4):
                        if l == 0 and j == 1:
                            mod_reduce(10, it=g)
                        slab(l, U_MLP + j, h_hi, h_lo, h2_tile if first else none, bank_free=None if first else free, it=g)

                mlp_group(0, True)
                with pe.Fori(1, MLP_G) as g:
                    mlp_group(g, False)

                def f_tile(k):
                    pe.wait_ge(f_ready, FT * l + k + 1)

                for u in range(U_DOWN, UNITS):
                    i = u - U_DOWN
                    if l == 0 and i < MOD_DOWN and i % 4 == 1:
                        mod_reduce(21 + i // 4)
                    if i < DOWN_SLABS:
                        free = lambda m: pe.wait_ge(mlp_a if m < 2 else mlp_f, FT * (l + 1) - 1 + m % 2)
                    else:
                        free = lambda m: pe.wait_ge(ln_r, 16 * l + 8 + m + 1)
                    if i % DOWN_SLABS != DOWN_SLABS - 1:
                        slab(l, u, f_hi, f_lo, f_tile, bank_free=free, slabs=2 if i % DOWN_SLABS == DOWN_SLABS - 2 else 1)
                ln_sums(2 * l + 1)
                ln_spread(2 * l + 1)

        @block.scalar
        def _(act):
            chained = [0]

            def chain(ins):
                chained[0] += 1
                ins.then_inc(act_chain, 1)
                act.wait_ge(act_chain, chained[0])

            def hi(l, u, it=0):
                if UNITS * l + u >= LAYERS * UNITS:
                    return
                s = UNITS * l + u
                r = raw_of(l, u)
                wait_loaded(act, r, it, raw_step(l))
                wait_used(act, s - RING, it)
                act.activation(w_hi[:, s % RING, :, :], raw[:, r % RING, :, :], ACT.Copy).then_inc(hi_ready, 1)

            def affine(e, k):
                n = e - 1
                if n < 0:
                    if k == 0:
                        act.wait_ge(x_loaded, 16)
                else:
                    act.wait_ge(ln_t, 8 * n + k + 1)
                if k == 0:
                    act.wait_ge(vec_ready, e + 1)
                if k >= 2:
                    act.wait_ge(h_ready, 8 * e + k - 1)
                act.activation(h32[:, k % 2, :], xr[:, k, :], ACT.Identity, bias=vecs[:, VB, k:k + 1],
                               scale=vecs[:, VG, k:k + 1]).then_inc(h32_ready, 1)
                act.wait_ge(h32_ready, 8 * e + k + 1)
                act.activation(h_hi[:, k, :], h32[:, k % 2, :], ACT.Copy).then_inc(h_hi_ready, 1)

            def conv_evac(l, t):
                act.wait_ge(bank_done, 4 * (NG * l + t // 4) + t % 4 + 1)
                act.activation(conv_in[:, t, 3:SEQ + 3], ps[:, t % 4, :], ACT.Copy)
                if t == 0:
                    act.wait_ge(vec_ready, 1)
                dst = xsF[:, t, :] if t < 4 else bcF[:, t - 4, :]
                act.activation(dst, ps[:, t % 4, :], ACT.Identity, bias=prm[:, l, C_CONVB + t:C_CONVB + t + 1],
                               scale=prm[:, l, C_CONVW + 4 * t + 3:C_CONVW + 4 * t + 4]).then_inc(conv_raw, 1)

            def conv_tanhs(l, t):
                act.wait_ge(conv_lin, 8 * l + t + 1)
                if t >= 2:
                    act.wait_ge(conv_out, 8 * l + t - 1)
                src = xsF[:, t, :] if t < 4 else bcF[:, t - 4, :]
                act.activation(conv_th[:, t % 2, :], src, ACT.Tanh).then_inc(conv_tanh, 1)

            def qk_evac(l, t):
                act.wait_ge(bank_done, 4 * (NG * l + 2 + t // 4) + t % 4 + 1)
                dst = q[:, t, :] if t < 4 else kpad[:, 0, t - 4, :]
                act.activation(dst, ps[:, t % 4, :], ACT.Copy).then_inc(qk_raw, 1)

            def z_tanhs(l, c):
                act.wait_ge(bank_done, 4 * (NG * l + 5) + c + 1)
                act.activation(zs[:, c, :], ps[:, c, :], ACT.Tanh, scale=0.5).then_inc(z_tanh, 1)

            def gate_squares(l, c):
                act.wait_ge(gated, CH * l + c + 1)
                for g in range(2):
                    last = act.activation(zs[:, c, g * 256:(g + 1) * 256], yt[:, c, g * 256:(g + 1) * 256], ACT.Square,
                                          accum_out=nrm[:, 5, 2 * c + g:2 * c + g + 1])
                last.then_inc(gate_sq, 1)

            def ssd_act(l, c):
                act.wait_ge(ssd_p1, CH * l + c + 1)
                act.activation(xs_tok[:, c, :], ps[:, 6, :], ACT.Copy)
                act.activation(b_tok[:, c, :], ps[:, 7, 256:512], ACT.Copy).then_inc(tok_copied, 1)
                if c:
                    act.wait_ge(m_ready, CH * l + c)
                for hh in range(HEADS):
                    col = c * HEADS + hh
                    last = act.activation(lm[:, hh, :], ps[:, 4 + hh // 4, (hh % 4) * P:(hh % 4 + 1) * P], ACT.Exp,
                                          bias=dts[:, DN, col:col + 1])
                last.then_inc(l_ready, 1)

            def exps(l, t):
                i, h = divmod(t, AH)
                act.wait_ge(nb_ready, 16 * l + t + 1)
                if t >= 2:
                    act.wait_ge(wt_mm, 16 * l + t - 1)
                n = (i + 1) * P
                for m in range(2):
                    last = act.activation(prob[:, t % 2, m, 0:n], ps[:, 4 + m, 0:n], ACT.Exp,
                                          bias=att[:, 0, 2 * h + m:2 * h + m + 1], scale=0.125,
                                          accum_out=att[:, 1, 2 * h + m:2 * h + m + 1])
                last.then_inc(exp_done, 1)

            def wt_copy(l, t):
                act.wait_ge(wt_mm, 16 * l + t + 1)
                if t >= 2:
                    act.wait_ge(pv_done, 16 * l + t - 1)
                n = t // AH + 1
                act.activation(wT[:, t % 2, 0:n, :], ps[:, 6, 0:n * P].rearrange("p (j t) -> p j t", j=n), ACT.Copy)\
                   .then_inc(wt_ready, 1)

            def o_squares(l, i):
                act.wait_ge(pv_done, 16 * l + 4 * i + 4)
                for h in range(AH):
                    last = act.activation(junk[:, h * P:(h + 1) * P], ps[:, 7, h * P:(h + 1) * P], ACT.Square,
                                          accum_out=ssq[:, h:h + 1])
                last.then_inc(o_sq, 1)

            def root(v_sem, value, y_sem, n):
                act.wait_ge(v_sem, value)
                chain(act.activation(nrm[:, 1, 0:n], nrm[:, 0, 0:n], ACT.Ln))
                act.activation(nrm[:, 2, 0:n], nrm[:, 1, 0:n], ACT.Exp, scale=-0.5).then_inc(y_sem, 1)

            def yo_high(l, i):
                act.wait_ge(tro_mm, CH * l + i + 1)
                act.activation(y_hi[:, 4:8, i * P:(i + 1) * P], ps[:, 6, :].rearrange("p (h t) -> p h t", h=4),
                               ACT.Copy, scale=awc[:, l:l + 1]).then_inc(yo_hi, 1)

            def o_root(l, t):
                root(att_v, CH * l + (t - 4) // 4 + 1, att_y0, 4)

            def step(l, t):
                if 1 <= t <= 16:
                    wt_copy(l, t - 1)
                if t < 16:
                    exps(l, t)
                if t >= 4 and t % 4 == 0:
                    o_squares(l, (t - 4) // 4)
                    if t != AHEAD_OF_OUT - 1:
                        o_root(l, t)
                if t >= 5 and t % 4 == 1:
                    yo_high(l, (t - 5) // 4)

            def squares(n, m):
                act.wait_ge(ln_r, 8 * n + m + 1)
                if m >= 2:
                    act.wait_ge(ln_s2, 7 * n + max(m - 2, 1))
                act.activation(sq[:, m % 2, :], xr[:, m, :], ACT.Square).then_inc(ln_sq, 1)

            def ln_head(n):
                root(ln_v, n + 1, ln_y0, 4)

            def mlp_evac(l, it, last=False):
                for j in range(2):
                    act.wait_ge(bank_done, 4 * (NG * l + G_MLP) + j + 1 + 4 * it)
                    act.activation(sq[:, j, :], ps[:, j, :], ACT.Tanh, scale=0.5).then_inc(mlp_th, 1)
                for j in range(2):
                    act.wait_ge(mlp_f, FT * l + j + 1 + 2 * it)
                    act.activation(f_hi[:, bass.ds(2 * it + j, 1), :], h32[:, j:j + 1, :], ACT.Copy).then_inc(f_hi_ready, 1)

            act.dma_start(cvec, ccol).then_inc(c_loaded, 16)
            act.dma_start(cst[:, :], consts).then_inc(small_loaded, 16)
            act.dma_start(prm[:, :, :], par).then_inc(small_loaded, 16)
            act.dma_start(lamt[:, :, :, :], lamqk).then_inc(small_loaded, 16)
            act.dma_start(xr[:, :, :], xT.rearrange("(k p) t -> p k t", p=P)).then_inc(x_loaded, 16)
            act.preload_act_table_set("exp_and_others")
            act.wait_ge(cond_half, 1)
            act.activation(cond[:, 2, :], cond[:, 1, :], ACT.Tanh).then_inc(cond_tanh, 1)
            act.wait_ge(small_loaded, 48)
            for l in range(LAYERS):
                last = act.activation(expa[:, l, :], prm[:, l, C_ALOG:C_ALOG + HEADS], ACT.Exp)
            act.wait_ge(lam_sums, 1)
            act.activation(lam[:, :, 2:4], lam[:, :, 0:2], ACT.Exp).then_inc(lam_exp, 1)
            hi(0, 0)
            hi(0, 1)
            hi(0, 2)
            affine(0, 0)
            affine(0, 1)
            for l in range(LAYERS):
                for u in range(U_MLP):
                    if u in (4, 8):
                        for t in range(4):
                            conv_evac(l, u - 4 + t)
                    if u in (12, 16):
                        for t in range(4):
                            qk_evac(l, u - 12 + t)
                    if u == 20:
                        for c in range(CH):
                            act.wait_ge(bank_done, 4 * (NG * l + 4) + c + 1)
                            act.activation(v[:, c, :], ps[:, c, :], ACT.Copy).then_inc(v_ready, 1)
                    if u == 19:
                        act.preload_act_table_set("natural_log_exp_and_others")
                    if u not in (U_OUT - 1, U_MLP - 1):
                        hi(l, u + 3)
                    if u < 3:
                        affine(2 * l, 2 * u + 2)
                        affine(2 * l, 2 * u + 3)
                    if u == 0:
                        act.wait_ge(wdt_loaded, 16 * (l + 1))
                        act.activation(wdt_hi[:, :, :], wdt_raw[:, :, :], ACT.Copy).then_inc(wdt_hi_ready, 1)
                    if u == 4:
                        act.wait_ge(dt_mm, l + 1)
                        act.activation(dtF[0:HEADS, :], ps[0:HEADS, 7, :], ACT.Copy).then_inc(dt_copied, 1)
                        act.preload_act_table_set("natural_log_exp_and_others")
                        act.wait_ge(dt_abs, l + 1)
                        act.activation(dts[:, DE, :], dts[:, DA, :], ACT.Exp, scale=-1.0).then_inc(dt_exp, 1)
                        act.wait_ge(dt_w, l + 1)
                        act.activation(dts[:, DL, :], dts[:, DW, :], ACT.Ln).then_inc(dt_ln, 1)
                        act.preload_act_table_set("exp_and_others")
                    if 5 <= u <= 12:
                        conv_tanhs(l, u - 5)
                    if u == 7:
                        act.wait_ge(cs_ready, l + 1)
                        act.activation(dts[:, DEA, :], dts[:, DCS, :], ACT.Exp)
                        act.activation(dts[:, DDEC, :], dts[:, DDEC, :], ACT.Exp)
                        act.activation(dts[:, DTOT, :], ps[:, 7, 64:96], ACT.Exp).then_inc(cs_exp, 1)
                    if u == U_OUT:
                        act.preload_act_table_set("natural_log_exp_and_others")
                        o_root(l, AHEAD_OF_OUT - 1)
                        step(l, AHEAD_OF_OUT)
                        root(ssd_v, l + 1, ssd_y0, 8)
                        for c in range(CH):
                            act.wait_ge(trs_mm, CH * l + c + 1)
                            act.activation(y_hi[:, 0:4, c * P:(c + 1) * P], ps[:, c, :].rearrange("p (h t) -> p h t", h=4),
                                           ACT.Copy).then_inc(ys_hi, 1)
                    for what, t in between(u):
                        if what == "first":
                            ssd_act(l, t)
                        elif what == "step_a":
                            step(l, t)
                        elif what == "z":
                            z_tanhs(l, t)
                            if t:
                                gate_squares(l, t - 1)
                            if t == CH - 1:
                                gate_squares(l, t)
                    if u == U_OUT - 1:
                        hi(l, u + 3)
                    if u == Z_PAIR - 1:
                        act.preload_act_table_set("exp_and_others")
                    if u == 30:
                        for m in range(4):
                            squares(2 * l, m)
                for m in range(4, 8):
                    squares(2 * l, m)
                hi(l, U_MLP + 2)
                ln_head(2 * l)
                act.preload_act_table_set("exp_and_others")
                affine(2 * l + 1, 0)
                affine(2 * l + 1, 1)
                for j in range(4):
                    hi(l, U_MLP + j + 3)
                    if j < 3:
                        affine(2 * l + 1, 2 * j + 2)
                        affine(2 * l + 1, 2 * j + 3)
                with act.Fori(1, MLP_G) as g:
                    mlp_evac(l, g - 1)
                    for j in range(4):
                        hi(l, U_MLP + j + 3, it=g)
                for u in range(U_DOWN, UNITS):
                    if u == U_DOWN:
                        mlp_evac(l, MLP_G - 1)
                        act.preload_act_table_set("natural_log_exp_and_others")
                    if u < UNITS - 1:
                        hi(l, u + 3)
                    if u == U_DOWN + DOWN_SLABS:
                        for m in range(4):
                            squares(2 * l + 1, m)
                for m in range(4, 8):
                    squares(2 * l + 1, m)
                hi(l, UNITS - 1 + 3)
                ln_head(2 * l + 1)
                if l + 1 < LAYERS:
                    act.preload_act_table_set("exp_and_others")
                    affine(2 * l + 2, 0)
                    affine(2 * l + 2, 1)

        @block.gpsimd
        def _(pool):
            def rotate(l, t):
                src = q[:, t, :] if t < 4 else kpad[:, 0, t - 4, :]
                pool.wait_ge(qk_raw, 8 * l + t + 1)
                if t >= 2:
                    pool.wait_ge(rope_done, 8 * l + t - 1)
                for b in range(4):
                    o = b ^ 1
                    pool.dma_start(rot[32 * b:32 * b + 32, t % 2, :], src[32 * o:32 * o + 32, :])\
                        .then_inc(rot_dma[t % 2], 16)

            def pad(l, h):
                pool.wait_ge(rope_done, 8 * l + 4 + h + 1)
                pool.memset(kpad[64:128, 0, h, :], 0.0).then_inc(pad_half, 1)
                pool.wait_ge(pad_half, AH * l + h + 1)
                pool.memset(kpad[0:64, 1, h, :], 0.0).then_inc(kpad_ready, 1)
                pool.wait_ge(kpad_ready, AH * l + h + 1)

            def skip_term(l, c):
                pool.wait_ge(tok_copied, CH * l + c + 1)
                d = prm[:, l, C_DSKIP:C_DSKIP + HEADS].unsqueeze(2).to_broadcast([P, HEADS, HDIM])
                pool.tensor_tensor(yt[:, c, :].rearrange("p (h d) -> p h d", h=HEADS),
                                   xs_tok[:, c, :].rearrange("p (h d) -> p h d", h=HEADS), d, ALU.mult)\
                    .then_inc(skip_ready, 1)
                pool.wait_ge(skip_ready, CH * l + c + 1)

            def sum_squares(n, m):
                pool.wait_ge(ln_sq, 8 * n + m + 1)
                if m == 1:
                    pool.tensor_tensor(s2[:, :], sq[:, 0, :], sq[:, 1, :], ALU.add).then_inc(ln_s2, 1)
                elif m > 1:
                    pool.wait_ge(ln_s2, 7 * n + m - 1)
                    pool.tensor_tensor(s2[:, :], s2[:, :], sq[:, m % 2, :], ALU.add).then_inc(ln_s2, 1)

            def next_residual(e, k):
                pool.wait_ge(h_hi_ready, 8 * e + k + 1)
                if e == 0:
                    pool.tensor_scalar(xr[:, k, :], xr[:, k, :], ALPHA, 0.0, ALU.mult, ALU.add).then_inc(xa_ready, 1)
                else:
                    pool.tensor_scalar(xr[:, k, :], xr[:, k, :], vecs[:, VAG, k:k + 1], vecs[:, VAB, k:k + 1],
                                       ALU.mult, ALU.add).then_inc(xa_ready, 1)

            for k in range(KD):
                next_residual(0, k)
            for l in range(LAYERS):
                pool.wait_ge(h_ready, 8 * (2 * l + 1))
                pool.memset(conv_in[:, :, 0:3], 0.0).then_inc(pads_ready, 1)
                for t in range(3):
                    rotate(l, t)
                skip_term(l, 0)
                rotate(l, 3)
                skip_term(l, 1)
                rotate(l, 4)
                rotate(l, 5)
                skip_term(l, 2)
                rotate(l, 6)
                pad(l, 0)
                skip_term(l, 3)
                rotate(l, 7)
                for h in range(1, AH):
                    pad(l, h)
                for m in range(KD - 1):
                    sum_squares(2 * l, m)
                for k in range(KD):
                    next_residual(2 * l + 1, k)
                for m in range(KD - 1):
                    sum_squares(2 * l + 1, m)
                if l + 1 < LAYERS:
                    for k in range(KD):
                        next_residual(2 * l + 2, k)

        @block.vector
        def _(dve):
            chained = [0]

            def chain(ins, loop=0):
                chained[0] += 1
                ins.then_inc(dve_chain, 1)
                dve.wait_ge(dve_chain, chained[0] + loop)

            def split(l, u, it=0):
                if UNITS * l + u >= LAYERS * UNITS:
                    return
                s = UNITS * l + u
                r = raw_of(l, u)
                dve.wait_ge(hi_ready, s + 1 + 4 * it)
                dve.tensor_tensor(w_lo[:, s % RING, :, :], raw[:, r % RING, :, :], w_hi[:, s % RING, :, :].bitcast(F32),
                                  ALU.subtract).then_inc(slab_split, 1)

            def fold_mod(i, j, it=0, loop=0, at=0):
                if i < MOD_FRONT:
                    r = 4 * i + j
                elif i < 10:
                    r = at
                else:
                    r = raw_of(0, U_MLP + 4 * (i - 10) + j) + 1
                step = 8
                wait_loaded(dve, r, it, step)
                if j == 0:
                    if i:
                        dve.wait_ge(mod_mm, i + it)
                    chain(dve.tensor_scalar(macc[:, :], raw[:, r % RING, 0, :], cvec[:, 0:1], None, ALU.mult), loop)
                else:
                    dve.wait_ge(slab_split, r + step * it)
                    chain(dve.scalar_tensor_tensor(macc[:, :], raw[:, r % RING, 0, :], cvec[:, 2 * j:2 * j + 1], macc[:, :],
                                                   ALU.mult, ALU.add), loop)
                dve.scalar_tensor_tensor(macc[:, :], raw[:, r % RING, 1, :], cvec[:, 2 * j + 1:2 * j + 2], macc[:, :],
                                         ALU.mult, ALU.add).then_inc(slab_split, 1)

            def mod_bias(i, it=0):
                lb, blk = mod_block(i)
                dve.wait_ge(mod_mm, i + 1 + it)
                dst = modc[:, lb, bass.ds(4 * it + 4 * blk, 4)]
                bias = prm[:, lb, bass.ds(4 * it + 4 * blk, 4)]
                dve.tensor_tensor(dst, ps[:, mod_bank(i), 0:4], bias, ALU.add).then_inc(mod_col, 1)

            def mod_in_a(u):
                for i, j, r in mod_behind(u):
                    fold_mod(i, j, at=r)
                    if j == 1 and i not in (MOD_FRONT, 8):
                        mod_bias(i - 1)

            def h_low(e, k):
                dve.wait_ge(h_hi_ready, 8 * e + k + 1)
                dve.tensor_tensor(h_lo[:, k, :], h32[:, k % 2, :], h_hi[:, k, :].bitcast(F32), ALU.subtract)\
                   .then_inc(h_ready, 1)

            def gate_vector(n, gate):
                if n:
                    dve.wait_ge(xa_ready, 8 * (n + 1))
                chain(dve.tensor_scalar(vecs[:, VGP, :], gate, 1.0, None, ALU.add))

            def vectors(e):
                n = e - 1
                m = modc
                if n % 2 == 0:
                    l = n // 2
                    gate, sc, sh = m[:, l, 16:24], m[:, l, 32:40], m[:, l, 24:32]
                    g, b = prm[:, l, C_LN1G:C_LN1G + KD], prm[:, l, C_LN1B:C_LN1B + KD]
                else:
                    l = n // 2
                    dve.wait_ge(mod_col, 24)
                    gate = m[:, l, 40:48]
                    g, b = prm[:, l, C_LN2G:C_LN2G + KD], prm[:, l, C_LN2B:C_LN2B + KD]
                    if l + 1 < LAYERS:
                        sc, sh = m[:, l + 1, 8:16], m[:, l + 1, 0:8]
                if n % 2:
                    gate_vector(n, gate)
                else:
                    dve.wait_ge(mod_col, 10)
                if n == 2 * LAYERS - 1:
                    return
                chain(dve.tensor_scalar(vecs[:, VS, :], sc, 1.0, None, ALU.add))
                dve.tensor_scalar(vecs[:, VAG, :], g, ALPHA, None, ALU.mult)
                dve.tensor_scalar(vecs[:, VAB, :], b, ALPHA, None, ALU.mult)
                dve.tensor_tensor(vecs[:, VG, :], g, vecs[:, VS, :], ALU.mult)
                chain(dve.tensor_tensor(vecs[:, VB, :], b, vecs[:, VS, :], ALU.mult))
                dve.tensor_tensor(vecs[:, VB, :], vecs[:, VB, :], sh, ALU.add).then_inc(vec_ready, 1)

            def residual(n, m):
                l, w = divmod(n, 2)
                g = NG * l + (G_OUT + 2 if w == 0 else NG - 2) + m // 4
                dve.wait_ge(xa_ready, 8 * n + m + 1)
                dve.wait_ge(bank_done, 4 * g + m % 4 + 1)
                if w == 0 and m == 0:
                    dve.wait_ge(out_half, 8 * (l + 1))
                dve.scalar_tensor_tensor(xr[:, m, :], ps[:, m % 4, :], vecs[:, VGP, m:m + 1], xr[:, m, :], ALU.mult, ALU.add)\
                   .then_inc(ln_r, 1)
                dve.wait_ge(ln_r, 8 * n + m + 1)
                if m == 1:
                    dve.tensor_tensor(s1[:, :], xr[:, 0, :], xr[:, 1, :], ALU.add).then_inc(ln_s1, 1)
                elif m > 1:
                    dve.wait_ge(ln_s1, 7 * n + m - 1)
                    dve.tensor_tensor(s1[:, :], s1[:, :], xr[:, m, :], ALU.add).then_inc(ln_s1, 1)

            def last_square(n):
                dve.wait_ge(ln_sq, 8 * (n + 1))
                dve.wait_ge(ln_s2, 7 * n + KD - 2)
                dve.tensor_tensor(s2[:, :], s2[:, :], sq[:, (KD - 1) % 2, :], ALU.add).then_inc(ln_s2, 1)

            def residual_ssd(l, m):
                dve.wait_ge(xa_ready, 16 * l + m + 1)
                dve.wait_ge(bank_done, 4 * (NG * l + G_OUT + m // 4) + m % 4 + 1)
                dve.scalar_tensor_tensor(xr[:, m, :], ps[:, m % 4, :], vecs[:, VGP, m:m + 1], xr[:, m, :], ALU.mult, ALU.add)\
                   .then_inc(out_half, 1)

            def gate(l, c):
                dve.wait_ge(z_tanh, CH * l + c + 1)
                dve.scalar_tensor_tensor(zs[:, c, :], zs[:, c, :], 1.0, ps[:, c, :], ALU.add, ALU.mult).then_inc(z_ready, 1)
                dve.wait_ge(z_ready, CH * l + c + 1)
                dve.scalar_tensor_tensor(yt[:, c, :], yt[:, c, :], 0.5, zs[:, c, :], ALU.mult, ALU.mult).then_inc(gated, 1)

            def newton(w):
                v0, y0, a = nrm[:, 0, 0:w], nrm[:, 2, 0:w], nrm[:, 3, 0:w]
                chain(dve.tensor_tensor(a, y0, y0, ALU.mult))
                chain(dve.tensor_tensor(a, a, v0, ALU.mult))
                chain(dve.tensor_scalar(a, a, -0.5, 1.5, ALU.mult, ALU.add))
                chain(dve.tensor_tensor(a, a, y0, ALU.mult))

            def ln_scale(n):
                dve.wait_ge(ln_stats, n + 1)
                st = nrm[:, 4, :]
                chain(dve.tensor_copy(st, ps[:, 4, 0:8]))
                chain(dve.tensor_tensor(nrm[:, 3, 0:4], st[:, 0:4], st[:, 0:4], ALU.mult))
                dve.scalar_tensor_tensor(nrm[:, 0, 0:4], st[:, 4:8], EPS, nrm[:, 3, 0:4], ALU.add, ALU.subtract)\
                   .then_inc(ln_v, 1)
                dve.wait_ge(ln_y0, n + 1)
                newton(4)
                y = nrm[:, 3, 0:4]
                eye = ident.unsqueeze(1).to_broadcast([P, CH, P])
                dve.tensor_tensor(diag[:, 0, :, :], eye, y.unsqueeze(2).to_broadcast([P, CH, P]), ALU.mult)\
                   .then_inc(ln_diag, 1)
                chain(dve.scalar_tensor_tensor(nrm[:, 5, 0:4], st[:, 0:4], -1.0, y, ALU.mult, ALU.mult))
                dve.tensor_tensor(diag[:, 1, :, :], eye, nrm[:, 5, 0:4].unsqueeze(2).to_broadcast([P, CH, P]), ALU.mult)\
                   .then_inc(ln_diag, 1)

            def ln_tiles(n, ks):
                for k in ks:
                    dve.wait_ge(ln_rows, 2 * (n + 1))
                    chain(dve.tensor_tensor(xr[:, k, :], xr[:, k, :], ps[:, 5, :], ALU.mult))
                    dve.tensor_tensor(xr[:, k, :], xr[:, k, :], ps[:, 6, :], ALU.add).then_inc(ln_t, 1)
                if n < 2 * LAYERS - 1:
                    for k in ks:
                        h_low(n + 1, k)

            def conv(l, t):
                dve.wait_ge(conv_raw, 8 * l + t + 1)
                if t == 0:
                    dve.wait_ge(pads_ready, l + 1)
                dst = xsF[:, t, :] if t < 4 else bcF[:, t - 4, :]
                w = prm[:, l, C_CONVW + 4 * t:C_CONVW + 4 * t + 4]
                for i in (2, 1, 0):
                    ins = dve.scalar_tensor_tensor(dst, conv_in[:, t, i:i + SEQ], w[:, i:i + 1], dst, ALU.mult, ALU.add)
                    if i:
                        chain(ins)
                ins.then_inc(conv_lin, 1)

            def conv_end(l, t):
                dve.wait_ge(conv_tanh, 8 * l + t + 1)
                dst = xsF[:, t, :] if t < 4 else bcF[:, t - 4, :]
                dve.scalar_tensor_tensor(dst, conv_th[:, t % 2, :], 1.0, dst, ALU.add, ALU.mult).then_inc(conv_out, 1)

            def dt_first(l):
                dve.wait_ge(dt_turned, l + 1)
                bias = prm[:, l, C_DTB:C_DTB + HEADS].unsqueeze(1).to_broadcast([P, CH, HEADS])
                chain(dve.tensor_tensor(dts[:, DU, :].rearrange("p (c h) -> p c h", c=CH),
                                        ps[:, 7, 0:32].rearrange("p (c h) -> p c h", c=CH), bias, ALU.add))
                dve.scalar_tensor_tensor(dts[:, DA, :], dts[:, DU, :], -1.0, dts[:, DU, :], ALU.mult, ALU.max)\
                   .then_inc(dt_abs, 1)

            def dt_second(l):
                dve.wait_ge(dt_exp, l + 1)
                dve.tensor_scalar(dts[:, DW, :], dts[:, DE, :], 1.0, None, ALU.add).then_inc(dt_w, 1)
                dve.wait_ge(dt_w, l + 1)
                dve.scalar_tensor_tensor(dts[:, DN, :], dts[:, DW, :], -1.0, dts[:, DE, :], ALU.add, ALU.subtract)
                chain(dve.reciprocal(dts[:, DA, :], dts[:, DW, :]))
                chain(dve.tensor_tensor(dts[:, DN, :], dts[:, DN, :], dts[:, DA, :], ALU.mult))
                chain(dve.scalar_tensor_tensor(dts[:, DT, :], dts[:, DU, :], 0.0, dts[:, DN, :], ALU.max, ALU.subtract))
                dve.wait_ge(dt_ln, l + 1)
                chain(dve.tensor_tensor(dts[:, DT, :], dts[:, DT, :], dts[:, DL, :], ALU.add))
                ea = expa[:, l, :].unsqueeze(1).to_broadcast([P, CH, HEADS])
                dve.scalar_tensor_tensor(dts[:, DAA, :].rearrange("p (c h) -> p c h", c=CH),
                                         dts[:, DT, :].rearrange("p (c h) -> p c h", c=CH), -1.0, ea, ALU.mult, ALU.mult)\
                   .then_inc(a_ready, 1)

            def sums(l):
                dve.wait_ge(cs_mm, l + 1)
                chain(dve.tensor_copy(dts[:, DCS, :], ps[:, 7, 32:64]))
                dve.tensor_scalar(dts[:, DN, :], dts[:, DCS, :], -1.0, None, ALU.mult)
                dve.tensor_tensor(dts[:, DDEC, :], ps[:, 7, 64:96], dts[:, DCS, :], ALU.subtract).then_inc(cs_ready, 1)

            def per_head(ap):
                return ap.unsqueeze(2).to_broadcast([P, HEADS, HDIM])

            def heads(ap):
                return ap.rearrange("p (h d) -> p h d", h=HEADS)

            def ssd_mid(l, c):
                cs = slice(c * HEADS, (c + 1) * HEADS)
                if c == 0:
                    dve.wait_ge(cs_exp, l + 1)
                    chain(dve.tensor_tensor(dts[:, DDEC, :], dts[:, DDEC, :], dts[:, DT, :], ALU.mult))
                dve.wait_ge(tok_copied, CH * l + c + 1)
                dve.tensor_tensor(heads(xdt[:, :]), heads(xs_tok[:, c, :]), per_head(dts[:, DT, cs]), ALU.mult)
                dve.tensor_tensor(heads(xdec[:, :]), heads(xs_tok[:, c, :]), per_head(dts[:, DDEC, cs]), ALU.mult)\
                   .then_inc(xd_ready, 1)
                dve.wait_ge(l_ready, CH * l + c + 1)
                for g in range(2):
                    cb = ps[:, 7, g * P:(g + 1) * P].unsqueeze(1).to_broadcast([P, 4, P])
                    last = dve.tensor_tensor(mm[:, 4 * g:4 * g + 4, :], lm[:, 4 * g:4 * g + 4, :], cb, ALU.mult)
                last.then_inc(m_ready, 1)

            def ssd_end(l, c):
                cs = slice(c * HEADS, (c + 1) * HEADS)
                dve.wait_ge(ssd_p2, CH * l + c + 1)
                dve.wait_ge(skip_ready, CH * l + c + 1)
                off = lm[:, 0:4, :].rearrange("p a b -> p (a b)")
                if c:
                    dve.tensor_tensor(heads(off), heads(ps[:, 5, :]), per_head(dts[:, DEA, cs]), ALU.mult)
                chain(dve.tensor_tensor(yt[:, c, :], yt[:, c, :], ps[:, 4, :], ALU.add))
                if c:
                    chain(dve.tensor_tensor(heads(state[:, :]), heads(state[:, :]), per_head(dts[:, DTOT, cs]), ALU.mult))
                    dve.tensor_tensor(yt[:, c, :], yt[:, c, :], off, ALU.add)
                    dve.tensor_tensor(state[:, :], state[:, :], ps[:, 6, :], ALU.add).then_inc(ssd_d2, 1)
                else:
                    dve.tensor_copy(state[:, :], ps[:, 6, :]).then_inc(ssd_d2, 1)
                dve.wait_ge(ssd_d2, CH * l + c + 1)

            def rope_tile(l, t):
                if t == 0:
                    dve.wait_ge(rope_loaded, 32 * (l + 1))
                dve.wait_ge(rot_dma[t % 2], 64 * (4 * l + t // 2 + 1))
                x = q[:, t, :] if t < 4 else kpad[:, 0, t - 4, :]
                r = rot[:, t % 2, :]
                dve.tensor_tensor(r, r, sinT[:, :], ALU.mult)
                chain(dve.tensor_tensor(x, x, cosT[:, :], ALU.mult))
                if t < 4:
                    dve.tensor_tensor(x, x, r, ALU.add).then_inc(rope_done, 1)
                else:
                    h = t - 4
                    dve.tensor_tensor(kpad[0:64, 0, h, :], x[0:64, :], r[0:64, :], ALU.add)
                    dve.tensor_tensor(kpad[64:128, 1, h, :], x[64:128, :], r[64:128, :], ALU.add).then_inc(rope_done, 1)

            def biggest(l, t):
                i, h = divmod(t, AH)
                dve.wait_ge(qk_done, 16 * l + t + 1)
                chain(dve.tensor_reduce(att[:, 2, 2 * h:2 * h + 2], ps[:, 4:6, 0:(i + 1) * P], AXX, ALU.max))
                dve.tensor_scalar(att[:, 0, 2 * h:2 * h + 2], att[:, 2, 2 * h:2 * h + 2], -0.125, None, ALU.mult)\
                   .then_inc(nb_ready, 1)

            def combine(l, t):
                i, h = divmod(t, AH)
                n = (i + 1) * P
                dve.wait_ge(exp_done, 16 * l + t + 1)
                rs = att[:, 3, 2 * h:2 * h + 2]
                chain(dve.reciprocal(rs, att[:, 1, 2 * h:2 * h + 2]))
                dve.tensor_tensor(rs[:, 1:2], rs[:, 1:2], lam[:, l, 0:1], ALU.mult)
                p0, p1 = prob[:, t % 2, 0, 0:n], prob[:, t % 2, 1, 0:n]
                chain(dve.tensor_scalar(p0, p0, rs[:, 0:1], None, ALU.mult))
                dve.scalar_tensor_tensor(p0, p1, rs[:, 1:2], p0, ALU.mult, ALU.add).then_inc(w_ready, 1)

            def o_out(l, i):
                dve.wait_ge(pv_done, 16 * l + 4 * i + 4)
                if i:
                    dve.wait_ge(tro_mm, CH * l + i)
                dve.wait_ge(o_sq, CH * l + i + 1)
                dve.tensor_copy(o_tok[:, :], ps[:, 7, :]).then_inc(o_copied, 1)
                dve.tensor_scalar(nrm[:, 0, 0:4], ssq[:, 0:4], 1.0 / P, EPS, ALU.mult, ALU.add).then_inc(att_v, 1)

            def o_scale(l, i):
                dve.wait_ge(att_y0, CH * l + i + 1)
                newton(4)
                o3 = o_tok[:, :].rearrange("p (h d) -> p h d", h=AH)
                dve.tensor_tensor(o3, o3, nrm[:, 3, 0:4].unsqueeze(2).to_broadcast([P, AH, P]), ALU.mult)\
                   .then_inc(o_scaled, 1)

            def yo_low(l, i):
                tok = slice(i * P, (i + 1) * P)
                dve.wait_ge(yo_hi, CH * l + i + 1)
                dve.scalar_tensor_tensor(y_lo[:, 4:8, tok], ps[:, 6, :].rearrange("p (h t) -> p h t", h=4), awc[:, l:l + 1],
                                         y_hi[:, 4:8, tok].bitcast(F32), ALU.mult, ALU.subtract).then_inc(yo_ready, 1)

            def step(l, t):
                if 1 <= t <= 16:
                    combine(l, t - 1)
                if t >= 5 and t % 4 == 1:
                    o_scale(l, (t - 5) // 4)
                if t < 16:
                    biggest(l, t)
                if t >= 4 and t % 4 == 0:
                    o_out(l, (t - 4) // 4)
                if t in (STEP_COUNT - 5, STEP_COUNT - 1):
                    for m in range(4):
                        residual_ssd(l, m if t == STEP_COUNT - 5 else 4 + m)
                if t >= 5 and t % 4 == 1:
                    yo_low(l, (t - 5) // 4)

            def mlp_end(l, it):
                for j in range(2):
                    dve.wait_ge(mlp_th, FT * l + j + 1 + 2 * it)
                    dve.scalar_tensor_tensor(sq[:, j, :], sq[:, j, :], 1.0, ps[:, j, :], ALU.add, ALU.mult).then_inc(mlp_a, 1)
                for j in range(2):
                    dve.wait_ge(bank_done, 4 * (NG * l + G_MLP) + 2 + j + 1 + 4 * it)
                    dve.wait_ge(mlp_a, FT * l + j + 1 + 2 * it)
                    dve.scalar_tensor_tensor(h32[:, j, :], sq[:, j, :], 0.5, ps[:, 2 + j, :], ALU.mult, ALU.mult)\
                       .then_inc(mlp_f, 1)
                for j in range(2):
                    dve.wait_ge(f_hi_ready, FT * l + j + 1 + 2 * it)
                    dve.tensor_tensor(f_lo[:, bass.ds(2 * it + j, 1), :], h32[:, j:j + 1, :],
                                      f_hi[:, bass.ds(2 * it + j, 1), :].bitcast(F32), ALU.subtract).then_inc(f_ready, 1)

            dve.wait_ge(c_loaded, 16)
            dve.memset(meancol[:, :], 1.0 / D)
            dve.tensor_scalar(cond[:, 1, :], cvec, 0.5, None, ALU.mult).then_inc(cond_half, 1)
            dve.wait_ge(cond_tanh, 1)
            chain(dve.scalar_tensor_tensor(cvec, cond[:, 2, :], 1.0, cond[:, 1, :], ALU.add, ALU.mult))
            fold_mod(0, 0)
            dve.wait_ge(small_loaded, 48)
            dve.tensor_copy(maskb[:, :], maskf)
            dve.tensor_copy(identb[:, :], ident).then_inc(consts_ready, 1)
            lq = lamt[:, :, :, :].rearrange("p l (a b) d -> p l a b d", b=2)
            chain(dve.tensor_tensor(lamp[:, :, :, :], lq[:, :, :, 0, :], lq[:, :, :, 1, :], ALU.mult))
            for l in range(LAYERS):
                last = dve.tensor_reduce(lam[:, l, 0:2], lamp[:, l, :, :], AXX, ALU.add)
            last.then_inc(lam_sums, 1)
            for l in range(LAYERS):
                init = 0.8 - 0.6 * math.exp(-0.3 * l)
                dve.tensor_scalar(prm[:, l, C_CONVW:C_CONVW + 40], prm[:, l, C_CONVW:C_CONVW + 40], 0.5, None, ALU.mult)
                dve.tensor_scalar(awc[:, l:l + 1], prm[:, l, C_ATTNW:C_ATTNW + 1], 1.0 - init, None, ALU.mult)
            dve.wait_ge(lam_exp, 1)
            for l in range(LAYERS):
                init = 0.8 - 0.6 * math.exp(-0.3 * l)
                chain(dve.tensor_tensor(lam[:, l, 0:1], lam[:, l, 3:4], lam[:, l, 2:3], ALU.subtract))
                chain(dve.tensor_scalar(lam[:, l, 0:1], lam[:, l, 0:1], -init, None, ALU.add))
            for i in range(MOD_FRONT):
                for j in range(4):
                    if i or j:
                        fold_mod(i, j)
                mod_bias(i)
            dve.wait_ge(mod_col, MOD_FRONT)
            dve.tensor_scalar(vecs[:, VG, :], modc[:, 0, 8:16], 1.0, None, ALU.add)
            dve.tensor_copy(vecs[:, VB, :], modc[:, 0, 0:8]).then_inc(vec_ready, 1)
            for u in range(3):
                split(0, u)
                mod_in_a(u)
            h_low(0, 0)
            h_low(0, 1)
            for l in range(LAYERS):
                e = 2 * l
                for u in range(U_MLP):
                    if u not in (U_OUT - 1, U_MLP - 1):
                        split(l, u + 3)
                    if l == 0:
                        mod_in_a(u + 3)
                        if U_MLP <= u + 3 < U_MLP + 2:
                            fold_mod(10, u + 3 - U_MLP)
                    for i in (7, 9):
                        if u == MOD_LAST[i][0] - 1 and l == 0:
                            mod_bias(i)
                    if u < 3:
                        if l:
                            ln_tiles(2 * l - 1, [2 * u + 2, 2 * u + 3])
                        else:
                            h_low(0, 2 * u + 2)
                            h_low(0, 2 * u + 3)
                    if u == 0:
                        dve.wait_ge(wdt_hi_ready, l + 1)
                        dve.tensor_tensor(wdt_lo[:, :, :], wdt_raw[:, :, :], wdt_hi[:, :, :].bitcast(F32), ALU.subtract)\
                           .then_inc(wdt_ready, 1)
                    if u == 4:
                        dt_first(l)
                    if 4 <= u <= 11:
                        conv(l, u - 4)
                    if u == 4:
                        dt_second(l)
                    if 5 <= u <= 12:
                        conv_end(l, u - 5)
                    if u == 7:
                        sums(l)
                    if u == U_OUT:
                        step(l, AHEAD_OF_OUT)
                        dve.wait_ge(gate_sq, CH * (l + 1))
                        dve.tensor_scalar(nrm[:, 0, :], nrm[:, 5, :], 1.0 / 256, EPS, ALU.mult, ALU.add).then_inc(ssd_v, 1)
                        dve.wait_ge(ssd_y0, l + 1)
                        newton(8)
                        dve.wait_ge(ssdw_loaded, 16 * (l + 1))
                        for c in range(CH):
                            for g in range(2):
                                gd = slice(g * 256, (g + 1) * 256)
                                last = dve.scalar_tensor_tensor(yt[:, c, gd], yt[:, c, gd],
                                                                nrm[:, 3, 2 * c + g:2 * c + g + 1],
                                                                ssdw_row[:, gd], ALU.mult, ALU.mult)
                            last.then_inc(ys_scaled, 1)
                        for c in range(CH):
                            tok = slice(c * P, (c + 1) * P)
                            dve.wait_ge(ys_hi, CH * l + c + 1)
                            dve.tensor_tensor(y_lo[:, 0:4, tok], ps[:, c, :].rearrange("p (h t) -> p h t", h=4),
                                              y_hi[:, 0:4, tok].bitcast(F32), ALU.subtract).then_inc(ys_ready, 1)
                    for what, t in between(u):
                        if what == "first":
                            ssd_mid(l, t)
                        elif what == "second":
                            ssd_end(l, t)
                        elif what == "step_a":
                            step(l, t)
                        elif what == "z":
                            gate(l, t)
                    if u == U_OUT - 1:
                        split(l, u + 3)
                    for t in ROPE_AT.get(u, []):
                        rope_tile(l, t)
                    if u == U_OUT:
                        if l == 0:
                            dve.wait_ge(mod_col, 6)
                        gate_vector(2 * l, modc[:, l, 16:24])
                    if u == 30:
                        for m in range(4):
                            residual(2 * l, m)
                        vectors(2 * l + 1)
                for m in range(4, 8):
                    residual(2 * l, m)
                last_square(2 * l)
                split(l, U_MLP + 2)
                if l == 0:
                    fold_mod(10, 2)
                ln_scale(2 * l)
                ln_tiles(2 * l, [0, 1])

                def mlp_mod(j, it, loop):
                    if l:
                        return
                    fold_mod(10, (j + 3) % 4, it=it if j == 0 else it + 1, loop=loop)
                    if j == 2:
                        mod_bias(10, it)

                for j in range(4):
                    split(l, U_MLP + j + 3)
                    if l == 0:
                        fold_mod(*((11, j - 1) if j else (10, 3)))
                        if j == 2:
                            mod_bias(10)
                    if j < 3:
                        ln_tiles(2 * l, [2 * j + 2, 2 * j + 3])
                before = chained[0]
                with dve.Fori(1, MLP_G) as g:
                    loop = (g - 1) * (4 if l == 0 else 0)
                    mlp_end(l, g - 1)
                    for j in range(4):
                        split(l, U_MLP + j + 3, it=g)
                        mlp_mod(j, g, loop)
                if l == 0:
                    assert chained[0] - before == 4
                    chained[0] = before + 4 * (MLP_G - 1)
                for u in range(U_DOWN, UNITS):
                    i = u - U_DOWN
                    if i == 0:
                        mlp_end(l, MLP_G - 1)
                    if i < 2 * DOWN_SLABS - 1:
                        split(l, u + 3)
                    if l == 0 and i + 3 < MOD_DOWN:
                        fold_mod(21 + (i + 3) // 4, (i + 3) % 4)
                    if l == 0 and i in (2, 6, 10):
                        mod_bias(21 + (i - 2) // 4)
                    if i == 11:
                        vectors(2 * l + 2)
                        for m in range(4):
                            residual(2 * l + 1, m)
                for m in range(4, 8):
                    residual(2 * l + 1, m)
                last_square(2 * l + 1)
                split(l, UNITS - 1 + 3)
                ln_scale(2 * l + 1)
                if l + 1 < LAYERS:
                    ln_tiles(2 * l + 1, [0, 1])
                else:
                    ln_tiles(2 * l + 1, range(KD))
                    dve.wait_ge(ln_t, 8 * 2 * LAYERS)
                    for k in range(KD):
                        dve.tensor_scalar(xr[:, k, :], xr[:, k, :], prm[:, l, C_LN2G + k:C_LN2G + k + 1],
                                          prm[:, l, C_LN2B + k:C_LN2B + k + 1], ALU.mult, ALU.add).then_inc(out_tile, 1)


def kernel(**inputs):
    import numpy as _np
    import concourse.bacc as _bacc
    from concourse import mybir as _mybir
    from concourse.bass_utils import run_bass_kernel_spmd as _run

    f = {k: _np.asarray(a) for k, a in inputs.items()}
    L = LAYERS
    SSD_IN = 512

    def cols(a):
        return a.reshape(-1, P).T

    def rows(a):
        return _np.broadcast_to(a.reshape(1, -1), (P, a.size))

    w = f["w_in"]
    z, xbc, dt, qkv = w[:, :, :SSD_IN], w[:, :, SSD_IN:SSD_IN + D], w[:, :, SSD_IN + D:SSD_IN + D + HEADS], \
        w[:, :, SSD_IN + D + HEADS:]
    par = _np.stack([_np.concatenate(
        [cols(f["b_mod"][l]), cols(f["ln1_g"][l]), cols(f["ln1_b"][l]), cols(f["ln2_g"][l]), cols(f["ln2_b"][l])]
        + [f["conv_w"][l][:, t * P:(t + 1) * P].T for t in range(8)]
        + [cols(f["conv_b"][l]), cols(f["attn_norm_w"][l]), rows(f["dt_bias"][l]), rows(f["a_log"][l]),
           rows(f["d_skip"][l])], axis=1) for l in range(L)], axis=1)
    eye = _np.eye(P, dtype=_np.float32)
    tri = _np.triu(_np.ones((P, P), _np.float32))
    mask = ((tri - 1) * _np.float32(-NEG)).astype(_np.float32)
    inv = (1.0 / (_np.float32(10000.0) ** (_np.arange(0, HDIM, 2, dtype=_np.float32) / _np.float32(HDIM))))
    ang = _np.arange(SEQ, dtype=_np.float32)[:, None] * inv.astype(_np.float32)[None, :]
    ang = _np.concatenate([ang, ang], -1).T
    sign = _np.where(_np.arange(HDIM) < HDIM // 2, -1.0, 1.0).astype(_np.float32)[:, None]
    rope = _np.stack([_np.tile(_np.cos(ang), (2, 1)), _np.tile(_np.sin(ang) * sign, (2, 1))]).astype(_np.float32)
    arrays = {
        "xT": f["x"][0].T,
        "ccol": cols(f["c"][0]),
        "w_mod": f["w_mod"],
        "w_in": _np.concatenate([xbc, qkv, z], axis=2),
        "w_out": f["w_out"],
        "w_gu": f["w_gate_up"].reshape(L, D, 2, MLP_G, 256).transpose(0, 1, 3, 2, 4).reshape(L, D, 2 * D_FF),
        "w_down": f["w_down"],
        "par": par,
        "ssdw": _np.stack([rows(f["ssd_norm_w"][l]) for l in range(L)]),
        "lamqk": _np.broadcast_to(f["lam_qk"][None], (P, L, 4, 64)),
        "wdt": dt.reshape(L, KD, P, HEADS).transpose(0, 2, 1, 3),
        "consts": _np.concatenate([eye, tri, mask, _np.ones((P, P), _np.float32)], axis=1),
        "rope": rope,
    }
    arrays = {k: _np.ascontiguousarray(a) for k, a in arrays.items()}
    nc = _bacc.Bacc("TRN2", target_bir_lowering=False, num_devices=1)
    args = [nc.dram_tensor(f"in_{k}", a.shape, _mybir.dt.from_np(a.dtype), kind="ExternalInput").ap()
            for k, a in arrays.items()]
    out = nc.dram_tensor("outT", (D, SEQ), F32, kind="ExternalOutput").ap()
    kernel_body(nc, *args, out)
    r = _run(nc, [{f"in_{k}": a for k, a in arrays.items()}], core_ids=[0])
    return r.results[0]["outT"].T[None]
```

```python
import math
from contextlib import ExitStack

import numpy as np

import concourse.bass as bass
from concourse import mybir

F32 = mybir.dt.float32
F32R = mybir.dt.float32r
BF16 = mybir.dt.bfloat16
ALU = mybir.AluOpType
ACT = mybir.ActivationFunctionType
AXX = mybir.AxisListType.X

P = 128
LAYERS = 2
D = 1024
SEQ = 512
CH = SEQ // P
KD = D // P
HEADS = 8
HDIM = 64
AH = 4
D_FF = 2816
FT = D_FF // P
EPS = 1e-5
ALPHA = (2 * LAYERS) ** 0.25
NEG = -1.0e30
RING = 4

MLP_G = FT // 2
GROUPS = ["xs", "bc", "q", "k", "v", "z", "out_s0", "out_s1", "out_a0", "out_a1"] + \
    [f"mlp{g}" for g in range(MLP_G)] + ["down0", "down1"]
NG = len(GROUPS)
G_OUT, G_MLP = GROUPS.index("out_s0"), GROUPS.index("mlp0")
U_OUT = 4 * G_OUT
U_MLP = U_OUT + 2 * 4
U_DOWN = U_MLP + 4 * MLP_G
DOWN_SLABS = FT // 2
UNITS = U_DOWN + 2 * DOWN_SLABS
MOD_FRONT = 4
MOD_A = [0] * 3 + [2] * 6 + [1] * 4 + [0] * 9 + [1] * 8
MOD_GATHER_AT = (2, 4, 6, 9)
MOD_ROWS = 14
MOD_DOWN = [1] * 3 + [2] * 4 + [1] * 5

C_LN1G, C_LN1B, C_LN2G, C_LN2B = 48, 56, 64, 72
C_CONVW, C_CONVB, C_ATTNW, C_DTB, C_ALOG, C_DSKIP = 80, 112, 120, 121, 129, 137
NPAR = 145


def mod_block(i):
    if i < MOD_FRONT:
        return 0, (0, 2, 1, 3)[i]
    if i < 10:
        return 0, i
    if i < 22:
        return 1, i - 10
    return 0, i - 12


def mod_bank(i):
    return 5 + i % 2 if i < 8 else (7, 5)[i - 8]


def mod_slot(i):
    return i % 2 if i < 10 else 0


def raw_mlp():
    return 4 * MOD_FRONT + sum(MOD_A) + U_MLP


def raw_at(l, u, it):
    if isinstance(it, int) or l:
        return raw_of(l, u)
    return raw_mlp() + 2 * (u - U_MLP) - 4


def raw_of(l, u):
    if u >= UNITS:
        return raw_of(l + 1, u - UNITS)
    if l == 0:
        front = 4 * MOD_FRONT
        if u < 2:
            return front // 2 + u
        if u < U_MLP:
            return front + u + sum(MOD_A[:u])
        i = u - U_MLP
        at = raw_mlp()
        if i < 4:
            return at + i
        if u < U_DOWN:
            return at + 2 * i - 4
        return at + 8 * MLP_G - 4 + u - U_DOWN + sum(MOD_DOWN[:u - U_DOWN])
    return raw_of(0, UNITS - 1) + 1 + u


def mod_front(i, j):
    return 4 * i + j + (0 if i < MOD_FRONT // 2 else 2)


def mod_behind(u):
    first = sum(MOD_A[:u])
    n = MOD_A[u] if u < len(MOD_A) else 0
    return [(MOD_FRONT + m // 4, m % 4, raw_of(0, u) + 1 + m - first) for m in range(first, first + n)]


MOD_LAST = {i: (u, r) for u in range(len(MOD_A)) for i, j, r in mod_behind(u) if j == 3}


def mod_reduced_at(i):
    return MOD_LAST[i][0] - (i > 4) if i < 8 else U_OUT + 4


def mod_behind_down(u):
    first = 4 * (MLP_G - 1) + sum(MOD_DOWN[:u - U_DOWN])
    n = MOD_DOWN[u - U_DOWN] if u - U_DOWN < len(MOD_DOWN) else 0
    return [(m // 4, m % 4, raw_of(0, u) + 1 + m - first) for m in range(first, first + n)]


def group_of(u):
    if u < U_OUT:
        return u // 4, u % 4, 4
    if u < U_MLP:
        return G_OUT + (u - U_OUT) // 2, (u - U_OUT) % 2, 2
    if u < U_DOWN:
        return G_MLP + (u - U_MLP) // 4, u % 4, 4
    return NG - 2 + (u - U_DOWN) // DOWN_SLABS, (u - U_DOWN) % DOWN_SLABS, DOWN_SLABS


STEP_COUNT = AH * CH + 2
AHEAD_OF_OUT = 9
FIRST_STEP_AT = 39
Z_PAIR = U_OUT - 2
V_PAIR = Z_PAIR - 4
PAIRS = (V_PAIR, Z_PAIR, U_OUT + 4, U_OUT + 6)
BETWEEN = {17: [("dt", 0)]}
for c in range(CH):
    BETWEEN[2 * (26 + 3 * c) + 1] = [("first", c)]
    BETWEEN[2 * (28 + 3 * c) + 1] = [("second", c)]
for t in range(AHEAD_OF_OUT):
    BETWEEN.setdefault(2 * (FIRST_STEP_AT + t) + 1, []).append(("step_a", t))
    if t < AHEAD_OF_OUT - 1:
        BETWEEN.setdefault(2 * (FIRST_STEP_AT + t) + 2, []).append(("step_b", t))
for c in range(CH):
    BETWEEN[4 * Z_PAIR + 2 * c + 1].append(("z", c))
BETWEEN[4 * U_OUT] = [("turn_w", AHEAD_OF_OUT - 1)]
BETWEEN[4 * U_OUT + 1] = [("step_b", AHEAD_OF_OUT)]
for t in range(AHEAD_OF_OUT + 1, STEP_COUNT - 1):
    at = 4 * U_OUT + 2 * (t - AHEAD_OF_OUT)
    BETWEEN[at] = [("step_a", t)]
    BETWEEN[at + 1] = [("step_b", t)]
ROPE_AT = {13: [0, 1], 14: [2], 15: [3], 16: [4], 17: [5], 18: [6], 19: [7]}


def between(u):
    return [x for i in range(4) for x in BETWEEN.get(4 * u + i, [])]


def split_in_step(u):
    if FIRST_STEP_AT // 2 < u < U_OUT - 1 or U_OUT <= u < U_OUT + 4:
        what, t = [x for x in between(u) if x[0] in ("step_a", "turn_w")][0]
        return t + (what == "turn_w")
    return None


def kernel_body(nc, xT, ccol, w_mod, w_in, w_out, w_gu, w_down, par, ssdw, lamqk, wdt, consts, rope, outT):
    ctx = ExitStack()
    with ctx:
        base = nc.sbuf_base
        base += -base % 32
        used = [0]

        def place(name, shape, dt, at=None):
            size = int(np.prod(shape[1:])) * (2 if dt == BF16 else 4)
            off = used[0] if at is None else at
            if at is None:
                used[0] += size + (-size) % 32
            return nc.alloc_sbuf_tensor_at(name, shape, dt, offset=base + off)

        KB = 1024
        xr = place("residual", [P, KD, SEQ], F32)
        h_hi = place("h_hi", [P, KD, SEQ], F32R)
        h_lo = place("h_lo", [P, KD, SEQ], F32R)
        F0 = used[0]
        used[0] += 88 * KB
        T0 = used[0]
        used[0] += 12 * KB
        f_hi = place("f_hi", [P, FT, SEQ], F32R, F0)
        f_lo = place("f_lo", [P, FT, SEQ], F32R, F0 + 44 * KB)
        conv_in = place("conv_in", [P, 8, SEQ + 3], F32, F0)
        q = place("q", [P, AH, SEQ], F32, F0)
        kpad = place("kpad", [P, 2, AH, SEQ], F32, F0 + 8 * KB)
        v = place("v", [P, CH, SEQ], F32, F0 + 24 * KB)
        xsF = place("xsF", [P, 4, SEQ], F32, F0 + 32 * KB)
        zs = place("zs", [P, CH, SEQ], F32, F0 + 32 * KB)
        yt = place("y_tok", [P, CH, SEQ], F32, F0 + 40 * KB)
        bcF = place("bcF", [P, 4, SEQ], F32, F0 + 48 * KB)
        xs_tok = place("xs_tok", [P, CH, SEQ], F32, F0 + 56 * KB)
        y_hi = place("y_hi", [P, KD, SEQ], F32R, F0 + 48 * KB)
        b_tok = place("b_tok", [P, CH, 256], F32, F0 + 64 * KB)
        xdt = place("xdt", [P, SEQ], F32, F0 + 68 * KB)
        xdec = place("xdec", [P, SEQ], F32, F0 + 70 * KB)
        lm = place("decay_l", [P, HEADS, P], F32, F0 + 72 * KB)
        mm = place("m_t", [P, HEADS, P], F32, F0 + 76 * KB)
        conv_th = place("conv_th", [P, 2, SEQ], F32, F0 + 76 * KB)
        y_lo = place("y_lo", [P, KD, SEQ], F32R, F0 + 64 * KB)
        o_tok = place("o_tok", [P, SEQ], F32, F0 + 80 * KB)
        junk = place("junk", [P, SEQ], F32, F0 + 82 * KB)
        cosT = place("cosT", [P, SEQ], F32, F0 + 84 * KB)
        sinT = place("sinT", [P, SEQ], F32, F0 + 86 * KB)
        ssdw_row = place("ssdw_row", [P, SEQ], F32, F0 + 84 * KB)
        s1 = place("s1", [P, SEQ], F32, T0)
        s2 = place("s2", [P, SEQ], F32, T0 + 2 * KB)
        sq = place("sq", [P, 2, SEQ], F32, T0 + 4 * KB)
        diag = place("diag", [P, 2, CH, P], F32, T0 + 4 * KB)
        h32 = place("h32", [P, 2, SEQ], F32, T0 + 8 * KB)
        mparts = place("mod_parts", [P, 2, SEQ], F32R, T0)
        modT = place("mod_t", [P, SEQ], F32, T0)
        dtF = place("dt_feature", [P, SEQ], F32, T0)
        rot = place("rot", [P, 2, SEQ], F32, F0 + 80 * KB)
        state = place("state", [P, SEQ], F32, T0 + 4 * KB)
        prob = place("prob", [P, 2, 2, SEQ], F32, T0)
        wT = place("wT", [P, 2, CH, P], F32, T0 + 8 * KB)
        lamt = place("lamt", [P, LAYERS, 4, 64], F32, T0)
        lamp = place("lamp", [P, LAYERS, 2, 64], F32, T0 + 2 * KB)
        raw = place("raw", [P, RING, 2, SEQ], F32)
        w_hi = place("w_hi", [P, RING, 2, SEQ], F32R)
        w_lo = place("w_lo", [P, RING, 2, SEQ], F32R)
        macc = place("mod_acc", [P, 2, SEQ], F32)
        cst = place("consts", [P, 4 * P], F32)
        ident, tri, maskf, ones = (cst[:, i * P:(i + 1) * P] for i in range(4))
        sel = place("mod_select", [P, 2 * MOD_ROWS], F32)
        sel_row = place("mod_select_row", [P, MOD_ROWS], F32R)
        maskb = place("mask_bf", [P, P], BF16)
        identb = place("ident_bf", [P, P], BF16)
        meancol = place("meancol", [P, 1], F32)
        prm = place("params", [P, LAYERS, NPAR], F32)
        modc = place("modc", [P, LAYERS, 48], F32)
        cond = place("cond", [P, 3, KD], F32)
        cvec = cond[:, 0, :]
        wdt_raw = place("wdt_raw", [P, KD, HEADS], F32)
        wdt_hi = place("wdt_hi", [P, KD, HEADS], F32R)
        wdt_lo = place("wdt_lo", [P, KD, HEADS], F32R)
        dts = place("dts", [P, 12, CH * HEADS], F32)
        (DU, DA, DE, DW, DN, DL, DT, DAA, DCS, DEA, DDEC, DTOT) = range(12)
        expa = place("expa", [P, LAYERS, HEADS], F32)
        lam = place("lam", [P, LAYERS, 4], F32)
        awc = place("attn_w", [P, LAYERS], F32)
        att = place("att_small", [P, 4, 2 * AH], F32)
        nrm = place("norm_small", [P, 6, 8], F32)
        nrs = place("norm_ssd_small", [P, 6, 8], F32)
        ssq = place("ssq", [P, 8], F32)
        vecs = place("ln_vecs", [P, 6, KD], F32)
        (VGP, VS, VG, VB, VAG, VAB) = range(6)
        assert base + used[0] <= nc.sbuf_usable_end, (used[0], nc.sbuf_usable_end - base)

        ps = ctx.enter_context(nc.psum_tensor("ps", [P, 8, SEQ], F32))

        def sem(name):
            return ctx.enter_context(nc.semaphore(name))

        raw_loaded = [sem(f"raw_loaded{i}") for i in range(RING)]
        small_loaded = sem("small_loaded")
        c_loaded = sem("c_loaded")
        x_loaded = sem("x_loaded")
        wdt_loaded = sem("wdt_loaded")
        rope_loaded = sem("rope_loaded")
        ssdw_loaded = sem("ssdw_loaded")
        hi_ready = sem("hi_ready")
        slab_split = sem("slab_split")
        slab_used = sem("slab_used")
        bank_done = sem("bank_done")
        dve_chain = sem("dve_chain")
        act_chain = sem("act_chain")
        consts_ready = sem("consts_ready")
        cond_half = sem("cond_half")
        cond_tanh = sem("cond_tanh")
        lam_sums = sem("lam_sums")
        lam_exp = sem("lam_exp")
        mod_mm = sem("mod_mm")
        mod_parts = sem("mod_parts")
        mod_rows = sem("mod_rows")
        mod_turned = sem("mod_turned")
        mod_col = sem("mod_col")
        vec_ready = sem("vec_ready")
        h_hi_ready = sem("h_hi_ready")
        h_ready = sem("h_ready")
        xa_ready = sem("xa_ready")
        wdt_hi_ready = sem("wdt_hi_ready")
        wdt_ready = sem("wdt_ready")
        conv_raw = sem("conv_raw")
        pads_ready = sem("pads_ready")
        conv_lin = sem("conv_lin")
        conv_tanh = sem("conv_tanh")
        conv_out = sem("conv_out")
        dt_mm = sem("dt_mm")
        dt_copied = sem("dt_copied")
        dt_turned = sem("dt_turned")
        dt_abs = sem("dt_abs")
        out_half = sem("out_half")
        dt_exp = sem("dt_exp")
        dt_w = sem("dt_w")
        dt_ln = sem("dt_ln")
        a_ready = sem("a_ready")
        cs_mm = sem("cs_mm")
        cs_ready = sem("cs_ready")
        cs_exp = sem("cs_exp")
        ssd_p1 = sem("ssd_p1")
        tok_copied = sem("tok_copied")
        l_ready = sem("l_ready")
        m_ready = sem("m_ready")
        xd_ready = sem("xd_ready")
        ssd_p2 = sem("ssd_p2")
        skip_ready = sem("skip_ready")
        ssd_d2 = sem("ssd_d2")
        qk_raw = sem("qk_raw")
        rot_dma = [sem(f"rot_dma{i}") for i in range(2)]
        rope_done = sem("rope_done")
        pad_half = sem("pad_half")
        kpad_ready = sem("kpad_ready")
        v_ready = sem("v_ready")
        z_tanh = sem("z_tanh")
        z_ready = sem("z_ready")
        gated = sem("gated")
        gate_sq = sem("gate_sq")
        ssd_v = sem("ssd_v")
        ssd_y0 = sem("ssd_y0")
        ys_scaled = sem("ys_scaled")
        ys_scaled_act = sem("ys_scaled_act")
        ys_weighted = sem("ys_weighted")
        ssd_rstd = sem("ssd_rstd")
        trs_mm = sem("trs_mm")
        ys_hi = sem("ys_hi")
        ys_ready = sem("ys_ready")
        qk_done = sem("qk_done")
        nb_ready = sem("nb_ready")
        exp_done = sem("exp_done")
        w_ready = sem("w_ready")
        wt_mm = sem("wt_mm")
        wt_ready = sem("wt_ready")
        pv_done = sem("pv_done")
        o_copied = sem("o_copied")
        o_sq = sem("o_sq")
        att_v = sem("att_v")
        att_y0 = sem("att_y0")
        o_scaled = sem("o_scaled")
        tro_mm = sem("tro_mm")
        yo_hi = sem("yo_hi")
        yo_ready = sem("yo_ready")
        ln_r = sem("ln_r")
        ln_s1 = sem("ln_s1")
        ln_sq = sem("ln_sq")
        ln_s2 = sem("ln_s2")
        ln_stats = sem("ln_stats")
        ln_v = sem("ln_v")
        ln_y0 = sem("ln_y0")
        ln_diag = sem("ln_diag")
        ln_rows = sem("ln_rows")
        ln_m = sem("ln_m")
        ln_t = sem("ln_t")
        h32_ready = sem("h32_ready")
        mlp_th = sem("mlp_th")
        mlp_a = sem("mlp_a")
        mlp_f = sem("mlp_f")
        f_hi_ready = sem("f_hi_ready")
        f_ready = sem("f_ready")
        out_tile = sem("out_tile")
        out_stored = sem("out_stored")

        def wait_loaded(eng, r, it=0, step=0):
            eng.wait_ge(raw_loaded[r % RING], 16 * (r // RING + 1) + (16 * step // RING) * it)

        def wait_used(eng, s, it=0):
            if s < 0:
                return
            l, u = divmod(s, UNITS)
            g, j, n = group_of(u)
            if j == n - 1:
                eng.wait_ge(bank_done, 4 * (NG * l + g + 1) + 4 * it)
            else:
                before = (UNITS - NG) * l + u - j - g
                eng.wait_ge(slab_used, before + j + 1 + 3 * it)

        def raw_step(l):
            return 8 if l == 0 else 4

        block = ctx.enter_context(nc.Block())

        @block.sync
        def _(sp):
            def w_src(l, u):
                g, j, _ = group_of(u)
                if g in (G_OUT + 2, G_OUT + 3):
                    j += 2
                rows = slice(2 * j * P, 2 * (j + 1) * P)
                if u < U_OUT:
                    return w_in[l, rows, g * SEQ:(g + 1) * SEQ].rearrange("(k p) n -> p k n", p=P)
                if u < U_MLP:
                    half = (g - G_OUT) % 2
                    return w_out[l, rows, half * SEQ:(half + 1) * SEQ].rearrange("(k p) n -> p k n", p=P)
                return w_down[l, rows, (g - NG + 2) * SEQ:(g - NG + 3) * SEQ].rearrange("(k p) n -> p k n", p=P)

            def room(r, it=0, step=0):
                if r >= RING:
                    sp.wait_ge(slab_split, r - RING + 1 + step * it)

            def load_w(l, u):
                r = raw_of(l, u)
                room(r)
                sp.dma_start(raw[:, r % RING, :, :], w_src(l, u)).then_inc(raw_loaded[r % RING], 16)

            def load_gu(l, j, it=0):
                r = raw_at(l, U_MLP + j, it)
                room(r, it, raw_step(l))
                src = w_gu[l, 2 * j * P:2 * (j + 1) * P, :].rearrange("(k p) n -> p k n", p=P)
                sp.dma_start(raw[:, r % RING, :, :], src[:, :, bass.ds(it * SEQ, SEQ)])\
                  .then_inc(raw_loaded[r % RING], 16)

            def load_mod(r, lb, j, it=0, step=0, blk=0):
                room(r, it, step)
                src = w_mod[lb, 2 * j * P:2 * (j + 1) * P, :].rearrange("(k p) n -> p k n", p=P)
                sp.dma_start(raw[:, r % RING, :, :], src[:, :, bass.ds(blk * SEQ, SEQ)])\
                  .then_inc(raw_loaded[r % RING], 16)

            def load_x(half):
                k = slice(4 * half, 4 * half + 4)
                sp.dma_start(xr[:, k, :], xT.rearrange("(k p) t -> p k t", p=P)[:, k, :]).then_inc(x_loaded, 16)

            for i in range(MOD_FRONT):
                if i == MOD_FRONT - 1:
                    load_x(1)
                if i == MOD_FRONT // 2:
                    load_x(0)
                    load_w(0, 0)
                    load_w(0, 1)
                for j in range(4):
                    load_mod(mod_front(i, j), 0, j, blk=mod_block(i)[1])
            for l in range(LAYERS):
                if l:
                    sp.wait_ge(wdt_ready, l)
                sp.dma_start(wdt_raw[:, :, :], wdt[l]).then_inc(wdt_loaded, 16)
                for u in range(U_MLP):
                    if l or u >= 2:
                        load_w(l, u)
                    if l == 0:
                        for i, j, r in mod_behind(u):
                            load_mod(r, 0, j, blk=i)
                    if u == 4:
                        if l:
                            sp.wait_ge(bank_done, 4 * NG * l)
                        sp.dma_start(cosT[:, :], rope[0]).then_inc(rope_loaded, 16)
                        sp.dma_start(sinT[:, :], rope[1]).then_inc(rope_loaded, 16)
                    if u == 24:
                        sp.wait_ge(rope_done, 8 * (l + 1))
                        sp.dma_start(ssdw_row[:, :], ssdw[l]).then_inc(ssdw_loaded, 16)
                for j in range(4):
                    load_gu(l, j)
                with sp.Fori(1, MLP_G) as g:
                    for j in range(4):
                        load_gu(l, j, g)
                        if l == 0:
                            load_mod(raw_at(0, U_MLP + j, g) + 1, 1, j, it=g, step=8, blk=g - 1)
                for u in range(U_DOWN, UNITS):
                    load_w(l, u)
                    if l == 0:
                        for row, j, r in mod_behind_down(u):
                            lb, blk = mod_block(10 + row)
                            load_mod(r, lb, j, blk=blk)
            for k in range(KD):
                sp.wait_ge(out_tile, k + 1)
                sp.dma_start(outT[k * P:(k + 1) * P, :], xr[:, k, :]).then_inc(out_stored, 16)
            sp.wait_ge(out_stored, 16 * KD)

        @block.tensor
        def _(pe):
            def slab(l, u, act_hi, act_lo, ready, weights_move=False, bank_free=None, it=0, slabs=1):
                g, j, n = group_of(u)
                step = raw_step(l)
                k0 = 4 if g in (G_OUT + 2, G_OUT + 3) else 0
                pe.wait_ge(slab_split, raw_at(l, u + slabs - 1, it) + 1 + step * it)

                def trio(kg, m, first):
                    k, kk, c = kg + k0, kg % 2, (UNITS * l + u + kg // 2 - j) % RING
                    if first:
                        ready[0](k)
                    if kg == 0 and bank_free:
                        bank_free(m)
                    cols = slice(m * P, (m + 1) * P)
                    if weights_move:
                        pairs = [(act_hi[:, k, cols], w_hi[:, c, kk, :]), (act_hi[:, k, cols], w_lo[:, c, kk, :]),
                                 (act_lo[:, k, cols], w_hi[:, c, kk, :])]
                    else:
                        pairs = [(w_hi[:, c, kk, cols], act_hi[:, k, :]), (w_lo[:, c, kk, cols], act_hi[:, k, :]),
                                 (w_hi[:, c, kk, cols], act_lo[:, k, :])]
                    for i, (stat, mov) in enumerate(pairs):
                        if first and i == 2:
                            ready[1](k)
                        mmi = pe.matmul(ps[:, m, :], stat, mov, start=(kg == 0 and i == 0),
                                        stop=(kg == 2 * n - 1 and i == 2))
                    if kg == 2 * n - 1:
                        mmi.then_inc(bank_done, 1)
                    elif kg % 2 and m == 3:
                        mmi.then_inc(slab_used, 1)

                if slabs == 1:
                    for kk in range(2):
                        for m in range(4):
                            trio(2 * j + kk, m, m == 0)
                            if l == 0 and m == 3 and kk == 0 and u == U_MLP + 2:
                                mod_clear() if isinstance(it, int) else mod_gather(it - 1)
                            if m % 2:
                                between_matmuls(l, u, 2 * kk + m // 2)
                else:
                    for m in range(4):
                        if m == 1 and l == 0 and u == U_DOWN + DOWN_SLABS - 2:
                            mod_turn()
                        for kg in range(2 * j, 2 * (j + slabs)):
                            trio(kg, m, m == 0)
                            if kg % 2:
                                between_matmuls(l, u, 2 * m + (kg // 2) % 2)

            def mod_clear():
                pe.matmul(ps[0:MOD_ROWS, 7, :], sel[:, MOD_ROWS:2 * MOD_ROWS], cst[:, :], start=True, stop=False,
                          skip_group_check=True)

            def mod_gather(row):
                pe.wait_ge(mod_parts, 2 * row + 2)
                for part in range(2):
                    last = pe.matmul(ps[0:MOD_ROWS, 7, :], sel_row[:, :], mparts[:, part, :], start=False,
                                     stop=(isinstance(row, int) and row == MOD_ROWS - 1 and part == 1),
                                     skip_group_check=True)
                last.then_inc(mod_mm, 1)

            def mod_turn():
                pe.wait_ge(mod_rows, 1)
                for j in range(4):
                    last = pe.transpose(ps[:, 7, j * MOD_ROWS:(j + 1) * MOD_ROWS], modT[0:MOD_ROWS, j * P:(j + 1) * P],
                                        ident[0:MOD_ROWS, 0:MOD_ROWS])
                last.then_inc(mod_turned, 1)

            def mod_reduce(i):
                if i < MOD_FRONT:
                    r = mod_front(i, 3)
                else:
                    r = MOD_LAST[i][1]
                pe.wait_ge(slab_split, r + 1)
                for j in range(4):
                    last = pe.matmul(ps[:, mod_bank(i), j:j + 1], macc[:, mod_slot(i), j * P:(j + 1) * P], ones[:, 0:1],
                                     start=True, stop=True)
                last.then_inc(mod_mm, 1)

            def dt_project(l):
                pe.wait_ge(wdt_ready, l + 1)
                for k in range(KD):
                    for i, (w, a) in enumerate([(wdt_hi, h_hi), (wdt_lo, h_hi), (wdt_hi, h_lo)]):
                        last = pe.matmul(ps[0:HEADS, 7, :], w[:, k, :], a[:, k, :], start=(k == 0 and i == 0),
                                         stop=(k == KD - 1 and i == 2))
                last.then_inc(dt_mm, 1)

            def dt_turn(l, _):
                pe.wait_ge(dt_copied, l + 1)
                for c in range(CH):
                    last = pe.transpose(ps[:, 7, c * HEADS:(c + 1) * HEADS], dtF[0:HEADS, c * P:(c + 1) * P],
                                        ident[0:HEADS, 0:HEADS])
                last.then_inc(dt_turned, 1)

            def cumsum(l):
                pe.wait_ge(a_ready, l + 1)
                pe.matmul(ps[:, 7, 32:64], tri, dts[:, DAA, :], start=True, stop=True)
                pe.matmul(ps[:, 7, 64:96], ones, dts[:, DAA, :], start=True, stop=True).then_inc(cs_mm, 1)

            def ssd_first(l, c):
                if c == 0:
                    pe.wait_ge(conv_out, 8 * (l + 1))
                    pe.wait_ge(cs_ready, l + 1)
                    pe.wait_ge(cs_exp, l + 1)
                else:
                    pe.wait_ge(ssd_d2, CH * l + c)
                tok = slice(c * P, (c + 1) * P)
                for j in range(4):
                    pe.transpose(ps[:, 6, j * P:(j + 1) * P], xsF[:, j, tok], ident)
                for g in range(2):
                    pe.transpose(ps[:, 7, 256 + g * P:256 + (g + 1) * P], bcF[:, g, tok], ident)
                for g in range(2):
                    pe.matmul(ps[:, 7, g * P:(g + 1) * P], bcF[:, g, tok], bcF[:, 2 + g, tok], start=True, stop=True)
                for b in range(2):
                    bank = ps[:, 4 + b, :].rearrange("p (e t) -> p e t", e=4)
                    pe.matmul(bank, identb[:, :], maskb[:, :].unsqueeze(1).to_broadcast([P, 4, P]), start=True, stop=False,
                              skip_group_check=True)
                    for e in range(4):
                        col = c * HEADS + 4 * b + e
                        last = pe.matmul(bank[:, e, :], dts[:, DAA, col:col + 1].to_broadcast([P, P]), tri,
                                         start=False, stop=(e == 3), skip_group_check=True)
                last.then_inc(ssd_p1, 1)

            def ssd_second(l, c):
                pe.wait_ge(m_ready, CH * l + c + 1)
                pe.wait_ge(xd_ready, CH * l + c + 1)
                tok = slice(c * P, (c + 1) * P)
                for hh in range(HEADS):
                    pd = slice(hh * HDIM, (hh + 1) * HDIM)
                    pe.matmul(ps[:, 4, pd], mm[:, hh, :], xdt[:, pd], start=True, stop=True)
                if c > 0:
                    for g in range(2):
                        gd = slice(g * 256, (g + 1) * 256)
                        pe.matmul(ps[:, 5, gd], bcF[:, 2 + g, tok], state[:, gd], start=True, stop=True)
                pe.wait_ge(tok_copied, CH * l + c + 1)
                for g in range(2):
                    gd = slice(g * 256, (g + 1) * 256)
                    last = pe.matmul(ps[:, 6, gd], b_tok[:, c, g * P:(g + 1) * P], xdec[:, gd], start=True, stop=True)
                last.then_inc(ssd_p2, 1)

            def qk(l, t):
                i, h = divmod(t, AH)
                if t < AH:
                    pe.wait_ge(rope_done, 8 * l + AH + h + 1)
                    pe.wait_ge(kpad_ready, AH * l + h + 1)
                if t == 0:
                    pe.wait_ge(ssd_d2, CH * (l + 1))
                else:
                    pe.wait_ge(exp_done, 16 * l + t)
                n = (i + 1) * P
                for m in range(2):
                    pe.matmul(ps[:, 4 + m, 0:n], q[:, h, i * P:(i + 1) * P], kpad[:, m, h, 0:n], start=True, stop=False,
                              skip_group_check=True)
                    last = pe.matmul(ps[:, 4 + m, i * P:n], maskb[:, :], identb[:, :], start=False, stop=True,
                                     skip_group_check=True)
                last.then_inc(qk_done, 1)

            def turn_w(l, t):
                pe.wait_ge(w_ready, 16 * l + t + 1)
                if t:
                    pe.wait_ge(wt_ready, 16 * l + t)
                if t >= 5 and t % 4 == 1:
                    pe.wait_ge(yo_hi, CH * l + (t - 1) // 4)
                    pe.wait_ge(yo_ready, CH * l + (t - 1) // 4)
                for j in range(t // AH + 1):
                    last = pe.transpose(ps[:, 6, j * P:(j + 1) * P], prob[:, t % 2, 0, j * P:(j + 1) * P], ident)
                last.then_inc(wt_mm, 1)

            def pv(l, t):
                i, h = divmod(t, AH)
                pe.wait_ge(wt_ready, 16 * l + t + 1)
                if t == 0:
                    pe.wait_ge(v_ready, CH * (l + 1))
                if h == 0 and i:
                    pe.wait_ge(o_copied, CH * l + i)
                    pe.wait_ge(o_sq, CH * l + i)
                for j in range(i + 1):
                    last = pe.matmul(ps[:, 7, h * P:(h + 1) * P], wT[:, t % 2, j, :], v[:, j, h * P:(h + 1) * P],
                                     start=(j == 0), stop=(j == i))
                last.then_inc(pv_done, 1)

            def turn_o(l, i):
                pe.wait_ge(o_scaled, CH * l + i + 1)
                pe.wait_ge(wt_ready, 16 * l + min(4 * i + 5, 16))
                for h in range(AH):
                    last = pe.transpose(ps[:, 6, h * P:(h + 1) * P], o_tok[:, h * P:(h + 1) * P], ident)
                last.then_inc(tro_mm, 1)

            def step_a(l, t):
                if t < 16:
                    qk(l, t)
                if 1 <= t <= 16:
                    turn_w(l, t - 1)

            def step_b(l, t):
                if t >= 5 and t % 4 == 1:
                    turn_o(l, (t - 5) // 4)
                if 1 <= t <= 16:
                    pv(l, t - 1)

            def turn_ys(l):
                for c in range(CH):
                    pe.wait_ge(ys_scaled, CH * l + c + 1)
                    pe.wait_ge(ys_scaled_act, CH * l + c + 1)
                    for j in range(4):
                        last = pe.transpose(ps[:, c, j * P:(j + 1) * P], yt[:, c, j * P:(j + 1) * P], ident)
                    last.then_inc(trs_mm, 1)

            def ln_sums(n):
                for i, (src, done) in enumerate(((s1, ln_s1), (s2, ln_s2))):
                    pe.wait_ge(done, (KD - 1) * (n + 1))
                    for c in range(CH):
                        last = pe.matmul(ps[:, 4, 4 * i + c:4 * i + c + 1], src[:, c * P:(c + 1) * P], meancol[:, :],
                                         start=True, stop=True)
                last.then_inc(ln_stats, 1)

            def ln_spread(n):
                for i in range(2):
                    pe.wait_ge(ln_diag, 2 * n + i + 1)
                    pe.matmul(ps[:, 5 + i, :], ones, diag[:, i, :, :], start=True, stop=True).then_inc(ln_rows, 1)

            def between_matmuls(l, u, quarter):
                for what, t in BETWEEN.get(4 * u + quarter, []) if u < U_MLP else []:
                    {"dt": dt_turn, "first": ssd_first, "second": ssd_second, "step_a": step_a, "step_b": step_b,
                     "turn_w": turn_w, "z": lambda l, c: None}[what](l, t)

            pe.wait_ge(consts_ready, 1)
            mod_reduce(0)
            mod_reduce(1)
            for l in range(LAYERS):
                def tiles(hi_sem, lo_sem, before):
                    return (lambda k: pe.wait_ge(hi_sem, before + k + 1), lambda k: pe.wait_ge(lo_sem, before + k + 1))

                none = (lambda k: None, lambda k: None)
                h_tile = tiles(h_hi_ready, h_ready, 16 * l)

                def y_tile(k):
                    if k == 0:
                        pe.wait_ge(ys_ready, CH * (l + 1))
                    if k == 4:
                        pe.wait_ge(yo_ready, CH * (l + 1))

                frees = {
                    1: lambda m: pe.wait_ge(conv_raw, 8 * l + m + 1),
                    2: lambda m: pe.wait_ge(conv_raw, 8 * l + 4 + m + 1),
                    3: lambda m: pe.wait_ge(qk_raw, 8 * l + m + 1),
                    4: lambda m: pe.wait_ge(qk_raw, 8 * l + 4 + m + 1),
                    5: lambda m: pe.wait_ge(v_ready, CH * l + m + 1),
                    7: lambda m: pe.wait_ge(out_half, 8 * l + m + 1),
                    8: lambda m: pe.wait_ge(out_half, 8 * l + 4 + m + 1),
                    9: lambda m: pe.wait_ge(ln_r, 16 * l + m + 1),
                }
                for u in range(U_MLP):
                    g = group_of(u)[0]
                    if u == U_OUT:
                        step_b(l, AHEAD_OF_OUT - 1)
                        qk(l, AHEAD_OF_OUT)
                        turn_ys(l)
                    pair = u in PAIRS
                    if u == U_OUT + 4:
                        step_b(l, STEP_COUNT - 1)
                    if l == 0 and u == 2:
                        mod_reduce(2)
                        mod_reduce(3)
                    if l == 0:
                        for i in MOD_LAST:
                            if u == mod_reduced_at(i):
                                mod_reduce(i)
                    if u - 1 in PAIRS:
                        continue
                    if u < U_OUT:
                        slab(l, u, h_hi, h_lo, h_tile if g == 0 else none, weights_move=GROUPS[g] in "vz",
                             bank_free=frees.get(g), slabs=2 if pair else 1)
                    else:
                        slab(l, u, y_hi, y_lo, (y_tile, lambda k: None), bank_free=frees.get(g), slabs=2 if pair else 1)
                    if u == 3:
                        dt_project(l)
                    if u == 6:
                        cumsum(l)
                ln_sums(2 * l)
                ln_spread(2 * l)

                h2_tile = tiles(h_hi_ready, h_ready, 16 * l + 8)

                def mlp_group(g, first):
                    def free(m):
                        sm = mlp_a if m < 2 else mlp_f
                        pe.wait_ge(sm, FT * l + m % 2 + 1 + 2 * (g - 1))

                    for j in range(4):
                        slab(l, U_MLP + j, h_hi, h_lo, h2_tile if first else none, bank_free=None if first else free, it=g)

                mlp_group(0, True)
                with pe.Fori(1, MLP_G) as g:
                    mlp_group(g, False)

                f_tile = tiles(f_hi_ready, f_ready, FT * l)

                for u in range(U_DOWN, UNITS):
                    i = u - U_DOWN
                    if l == 0 and i in MOD_GATHER_AT:
                        mod_gather(MLP_G - 1 + MOD_GATHER_AT.index(i))
                    if i < DOWN_SLABS:
                        free = lambda m: pe.wait_ge(mlp_a if m < 2 else mlp_f, FT * (l + 1) - 1 + m % 2)
                    else:
                        free = lambda m: pe.wait_ge(ln_r, 16 * l + 8 + m + 1)
                    if i % DOWN_SLABS != DOWN_SLABS - 1:
                        slab(l, u, f_hi, f_lo, f_tile, bank_free=free, slabs=2 if i % DOWN_SLABS == DOWN_SLABS - 2 else 1)
                ln_sums(2 * l + 1)
                ln_spread(2 * l + 1)

        @block.scalar
        def _(act):
            chained = [0]

            def chain(ins):
                chained[0] += 1
                ins.then_inc(act_chain, 1)
                act.wait_ge(act_chain, chained[0])

            def hi(l, u, it=0):
                if u >= UNITS and l == LAYERS - 1:
                    return
                s = UNITS * l + u
                r = raw_at(l, u, it)
                wait_loaded(act, r, it, raw_step(l))
                wait_used(act, s - RING, it)
                act.activation(w_hi[:, s % RING, :, :], raw[:, r % RING, :, :], ACT.Copy).then_inc(hi_ready, 1)

            def affine(e, k):
                n = e - 1
                if n < 0:
                    if k % 4 == 0:
                        act.wait_ge(x_loaded, 16 * (k // 4 + 1))
                else:
                    act.wait_ge(ln_t, 8 * n + k + 1)
                if k == 0:
                    act.wait_ge(vec_ready, e + 2 if e else 1)
                if e == 0 and k == 4:
                    act.wait_ge(vec_ready, 2)
                if k >= 2:
                    act.wait_ge(h_ready, 8 * e + k - 1)
                act.activation(h32[:, k % 2, :], xr[:, k, :], ACT.Identity, bias=vecs[:, VB, k:k + 1],
                               scale=vecs[:, VG, k:k + 1]).then_inc(h32_ready, 1)
                act.wait_ge(h32_ready, 8 * e + k + 1)
                act.activation(h_hi[:, k, :], h32[:, k % 2, :], ACT.Copy).then_inc(h_hi_ready, 1)

            def conv_evac(l, t):
                act.wait_ge(bank_done, 4 * (NG * l + t // 4) + t % 4 + 1)
                act.activation(conv_in[:, t, 3:SEQ + 3], ps[:, t % 4, :], ACT.Copy)
                if t == 0:
                    act.wait_ge(vec_ready, 2)
                dst = xsF[:, t, :] if t < 4 else bcF[:, t - 4, :]
                act.activation(dst, ps[:, t % 4, :], ACT.Identity, bias=prm[:, l, C_CONVB + t:C_CONVB + t + 1],
                               scale=prm[:, l, C_CONVW + 4 * t + 3:C_CONVW + 4 * t + 4]).then_inc(conv_raw, 1)

            def conv_tanhs(l, t):
                act.wait_ge(conv_lin, 8 * l + t + 1)
                if t >= 2:
                    act.wait_ge(conv_out, 8 * l + t - 1)
                src = xsF[:, t, :] if t < 4 else bcF[:, t - 4, :]
                act.activation(conv_th[:, t % 2, :], src, ACT.Tanh).then_inc(conv_tanh, 1)

            def qk_evac(l, t):
                act.wait_ge(bank_done, 4 * (NG * l + 2 + t // 4) + t % 4 + 1)
                dst = q[:, t, :] if t < 4 else kpad[:, 0, t - 4, :]
                act.activation(dst, ps[:, t % 4, :], ACT.Copy).then_inc(qk_raw, 1)

            def z_tanhs(l, c):
                act.wait_ge(bank_done, 4 * (NG * l + 5) + c + 1)
                act.activation(zs[:, c, :], ps[:, c, :], ACT.Tanh, scale=0.5).then_inc(z_tanh, 1)

            def gate_squares(l, c):
                act.wait_ge(gated, CH * l + c + 1)
                for g in range(2):
                    last = act.activation(zs[:, c, g * 256:(g + 1) * 256], yt[:, c, g * 256:(g + 1) * 256], ACT.Square,
                                          accum_out=nrs[:, 5, 2 * c + g:2 * c + g + 1])
                last.then_inc(gate_sq, 1)

            def ssd_act(l, c):
                act.wait_ge(ssd_p1, CH * l + c + 1)
                act.activation(xs_tok[:, c, :], ps[:, 6, :], ACT.Copy)
                act.activation(b_tok[:, c, :], ps[:, 7, 256:512], ACT.Copy).then_inc(tok_copied, 1)
                if c:
                    act.wait_ge(m_ready, CH * l + c)
                for hh in range(HEADS):
                    col = c * HEADS + hh
                    last = act.activation(lm[:, hh, :], ps[:, 4 + hh // 4, (hh % 4) * P:(hh % 4 + 1) * P], ACT.Exp,
                                          bias=dts[:, DN, col:col + 1])
                last.then_inc(l_ready, 1)

            def exps(l, t):
                i, h = divmod(t, AH)
                act.wait_ge(nb_ready, 16 * l + t + 1)
                if t >= 2:
                    act.wait_ge(wt_mm, 16 * l + t - 1)
                n = (i + 1) * P
                for m in range(2):
                    last = act.activation(prob[:, t % 2, m, 0:n], ps[:, 4 + m, 0:n], ACT.Exp,
                                          bias=att[:, 0, 2 * h + m:2 * h + m + 1], scale=0.125,
                                          accum_out=att[:, 1, 2 * h + m:2 * h + m + 1])
                last.then_inc(exp_done, 1)

            def wt_copy(l, t):
                act.wait_ge(wt_mm, 16 * l + t + 1)
                if t >= 2:
                    act.wait_ge(pv_done, 16 * l + t - 1)
                n = t // AH + 1
                act.activation(wT[:, t % 2, 0:n, :], ps[:, 6, 0:n * P].rearrange("p (j t) -> p j t", j=n), ACT.Copy)\
                   .then_inc(wt_ready, 1)

            def o_squares(l, i):
                act.wait_ge(pv_done, 16 * l + 4 * i + 4)
                for h in range(AH):
                    last = act.activation(junk[:, h * P:(h + 1) * P], ps[:, 7, h * P:(h + 1) * P], ACT.Square,
                                          accum_out=ssq[:, h:h + 1])
                last.then_inc(o_sq, 1)

            def root(v_sem, value, y_sem, n, nrm=nrm):
                act.wait_ge(v_sem, value)
                chain(act.activation(nrm[:, 1, 0:n], nrm[:, 0, 0:n], ACT.Ln))
                act.activation(nrm[:, 2, 0:n], nrm[:, 1, 0:n], ACT.Exp, scale=-0.5).then_inc(y_sem, 1)

            def yo_high(l, i):
                act.wait_ge(tro_mm, CH * l + i + 1)
                act.activation(y_hi[:, 4:8, i * P:(i + 1) * P], ps[:, 6, :].rearrange("p (h t) -> p h t", h=4),
                               ACT.Copy, scale=awc[:, l:l + 1]).then_inc(yo_hi, 1)

            def o_root(l, t):
                root(att_v, CH * l + (t - 4) // 4 + 1, att_y0, 4)

            def step(l, t):
                if 1 <= t <= 16:
                    wt_copy(l, t - 1)
                if t < 16:
                    exps(l, t)
                if t >= 4 and t % 4 == 0:
                    o_squares(l, (t - 4) // 4)
                    o_root(l, t)
                if t >= 5 and t % 4 == 1:
                    yo_high(l, (t - 5) // 4)

            def ahead_of_out(l):
                t = AHEAD_OF_OUT - 1
                z_tanhs(l, CH - 1)
                wt_copy(l, t - 1)
                gate_squares(l, CH - 2)
                gate_squares(l, CH - 1)
                act.preload_act_table_set("natural_log_exp_and_others")
                root(ssd_v, l + 1, ssd_y0, 8, nrs)
                exps(l, t)
                act.wait_ge(ssd_rstd, l + 1)
                for c in range(CH):
                    act.wait_ge(ys_weighted, CH * l + c + 1)
                    act.activation(yt[:, c, 256:512], yt[:, c, 256:512], ACT.Copy, scale=nrs[:, 3, 2 * c + 1:2 * c + 2])\
                       .then_inc(ys_scaled_act, 1)
                o_squares(l, (t - 4) // 4)
                for c in range(CH):
                    act.wait_ge(trs_mm, CH * l + c + 1)
                    act.activation(y_hi[:, 0:4, c * P:(c + 1) * P], ps[:, c, :].rearrange("p (h t) -> p h t", h=4),
                                   ACT.Copy).then_inc(ys_hi, 1)
                o_root(l, t)
                hi(l, U_OUT + 2)

            def squares(n, m):
                act.wait_ge(ln_r, 8 * n + m + 1)
                if m >= 2:
                    act.wait_ge(ln_s2, 7 * n + max(m - 2, 1))
                act.activation(sq[:, m % 2, :], xr[:, m, :], ACT.Square).then_inc(ln_sq, 1)

            def ln_head(n):
                root(ln_v, n + 1, ln_y0, 4)

            def mlp_evac(l, it):
                for j in range(2):
                    act.wait_ge(bank_done, 4 * (NG * l + G_MLP) + j + 1 + 4 * it)
                    act.activation(sq[:, j, :], ps[:, j, :], ACT.Tanh, scale=0.5).then_inc(mlp_th, 1)
                for j in range(2):
                    act.wait_ge(mlp_f, FT * l + j + 1 + 2 * it)
                    act.activation(f_hi[:, bass.ds(2 * it + j, 1), :], h32[:, j:j + 1, :], ACT.Copy).then_inc(f_hi_ready, 1)

            act.dma_start(cvec, ccol).then_inc(c_loaded, 16)
            act.dma_start(cst[:, :], consts).then_inc(small_loaded, 16)
            act.dma_start(prm[:, :, :], par).then_inc(small_loaded, 16)
            act.dma_start(lamt[:, :, :, :], lamqk).then_inc(small_loaded, 16)
            act.preload_act_table_set("exp_and_others")
            act.wait_ge(cond_half, 1)
            act.activation(cond[:, 2, :], cond[:, 1, :], ACT.Tanh).then_inc(cond_tanh, 1)
            act.wait_ge(small_loaded, 48)
            for l in range(LAYERS):
                last = act.activation(expa[:, l, :], prm[:, l, C_ALOG:C_ALOG + HEADS], ACT.Exp)
            act.wait_ge(lam_sums, 1)
            act.activation(lam[:, :, 2:4], lam[:, :, 0:2], ACT.Exp).then_inc(lam_exp, 1)
            for k in range(KD):
                if k % 2 == 0 and k < 6:
                    hi(0, k // 2)
                affine(0, k)
            for l in range(LAYERS):
                for u in range(U_MLP):
                    if u in (4, 8):
                        for t in range(4):
                            conv_evac(l, u - 4 + t)
                    if u in (12, 16):
                        for t in range(4):
                            qk_evac(l, u - 12 + t)
                    if u == 19:
                        act.preload_act_table_set("natural_log_exp_and_others")
                    if u == 29:
                        for m in range(4):
                            squares(2 * l, m)
                    if u < 3 and l:
                        affine(2 * l, 2 * u + 2)
                        affine(2 * l, 2 * u + 3)
                    if u not in (U_OUT - 1, U_MLP - 1):
                        hi(l, u + 3)
                    if u == V_PAIR + 1:
                        for c in range(CH):
                            act.wait_ge(bank_done, 4 * (NG * l + 4) + c + 1)
                            act.activation(v[:, c, :], ps[:, c, :], ACT.Copy).then_inc(v_ready, 1)
                    if u == 0:
                        act.wait_ge(wdt_loaded, 16 * (l + 1))
                        act.activation(wdt_hi[:, :, :], wdt_raw[:, :, :], ACT.Copy).then_inc(wdt_hi_ready, 1)
                    if u == 4:
                        act.wait_ge(dt_mm, l + 1)
                        act.activation(dtF[0:HEADS, :], ps[0:HEADS, 7, :], ACT.Copy).then_inc(dt_copied, 1)
                        act.preload_act_table_set("natural_log_exp_and_others")
                        act.wait_ge(dt_abs, l + 1)
                        act.activation(dts[:, DE, :], dts[:, DA, :], ACT.Exp, scale=-1.0).then_inc(dt_exp, 1)
                        act.wait_ge(dt_w, l + 1)
                        act.activation(dts[:, DL, :], dts[:, DW, :], ACT.Ln).then_inc(dt_ln, 1)
                        act.preload_act_table_set("exp_and_others")
                    if 5 <= u <= 12:
                        conv_tanhs(l, u - 5)
                    if u == 8:
                        act.wait_ge(cs_ready, l + 1)
                        act.activation(dts[:, DEA, :], dts[:, DCS, :], ACT.Exp)
                        act.activation(dts[:, DDEC, :], dts[:, DDEC, :], ACT.Exp)
                        act.activation(dts[:, DTOT, :], ps[:, 7, 64:96], ACT.Exp).then_inc(cs_exp, 1)
                    for what, t in between(u):
                        if (what, t) == ("step_a", AHEAD_OF_OUT - 1):
                            ahead_of_out(l)
                        elif what == "first":
                            ssd_act(l, t)
                        elif what == "step_a":
                            step(l, t)
                        elif what == "turn_w":
                            step(l, t + 1)
                        elif what == "z" and t < CH - 1:
                            z_tanhs(l, t)
                            if t:
                                gate_squares(l, t - 1)
                    if u == Z_PAIR - 1:
                        act.preload_act_table_set("exp_and_others")
                    if u == U_OUT + 3:
                        step(l, STEP_COUNT - 1)
                for m in range(4, 8):
                    squares(2 * l, m)
                hi(l, U_MLP + 2)
                ln_head(2 * l)
                act.preload_act_table_set("exp_and_others")
                affine(2 * l + 1, 0)
                affine(2 * l + 1, 1)
                for j in range(4):
                    if j < 3:
                        affine(2 * l + 1, 2 * j + 2)
                        affine(2 * l + 1, 2 * j + 3)
                    hi(l, U_MLP + j + 3)
                with act.Fori(1, MLP_G) as g:
                    mlp_evac(l, g - 1)
                    for j in range(4):
                        hi(l, U_MLP + j + 3, it=g)
                for u in range(U_DOWN, UNITS):
                    if u == U_DOWN:
                        mlp_evac(l, MLP_G - 1)
                        act.preload_act_table_set("natural_log_exp_and_others")
                    if u == U_DOWN + DOWN_SLABS - 1:
                        for m in range(4):
                            squares(2 * l + 1, m)
                    if u < UNITS - 1:
                        hi(l, u + 3)
                for m in range(4, 8):
                    squares(2 * l + 1, m)
                hi(l, UNITS - 1 + 3)
                ln_head(2 * l + 1)
                if l + 1 < LAYERS:
                    act.preload_act_table_set("exp_and_others")
                    affine(2 * l + 2, 0)
                    affine(2 * l + 2, 1)
                else:
                    for k in range(KD):
                        act.wait_ge(ln_t, 8 * (2 * l + 1) + k + 1)
                        act.activation(xr[:, k, :], xr[:, k, :], ACT.Identity, bias=prm[:, l, C_LN2B + k:C_LN2B + k + 1],
                                       scale=prm[:, l, C_LN2G + k:C_LN2G + k + 1]).then_inc(out_tile, 1)

        @block.gpsimd
        def _(pool):
            def rotate(l, t):
                src = q[:, t, :] if t < 4 else kpad[:, 0, t - 4, :]
                pool.wait_ge(qk_raw, 8 * l + t + 1)
                if t >= 2:
                    pool.wait_ge(rope_done, 8 * l + t - 1)
                for b in range(4):
                    o = b ^ 1
                    pool.dma_start(rot[32 * b:32 * b + 32, t % 2, :], src[32 * o:32 * o + 32, :])\
                        .then_inc(rot_dma[t % 2], 16)

            def pad(l, h):
                pool.wait_ge(rope_done, 8 * l + 4 + h + 1)
                pool.memset(kpad[64:128, 0, h, :], 0.0).then_inc(pad_half, 1)
                pool.wait_ge(pad_half, AH * l + h + 1)
                pool.memset(kpad[0:64, 1, h, :], 0.0).then_inc(kpad_ready, 1)
                pool.wait_ge(kpad_ready, AH * l + h + 1)

            def skip_term(l, c):
                pool.wait_ge(tok_copied, CH * l + c + 1)
                d = prm[:, l, C_DSKIP:C_DSKIP + HEADS].unsqueeze(2).to_broadcast([P, HEADS, HDIM])
                pool.tensor_tensor(yt[:, c, :].rearrange("p (h d) -> p h d", h=HEADS),
                                   xs_tok[:, c, :].rearrange("p (h d) -> p h d", h=HEADS), d, ALU.mult)\
                    .then_inc(skip_ready, 1)
                pool.wait_ge(skip_ready, CH * l + c + 1)

            def weigh(l, c):
                if c == 0:
                    pool.wait_ge(ssdw_loaded, 16 * (l + 1))
                pool.wait_ge(gate_sq, CH * l + c + 1)
                pool.tensor_tensor(yt[:, c, :], yt[:, c, :], ssdw_row[:, :], ALU.mult).then_inc(ys_weighted, 1)

            def sum_squares(n, m):
                pool.wait_ge(ln_sq, 8 * n + m + 1)
                if m == 1:
                    pool.tensor_tensor(s2[:, :], sq[:, 0, :], sq[:, 1, :], ALU.add).then_inc(ln_s2, 1)
                elif m > 1:
                    pool.wait_ge(ln_s2, 7 * n + m - 1)
                    pool.tensor_tensor(s2[:, :], s2[:, :], sq[:, m % 2, :], ALU.add).then_inc(ln_s2, 1)

            def next_residual(e, k):
                pool.wait_ge(h_hi_ready, 8 * e + k + 1)
                if e == 0:
                    pool.tensor_scalar(xr[:, k, :], xr[:, k, :], ALPHA, 0.0, ALU.mult, ALU.add).then_inc(xa_ready, 1)
                else:
                    pool.tensor_scalar(xr[:, k, :], xr[:, k, :], vecs[:, VAG, k:k + 1], vecs[:, VAB, k:k + 1],
                                       ALU.mult, ALU.add).then_inc(xa_ready, 1)

            for k in range(KD):
                next_residual(0, k)
            for l in range(LAYERS):
                pool.wait_ge(h_ready, 8 * (2 * l + 1))
                pool.memset(conv_in[:, :, 0:3], 0.0).then_inc(pads_ready, 1)
                for t in range(3):
                    rotate(l, t)
                skip_term(l, 0)
                rotate(l, 3)
                skip_term(l, 1)
                rotate(l, 4)
                rotate(l, 5)
                skip_term(l, 2)
                rotate(l, 6)
                pad(l, 0)
                skip_term(l, 3)
                rotate(l, 7)
                for h in range(1, AH):
                    pad(l, h)
                for c in range(CH):
                    weigh(l, c)
                for m in range(KD - 1):
                    sum_squares(2 * l, m)
                for k in range(KD):
                    next_residual(2 * l + 1, k)
                for m in range(KD - 1):
                    sum_squares(2 * l + 1, m)
                if l + 1 < LAYERS:
                    for k in range(KD):
                        next_residual(2 * l + 2, k)

        @block.vector
        def _(dve):
            chained = [0]

            def chain(ins, loop=0):
                chained[0] += 1
                ins.then_inc(dve_chain, 1)
                dve.wait_ge(dve_chain, chained[0] + loop)

            def split(l, u, it=0):
                if u >= UNITS and l == LAYERS - 1:
                    return
                s = UNITS * l + u
                r = raw_at(l, u, it)
                dve.wait_ge(hi_ready, s + 1 + 4 * it)
                dve.tensor_tensor(w_lo[:, s % RING, :, :], raw[:, r % RING, :, :], w_hi[:, s % RING, :, :].bitcast(F32),
                                  ALU.subtract).then_inc(slab_split, 1)

            def fold_quarter(acc, r, j, it=0, loop=0):
                wait_loaded(dve, r, it, 8)
                if j == 0:
                    chain(dve.tensor_scalar(acc, raw[:, r % RING, 0, :], cvec[:, 0:1], None, ALU.mult), loop)
                else:
                    dve.wait_ge(slab_split, r + 8 * it)
                    chain(dve.scalar_tensor_tensor(acc, raw[:, r % RING, 0, :], cvec[:, 2 * j:2 * j + 1], acc,
                                                   ALU.mult, ALU.add), loop)
                dve.scalar_tensor_tensor(acc, raw[:, r % RING, 1, :], cvec[:, 2 * j + 1:2 * j + 2], acc,
                                         ALU.mult, ALU.add).then_inc(slab_split, 1)

            def fold_mod(i, j, r):
                if j == 0 and i >= 2:
                    dve.wait_ge(mod_mm, i - 1)
                fold_quarter(macc[:, mod_slot(i), :], r, j)

            def fold_row(row, j, r, it=0, loop=0):
                acc = macc[:, 0, :]
                if j == 0:
                    if isinstance(row, int) and row == 0:
                        dve.wait_ge(mod_mm, 9)
                    else:
                        dve.wait_ge(mod_parts, 2 * row)
                fold_quarter(acc, r, j, it, loop)
                if j == 3:
                    dve.wait_ge(slab_split, r + 1 + 8 * it)
                    dve.wait_ge(mod_mm, 10 + row)
                    chain(dve.tensor_copy(mparts[:, 0, :], acc), loop)
                    dve.tensor_tensor(mparts[:, 1, :], acc, mparts[:, 0, :].bitcast(F32), ALU.subtract)\
                       .then_inc(mod_parts, 1)
                    dve.tensor_copy(sel_row[:, :], sel[:, bass.ds(MOD_ROWS - 1 - row, MOD_ROWS)]).then_inc(mod_parts, 1)

            def mod_rows_out():
                dve.wait_ge(mod_mm, 24)
                dve.tensor_copy(modT[0:MOD_ROWS, :], ps[0:MOD_ROWS, 7, :]).then_inc(mod_rows, 1)

            def mod_columns():
                dve.wait_ge(mod_turned, 1)
                turned = ps[:, 7, 0:4 * MOD_ROWS].rearrange("p (j b) -> p j b", b=MOD_ROWS)
                for lb, c0, b in ((1, 0, slice(0, 12)), (0, 40, slice(12, 14))):
                    dve.tensor_tensor(modc[:, lb, c0:48].rearrange("p (b j) -> p j b", j=4), turned[:, :, b],
                                      prm[:, lb, c0:48].rearrange("p (b j) -> p j b", j=4), ALU.add).then_inc(mod_col, 1)

            def mod_bias(i):
                lb, blk = mod_block(i)
                dve.wait_ge(mod_mm, i + 1)
                columns = slice(4 * blk, 4 * blk + 4)
                dve.tensor_tensor(modc[:, lb, columns], ps[:, mod_bank(i), 0:4], prm[:, lb, columns], ALU.add)\
                   .then_inc(mod_col, 1)

            def mod_in_a(u):
                for i, j, r in mod_behind(u):
                    fold_mod(i, j, r)

            def split_with_mod(l, u):
                split(l, u)
                if l == 0:
                    mod_in_a(u)

            def h_low(e, k):
                dve.wait_ge(h_hi_ready, 8 * e + k + 1)
                dve.tensor_tensor(h_lo[:, k, :], h32[:, k % 2, :], h_hi[:, k, :].bitcast(F32), ALU.subtract)\
                   .then_inc(h_ready, 1)

            def gate_vector(n, gate):
                if n:
                    dve.wait_ge(xa_ready, 8 * (n + 1))
                chain(dve.tensor_scalar(vecs[:, VGP, :], gate, 1.0, None, ALU.add))

            def vectors(e):
                n = e - 1
                m = modc
                if n % 2 == 0:
                    l = n // 2
                    gate, sc, sh = m[:, l, 16:24], m[:, l, 32:40], m[:, l, 24:32]
                    g, b = prm[:, l, C_LN1G:C_LN1G + KD], prm[:, l, C_LN1B:C_LN1B + KD]
                else:
                    l = n // 2
                    dve.wait_ge(mod_col, 12)
                    gate = m[:, l, 40:48]
                    g, b = prm[:, l, C_LN2G:C_LN2G + KD], prm[:, l, C_LN2B:C_LN2B + KD]
                    if l + 1 < LAYERS:
                        sc, sh = m[:, l + 1, 8:16], m[:, l + 1, 0:8]
                if n % 2:
                    gate_vector(n, gate)
                else:
                    dve.wait_ge(mod_col, 10)
                if n == 2 * LAYERS - 1:
                    return
                chain(dve.tensor_scalar(vecs[:, VS, :], sc, 1.0, None, ALU.add))
                dve.tensor_scalar(vecs[:, VAG, :], g, ALPHA, None, ALU.mult)
                dve.tensor_scalar(vecs[:, VAB, :], b, ALPHA, None, ALU.mult)
                dve.tensor_tensor(vecs[:, VG, :], g, vecs[:, VS, :], ALU.mult)
                chain(dve.tensor_tensor(vecs[:, VB, :], b, vecs[:, VS, :], ALU.mult))
                dve.tensor_tensor(vecs[:, VB, :], vecs[:, VB, :], sh, ALU.add).then_inc(vec_ready, 1)

            def residual(n, m):
                l, w = divmod(n, 2)
                g = NG * l + (G_OUT + 2 if w == 0 else NG - 2) + m // 4
                dve.wait_ge(xa_ready, 8 * n + m + 1)
                dve.wait_ge(bank_done, 4 * g + m % 4 + 1)
                if w == 0 and m == 0:
                    dve.wait_ge(out_half, 8 * (l + 1))
                dve.scalar_tensor_tensor(xr[:, m, :], ps[:, m % 4, :], vecs[:, VGP, m:m + 1], xr[:, m, :], ALU.mult, ALU.add)\
                   .then_inc(ln_r, 1)
                dve.wait_ge(ln_r, 8 * n + m + 1)
                if m == 1:
                    dve.tensor_tensor(s1[:, :], xr[:, 0, :], xr[:, 1, :], ALU.add).then_inc(ln_s1, 1)
                elif m > 1:
                    dve.wait_ge(ln_s1, 7 * n + m - 1)
                    dve.tensor_tensor(s1[:, :], s1[:, :], xr[:, m, :], ALU.add).then_inc(ln_s1, 1)

            def last_square(n):
                dve.wait_ge(ln_sq, 8 * (n + 1))
                dve.wait_ge(ln_s2, 7 * n + KD - 2)
                dve.tensor_tensor(s2[:, :], s2[:, :], sq[:, (KD - 1) % 2, :], ALU.add).then_inc(ln_s2, 1)

            def residual_ssd(l, m):
                dve.wait_ge(xa_ready, 16 * l + m + 1)
                dve.wait_ge(bank_done, 4 * (NG * l + G_OUT + m // 4) + m % 4 + 1)
                dve.scalar_tensor_tensor(xr[:, m, :], ps[:, m % 4, :], vecs[:, VGP, m:m + 1], xr[:, m, :], ALU.mult, ALU.add)\
                   .then_inc(out_half, 1)

            def gate(l, c):
                dve.wait_ge(z_tanh, CH * l + c + 1)
                dve.scalar_tensor_tensor(zs[:, c, :], zs[:, c, :], 1.0, ps[:, c, :], ALU.add, ALU.mult).then_inc(z_ready, 1)
                dve.wait_ge(z_ready, CH * l + c + 1)
                dve.scalar_tensor_tensor(yt[:, c, :], yt[:, c, :], 0.5, zs[:, c, :], ALU.mult, ALU.mult).then_inc(gated, 1)

            def newton(w, nrm=nrm, done=None, value=0):
                v0, y0, a = nrm[:, 0, 0:w], nrm[:, 2, 0:w], nrm[:, 3, 0:w]
                chain(dve.tensor_tensor(a, y0, y0, ALU.mult))
                chain(dve.tensor_tensor(a, a, v0, ALU.mult))
                chain(dve.tensor_scalar(a, a, -0.5, 1.5, ALU.mult, ALU.add))
                last = dve.tensor_tensor(a, a, y0, ALU.mult)
                if done is None:
                    chain(last)
                else:
                    last.then_inc(done, 1)
                    dve.wait_ge(done, value)

            def ln_scale(n):
                dve.wait_ge(ln_stats, n + 1)
                st = nrm[:, 4, :]
                chain(dve.tensor_copy(st, ps[:, 4, 0:8]))
                chain(dve.tensor_tensor(nrm[:, 3, 0:4], st[:, 0:4], st[:, 0:4], ALU.mult))
                dve.scalar_tensor_tensor(nrm[:, 0, 0:4], st[:, 4:8], EPS, nrm[:, 3, 0:4], ALU.add, ALU.subtract)\
                   .then_inc(ln_v, 1)
                dve.wait_ge(ln_y0, n + 1)
                newton(4)
                y = nrm[:, 3, 0:4]
                eye = ident.unsqueeze(1).to_broadcast([P, CH, P])
                dve.tensor_tensor(diag[:, 0, :, :], eye, y.unsqueeze(2).to_broadcast([P, CH, P]), ALU.mult)\
                   .then_inc(ln_diag, 1)
                chain(dve.scalar_tensor_tensor(nrm[:, 5, 0:4], st[:, 0:4], -1.0, y, ALU.mult, ALU.mult))
                dve.tensor_tensor(diag[:, 1, :, :], eye, nrm[:, 5, 0:4].unsqueeze(2).to_broadcast([P, CH, P]), ALU.mult)\
                   .then_inc(ln_diag, 1)

            def ln_tiles(n, ks):
                def scale(k):
                    dve.tensor_tensor(xr[:, k, :], xr[:, k, :], ps[:, 5, :], ALU.mult).then_inc(ln_m, 1)

                def shift(k):
                    dve.wait_ge(ln_m, 8 * n + k + 1)
                    dve.tensor_tensor(xr[:, k, :], xr[:, k, :], ps[:, 6, :], ALU.add).then_inc(ln_t, 1)

                for k in ks:
                    if k == 0:
                        dve.wait_ge(ln_rows, 2 * n + 1)
                        scale(0)
                        scale(1)
                        dve.wait_ge(ln_rows, 2 * (n + 1))
                    elif k > 1:
                        scale(k)
                    shift(k)
                    if k and n < 2 * LAYERS - 1:
                        h_low(n + 1, k - 1)
                if ks[-1] == KD - 1 and n < 2 * LAYERS - 1:
                    h_low(n + 1, KD - 1)

            def conv(l, t):
                dve.wait_ge(conv_raw, 8 * l + t + 1)
                if t == 0:
                    dve.wait_ge(pads_ready, l + 1)
                dst = xsF[:, t, :] if t < 4 else bcF[:, t - 4, :]
                w = prm[:, l, C_CONVW + 4 * t:C_CONVW + 4 * t + 4]
                for i in (2, 1, 0):
                    ins = dve.scalar_tensor_tensor(dst, conv_in[:, t, i:i + SEQ], w[:, i:i + 1], dst, ALU.mult, ALU.add)
                    if i:
                        chain(ins)
                ins.then_inc(conv_lin, 1)

            def conv_end(l, t):
                dve.wait_ge(conv_tanh, 8 * l + t + 1)
                dst = xsF[:, t, :] if t < 4 else bcF[:, t - 4, :]
                dve.scalar_tensor_tensor(dst, conv_th[:, t % 2, :], 1.0, dst, ALU.add, ALU.mult).then_inc(conv_out, 1)

            def dt_first(l):
                dve.wait_ge(dt_turned, l + 1)
                bias = prm[:, l, C_DTB:C_DTB + HEADS].unsqueeze(1).to_broadcast([P, CH, HEADS])
                chain(dve.tensor_tensor(dts[:, DU, :].rearrange("p (c h) -> p c h", c=CH),
                                        ps[:, 7, 0:32].rearrange("p (c h) -> p c h", c=CH), bias, ALU.add))
                dve.scalar_tensor_tensor(dts[:, DA, :], dts[:, DU, :], -1.0, dts[:, DU, :], ALU.mult, ALU.max)\
                   .then_inc(dt_abs, 1)

            def dt_second(l):
                dve.wait_ge(dt_exp, l + 1)
                dve.tensor_scalar(dts[:, DW, :], dts[:, DE, :], 1.0, None, ALU.add).then_inc(dt_w, 1)
                dve.wait_ge(dt_w, l + 1)
                dve.scalar_tensor_tensor(dts[:, DN, :], dts[:, DW, :], -1.0, dts[:, DE, :], ALU.add, ALU.subtract)
                chain(dve.reciprocal(dts[:, DA, :], dts[:, DW, :]))
                chain(dve.tensor_tensor(dts[:, DN, :], dts[:, DN, :], dts[:, DA, :], ALU.mult))
                chain(dve.scalar_tensor_tensor(dts[:, DT, :], dts[:, DU, :], 0.0, dts[:, DN, :], ALU.max, ALU.subtract))
                dve.wait_ge(dt_ln, l + 1)
                chain(dve.tensor_tensor(dts[:, DT, :], dts[:, DT, :], dts[:, DL, :], ALU.add))
                ea = expa[:, l, :].unsqueeze(1).to_broadcast([P, CH, HEADS])
                dve.scalar_tensor_tensor(dts[:, DAA, :].rearrange("p (c h) -> p c h", c=CH),
                                         dts[:, DT, :].rearrange("p (c h) -> p c h", c=CH), -1.0, ea, ALU.mult, ALU.mult)\
                   .then_inc(a_ready, 1)

            def sums(l):
                dve.wait_ge(cs_mm, l + 1)
                chain(dve.tensor_copy(dts[:, DCS, :], ps[:, 7, 32:64]))
                dve.tensor_scalar(dts[:, DN, :], dts[:, DCS, :], -1.0, None, ALU.mult)
                dve.tensor_tensor(dts[:, DDEC, :], ps[:, 7, 64:96], dts[:, DCS, :], ALU.subtract).then_inc(cs_ready, 1)

            def per_head(ap):
                return ap.unsqueeze(2).to_broadcast([P, HEADS, HDIM])

            def heads(ap):
                return ap.rearrange("p (h d) -> p h d", h=HEADS)

            def ssd_mid(l, c):
                cs = slice(c * HEADS, (c + 1) * HEADS)
                if c == 0:
                    dve.wait_ge(cs_exp, l + 1)
                    chain(dve.tensor_tensor(dts[:, DDEC, :], dts[:, DDEC, :], dts[:, DT, :], ALU.mult))
                dve.wait_ge(tok_copied, CH * l + c + 1)
                dve.tensor_tensor(heads(xdt[:, :]), heads(xs_tok[:, c, :]), per_head(dts[:, DT, cs]), ALU.mult)
                dve.tensor_tensor(heads(xdec[:, :]), heads(xs_tok[:, c, :]), per_head(dts[:, DDEC, cs]), ALU.mult)\
                   .then_inc(xd_ready, 1)
                dve.wait_ge(l_ready, CH * l + c + 1)
                for g in range(2):
                    cb = ps[:, 7, g * P:(g + 1) * P].unsqueeze(1).to_broadcast([P, 4, P])
                    last = dve.tensor_tensor(mm[:, 4 * g:4 * g + 4, :], lm[:, 4 * g:4 * g + 4, :], cb, ALU.mult)
                last.then_inc(m_ready, 1)

            def ssd_end(l, c):
                cs = slice(c * HEADS, (c + 1) * HEADS)
                dve.wait_ge(ssd_p2, CH * l + c + 1)
                dve.wait_ge(skip_ready, CH * l + c + 1)
                off = lm[:, 0:4, :].rearrange("p a b -> p (a b)")
                if c:
                    dve.tensor_tensor(heads(off), heads(ps[:, 5, :]), per_head(dts[:, DEA, cs]), ALU.mult)
                chain(dve.tensor_tensor(yt[:, c, :], yt[:, c, :], ps[:, 4, :], ALU.add))
                if c:
                    chain(dve.tensor_tensor(heads(state[:, :]), heads(state[:, :]), per_head(dts[:, DTOT, cs]), ALU.mult))
                    dve.tensor_tensor(yt[:, c, :], yt[:, c, :], off, ALU.add)
                    dve.tensor_tensor(state[:, :], state[:, :], ps[:, 6, :], ALU.add).then_inc(ssd_d2, 1)
                else:
                    dve.tensor_copy(state[:, :], ps[:, 6, :]).then_inc(ssd_d2, 1)
                dve.wait_ge(ssd_d2, CH * l + c + 1)

            def rope_tile(l, t):
                if t == 0:
                    dve.wait_ge(rope_loaded, 32 * (l + 1))
                dve.wait_ge(rot_dma[t % 2], 64 * (4 * l + t // 2 + 1))
                x = q[:, t, :] if t < 4 else kpad[:, 0, t - 4, :]
                r = rot[:, t % 2, :]
                dve.tensor_tensor(r, r, sinT[:, :], ALU.mult)
                chain(dve.tensor_tensor(x, x, cosT[:, :], ALU.mult))
                if t < 4:
                    dve.tensor_tensor(x, x, r, ALU.add).then_inc(rope_done, 1)
                else:
                    h = t - 4
                    dve.tensor_tensor(kpad[0:64, 0, h, :], x[0:64, :], r[0:64, :], ALU.add)
                    dve.tensor_tensor(kpad[64:128, 1, h, :], x[64:128, :], r[64:128, :], ALU.add).then_inc(rope_done, 1)

            def biggest(l, t):
                i, h = divmod(t, AH)
                dve.wait_ge(qk_done, 16 * l + t + 1)
                chain(dve.tensor_reduce(att[:, 2, 2 * h:2 * h + 2], ps[:, 4:6, 0:(i + 1) * P], AXX, ALU.max))
                dve.tensor_scalar(att[:, 0, 2 * h:2 * h + 2], att[:, 2, 2 * h:2 * h + 2], -0.125, None, ALU.mult)\
                   .then_inc(nb_ready, 1)

            def combine(l, t):
                i, h = divmod(t, AH)
                n = (i + 1) * P
                dve.wait_ge(exp_done, 16 * l + t + 1)
                rs = att[:, 3, 2 * h:2 * h + 2]
                chain(dve.reciprocal(rs, att[:, 1, 2 * h:2 * h + 2]))
                dve.tensor_tensor(rs[:, 1:2], rs[:, 1:2], lam[:, l, 0:1], ALU.mult)
                p0, p1 = prob[:, t % 2, 0, 0:n], prob[:, t % 2, 1, 0:n]
                chain(dve.tensor_scalar(p0, p0, rs[:, 0:1], None, ALU.mult))
                dve.scalar_tensor_tensor(p0, p1, rs[:, 1:2], p0, ALU.mult, ALU.add).then_inc(w_ready, 1)

            def o_out(l, i):
                dve.wait_ge(pv_done, 16 * l + 4 * i + 4)
                if i:
                    dve.wait_ge(tro_mm, CH * l + i)
                dve.wait_ge(o_sq, CH * l + i + 1)
                dve.tensor_scalar(nrm[:, 0, 0:4], ssq[:, 0:4], 1.0 / P, EPS, ALU.mult, ALU.add).then_inc(att_v, 1)
                dve.tensor_copy(o_tok[:, :], ps[:, 7, :]).then_inc(o_copied, 1)

            def o_scale(l, i):
                dve.wait_ge(att_y0, CH * l + i + 1)
                newton(4)
                o3 = o_tok[:, :].rearrange("p (h d) -> p h d", h=AH)
                dve.tensor_tensor(o3, o3, nrm[:, 3, 0:4].unsqueeze(2).to_broadcast([P, AH, P]), ALU.mult)\
                   .then_inc(o_scaled, 1)

            def yo_low(l, i):
                tok = slice(i * P, (i + 1) * P)
                dve.wait_ge(yo_hi, CH * l + i + 1)
                dve.scalar_tensor_tensor(y_lo[:, 4:8, tok], ps[:, 6, :].rearrange("p (h t) -> p h t", h=4), awc[:, l:l + 1],
                                         y_hi[:, 4:8, tok].bitcast(F32), ALU.mult, ALU.subtract).then_inc(yo_ready, 1)

            def ahead_of_out(l):
                t = AHEAD_OF_OUT - 1
                combine(l, t - 1)
                gate(l, CH - 1)
                biggest(l, t)
                dve.wait_ge(gate_sq, CH * (l + 1))
                dve.tensor_scalar(nrs[:, 0, :], nrs[:, 5, :], 1.0 / 256, EPS, ALU.mult, ALU.add).then_inc(ssd_v, 1)
                dve.wait_ge(ssd_y0, l + 1)
                newton(8, nrs, ssd_rstd, l + 1)
                for c in range(CH):
                    dve.wait_ge(ys_weighted, CH * l + c + 1)
                    dve.tensor_scalar(yt[:, c, 0:256], yt[:, c, 0:256], nrs[:, 3, 2 * c:2 * c + 1], None, ALU.mult)\
                       .then_inc(ys_scaled, 1)
                o_out(l, (t - 4) // 4)
                for c in range(CH):
                    tok = slice(c * P, (c + 1) * P)
                    dve.wait_ge(ys_hi, CH * l + c + 1)
                    dve.tensor_tensor(y_lo[:, 0:4, tok], ps[:, c, :].rearrange("p (h t) -> p h t", h=4),
                                      y_hi[:, 0:4, tok].bitcast(F32), ALU.subtract).then_inc(ys_ready, 1)
                split_with_mod(l, U_OUT + 2)

            def step(l, t, u=0):
                last = t == STEP_COUNT - 1
                if t == STEP_COUNT - 6:
                    gate_vector(2 * l, modc[:, l, 16:24])
                if 1 <= t <= 16:
                    combine(l, t - 1)
                if last:
                    residual_ssd(l, 4)
                if t >= 5 and t % 4 == 1:
                    o_scale(l, (t - 5) // 4)
                if last:
                    residual_ssd(l, 5)
                if t < 16:
                    biggest(l, t)
                if split_in_step(u) == t:
                    split_with_mod(l, u + 3)
                if t == STEP_COUNT - 6:
                    for m in range(4):
                        residual_ssd(l, m)
                if t >= 4 and t % 4 == 0:
                    o_out(l, (t - 4) // 4)
                if t >= 5 and t % 4 == 1:
                    yo_low(l, (t - 5) // 4)
                if last:
                    residual_ssd(l, 6)
                    residual_ssd(l, 7)

            def mlp_end(l, it):
                for j in range(2):
                    dve.wait_ge(mlp_th, FT * l + j + 1 + 2 * it)
                    dve.scalar_tensor_tensor(sq[:, j, :], sq[:, j, :], 1.0, ps[:, j, :], ALU.add, ALU.mult)\
                       .then_inc(mlp_a, 1)
                for j in range(2):
                    dve.wait_ge(bank_done, 4 * (NG * l + G_MLP) + 2 + j + 1 + 4 * it)
                    dve.wait_ge(mlp_a, FT * l + j + 1 + 2 * it)
                    dve.scalar_tensor_tensor(h32[:, j, :], sq[:, j, :], 0.5, ps[:, 2 + j, :], ALU.mult, ALU.mult)\
                       .then_inc(mlp_f, 1)
                for j in range(2):
                    dve.wait_ge(f_hi_ready, FT * l + j + 1 + 2 * it)
                    dve.tensor_tensor(f_lo[:, bass.ds(2 * it + j, 1), :], h32[:, j:j + 1, :],
                                      f_hi[:, bass.ds(2 * it + j, 1), :].bitcast(F32), ALU.subtract).then_inc(f_ready, 1)

            dve.wait_ge(c_loaded, 16)
            dve.memset(meancol[:, :], 1.0 / D)
            dve.tensor_scalar(cond[:, 1, :], cvec, 0.5, None, ALU.mult).then_inc(cond_half, 1)
            dve.wait_ge(cond_tanh, 1)
            chain(dve.scalar_tensor_tensor(cvec, cond[:, 2, :], 1.0, cond[:, 1, :], ALU.add, ALU.mult))
            for j in range(4):
                fold_mod(0, j, mod_front(0, j))
            dve.wait_ge(small_loaded, 48)
            dve.tensor_copy(maskb[:, :], maskf)
            dve.tensor_copy(identb[:, :], ident).then_inc(consts_ready, 1)
            chain(dve.tensor_scalar(sel[:, :], ones[:, 0:2 * MOD_ROWS], 0.0, None, ALU.mult))
            dve.tensor_copy(sel[:, MOD_ROWS - 1:MOD_ROWS], ones[:, 0:1])
            lq = lamt[:, :, :, :].rearrange("p l (a b) d -> p l a b d", b=2)
            chain(dve.tensor_tensor(lamp[:, :, :, :], lq[:, :, :, 0, :], lq[:, :, :, 1, :], ALU.mult))
            for l in range(LAYERS):
                last = dve.tensor_reduce(lam[:, l, 0:2], lamp[:, l, :, :], AXX, ALU.add)
            last.then_inc(lam_sums, 1)
            for l in range(LAYERS):
                init = 0.8 - 0.6 * math.exp(-0.3 * l)
                dve.tensor_scalar(prm[:, l, C_CONVW:C_CONVW + 40], prm[:, l, C_CONVW:C_CONVW + 40], 0.5, None, ALU.mult)
                dve.tensor_scalar(awc[:, l:l + 1], prm[:, l, C_ATTNW:C_ATTNW + 1], 1.0 - init, None, ALU.mult)
            dve.wait_ge(lam_exp, 1)
            for l in range(LAYERS):
                init = 0.8 - 0.6 * math.exp(-0.3 * l)
                chain(dve.tensor_tensor(lam[:, l, 0:1], lam[:, l, 3:4], lam[:, l, 2:3], ALU.subtract))
                chain(dve.tensor_scalar(lam[:, l, 0:1], lam[:, l, 0:1], -init, None, ALU.add))
            for j in range(4):
                fold_mod(1, j, mod_front(1, j))
            mod_bias(0)
            split(0, 0)
            mod_bias(1)

            def first_vectors(half):
                f = slice(4 * half, 4 * half + 4)
                dve.wait_ge(mod_col, 2 * (half + 1))
                dve.tensor_scalar(vecs[:, VG, f], modc[:, 0, 8 + 4 * half:12 + 4 * half], 1.0, None, ALU.add)
                dve.tensor_copy(vecs[:, VB, f], modc[:, 0, f]).then_inc(vec_ready, 1)

            first_vectors(0)
            split(0, 1)
            h_low(0, 0)
            h_low(0, 1)
            fold_mod(2, 0, mod_front(2, 0))
            h_low(0, 2)
            h_low(0, 3)
            for m in range(1, 8):
                fold_mod(2 + m // 4, m % 4, mod_front(2 + m // 4, m % 4))
            mod_bias(2)
            split(0, 2)
            mod_bias(3)
            first_vectors(1)
            for k in range(4, KD):
                h_low(0, k)
            for l in range(LAYERS):
                for u in range(U_MLP):
                    if u == 29:
                        for m in range(4):
                            residual(2 * l, m)
                    if u < 3 and l:
                        ln_tiles(2 * l - 1, [2 * u + 2, 2 * u + 3])
                    if split_in_step(u) is None and u not in (U_OUT - 1, U_MLP - 2, U_MLP - 1):
                        split_with_mod(l, u + 3)
                    for i in MOD_LAST:
                        if u == mod_reduced_at(i) + (i >= 8) and l == 0:
                            mod_bias(i)
                    if u == 0:
                        dve.wait_ge(wdt_hi_ready, l + 1)
                        dve.tensor_tensor(wdt_lo[:, :, :], wdt_raw[:, :, :], wdt_hi[:, :, :].bitcast(F32), ALU.subtract)\
                           .then_inc(wdt_ready, 1)
                    if u == 4:
                        dt_first(l)
                    if 4 <= u <= 11:
                        conv(l, u - 4)
                    if u == 4:
                        dt_second(l)
                    if 5 <= u <= 12:
                        conv_end(l, u - 5)
                    if u == 7:
                        sums(l)
                    for what, t in between(u):
                        if (what, t) == ("step_a", AHEAD_OF_OUT - 1):
                            ahead_of_out(l)
                        elif what == "first":
                            ssd_mid(l, t)
                        elif what == "second":
                            ssd_end(l, t)
                        elif what == "step_a":
                            step(l, t, u)
                        elif what == "turn_w":
                            step(l, t + 1, u)
                        elif what == "z" and t < CH - 1:
                            gate(l, t)
                    if u == U_OUT + 3:
                        step(l, STEP_COUNT - 1)
                    for t in ROPE_AT.get(u, []):
                        rope_tile(l, t)
                residual(2 * l, 4)
                split_with_mod(l, U_MLP + 1)
                residual(2 * l, 5)
                vectors(2 * l + 1)
                residual(2 * l, 6)
                residual(2 * l, 7)
                last_square(2 * l)
                split(l, U_MLP + 2)
                ln_scale(2 * l)
                ln_tiles(2 * l, [0, 1])

                for j in range(4):
                    if j < 3:
                        ln_tiles(2 * l, [2 * j + 2, 2 * j + 3])
                    split(l, U_MLP + j + 3)
                    if l == 0 and j:
                        fold_row(0, j - 1, raw_of(0, U_MLP + j + 3) + 1)
                before = chained[0]
                MOD_CHAIN = 5
                with dve.Fori(1, MLP_G) as g:
                    loop = (g - 1) * (MOD_CHAIN if l == 0 else 0)
                    mlp_end(l, g - 1)
                    for j in range(4):
                        split(l, U_MLP + j + 3, it=g)
                        if l == 0:
                            fold_row(g if j else g - 1, (j + 3) % 4, raw_at(0, U_MLP + j + 3, g) + 1, g, loop)
                if l == 0:
                    assert chained[0] - before == MOD_CHAIN
                    chained[0] = before + MOD_CHAIN * (MLP_G - 1)
                for u in range(U_DOWN, UNITS):
                    i = u - U_DOWN
                    if i == 0:
                        mlp_end(l, MLP_G - 1)
                    if l == 0 and i == DOWN_SLABS - 2:
                        mod_rows_out()
                    if l == 0 and i == DOWN_SLABS - 1:
                        mod_columns()
                    if i == DOWN_SLABS - 1:
                        vectors(2 * l + 2)
                        for m in range(4):
                            residual(2 * l + 1, m)
                    if i < 2 * DOWN_SLABS - 1:
                        split(l, u + 3)
                    if l == 0:
                        for row, j, r in mod_behind_down(u + 3):
                            fold_row(row, j, r)
                for m in range(4, 8):
                    residual(2 * l + 1, m)
                last_square(2 * l + 1)
                split(l, UNITS - 1 + 3)
                ln_scale(2 * l + 1)
                if l + 1 < LAYERS:
                    ln_tiles(2 * l + 1, [0, 1])
                else:
                    ln_tiles(2 * l + 1, range(KD))


def kernel(**inputs):
    import numpy as _np
    import concourse.bacc as _bacc
    from concourse import mybir as _mybir
    from concourse.bass_utils import run_bass_kernel_spmd as _run

    f = {k: _np.asarray(a) for k, a in inputs.items()}
    L = LAYERS
    SSD_IN = 512

    def cols(a):
        return a.reshape(-1, P).T

    def rows(a):
        return _np.broadcast_to(a.reshape(1, -1), (P, a.size))

    w = f["w_in"]
    z, xbc, dt, qkv = w[:, :, :SSD_IN], w[:, :, SSD_IN:SSD_IN + D], w[:, :, SSD_IN + D:SSD_IN + D + HEADS], \
        w[:, :, SSD_IN + D + HEADS:]
    par = _np.stack([_np.concatenate(
        [cols(f["b_mod"][l]), cols(f["ln1_g"][l]), cols(f["ln1_b"][l]), cols(f["ln2_g"][l]), cols(f["ln2_b"][l])]
        + [f["conv_w"][l][:, t * P:(t + 1) * P].T for t in range(8)]
        + [cols(f["conv_b"][l]), cols(f["attn_norm_w"][l]), rows(f["dt_bias"][l]), rows(f["a_log"][l]),
           rows(f["d_skip"][l])], axis=1) for l in range(L)], axis=1)
    eye = _np.eye(P, dtype=_np.float32)
    tri = _np.triu(_np.ones((P, P), _np.float32))
    mask = ((tri - 1) * _np.float32(-NEG)).astype(_np.float32)
    inv = (1.0 / (_np.float32(10000.0) ** (_np.arange(0, HDIM, 2, dtype=_np.float32) / _np.float32(HDIM))))
    ang = _np.arange(SEQ, dtype=_np.float32)[:, None] * inv.astype(_np.float32)[None, :]
    ang = _np.concatenate([ang, ang], -1).T
    sign = _np.where(_np.arange(HDIM) < HDIM // 2, -1.0, 1.0).astype(_np.float32)[:, None]
    rope = _np.stack([_np.tile(_np.cos(ang), (2, 1)), _np.tile(_np.sin(ang) * sign, (2, 1))]).astype(_np.float32)
    arrays = {
        "xT": f["x"][0].T,
        "ccol": cols(f["c"][0]),
        "w_mod": f["w_mod"],
        "w_in": _np.concatenate([xbc, qkv, z], axis=2),
        "w_out": f["w_out"],
        "w_gu": f["w_gate_up"].reshape(L, D, 2, MLP_G, 256).transpose(0, 1, 3, 2, 4).reshape(L, D, 2 * D_FF),
        "w_down": f["w_down"],
        "par": par,
        "ssdw": _np.stack([rows(f["ssd_norm_w"][l]) for l in range(L)]),
        "lamqk": _np.broadcast_to(f["lam_qk"][None], (P, L, 4, 64)),
        "wdt": dt.reshape(L, KD, P, HEADS).transpose(0, 2, 1, 3),
        "consts": _np.concatenate([eye, tri, mask, _np.ones((P, P), _np.float32)], axis=1),
        "rope": rope,
    }
    arrays = {k: _np.ascontiguousarray(a) for k, a in arrays.items()}
    nc = _bacc.Bacc("TRN2", target_bir_lowering=False, num_devices=1)
    args = [nc.dram_tensor(f"in_{k}", a.shape, _mybir.dt.from_np(a.dtype), kind="ExternalInput").ap()
            for k, a in arrays.items()]
    out = nc.dram_tensor("outT", (D, SEQ), F32, kind="ExternalOutput").ap()
    kernel_body(nc, *args, out)
    r = _run(nc, [{f"in_{k}": a for k, a in arrays.items()}], core_ids=[0])
    return r.results[0]["outT"].T[None]
```
